# Optimizing a Trainium2 kernel written in Bass

```python
import jax, jax.numpy as jnp
from jax import lax
import numpy as np

D_MODEL = 2048
BATCH = 1
SEQ = 256
DEPTH = 1

HEAD_DIM = 128
Q_BLOCK = 128
NEG = -1e30
FORCE = 1e9
EPS = 1e-6

MOBA_HEADS = 8
MOBA_BLOCK = 256
MOBA_TOPK = 3
MOBA_WIDTH = MOBA_HEADS * HEAD_DIM

NSA_HEADS = 8
NSA_KV_HEADS = 2
NSA_GROUP = NSA_HEADS // NSA_KV_HEADS
NSA_CMP_LEN = 32
NSA_CMP_STRIDE = 16
NSA_SLC_BLOCK = 64
NSA_TOPN = 8
NSA_WINDOW = 512
NSA_WIDTH = NSA_HEADS * HEAD_DIM
NSA_KV_WIDTH = NSA_KV_HEADS * HEAD_DIM

GLA_HEADS = 4
GLA_DK = 128
GLA_DV = 256
GLA_RANK = 16
GLA_TAU = 16.0
GLA_CHUNK = 64
GLA_KEY_WIDTH = GLA_HEADS * GLA_DK
GLA_WIDTH = GLA_HEADS * GLA_DV

N_BRANCH = 3
IN_SPLITS = (MOBA_WIDTH, MOBA_WIDTH, MOBA_WIDTH,
             NSA_WIDTH, 6 * NSA_KV_WIDTH, 3 * NSA_HEADS,
             GLA_KEY_WIDTH, GLA_KEY_WIDTH, GLA_WIDTH,
             GLA_RANK, GLA_WIDTH,
             N_BRANCH * D_MODEL)
IN_WIDTH = sum(IN_SPLITS)

MOE_GROUPS = 4
MOE_EXPERTS_PER_GROUP = 8
MOE_EXPERTS = MOE_GROUPS * MOE_EXPERTS_PER_GROUP
MOE_TOPK = 2
MOE_FF = D_MODEL // 4
MOE_ROW_BLOCK = 128

kernel_name = 'hybrid_moba_nsa_gla_hmoe_block'

def rmsnorm(x, g):
    xf = x.astype(jnp.float32)
    y = xf * lax.rsqrt(jnp.mean(xf * xf, axis=-1, keepdims=True) + EPS)
    return (y * g.astype(jnp.float32)).astype(x.dtype)

def moba_attention(q, k, v):
    B, S = q.shape[0], q.shape[1]
    Sp = -(-S // MOBA_BLOCK) * MOBA_BLOCK
    pad = ((0, 0), (0, Sp - S), (0, 0), (0, 0))
    q, k, v = jnp.pad(q, pad), jnp.pad(k, pad), jnp.pad(v, pad)
    nb = Sp // MOBA_BLOCK
    topk = min(MOBA_TOPK, nb)
    scale = HEAD_DIM ** -0.5
    heads = jnp.arange(MOBA_HEADS)[:, None, None]

    def per_example(args):
        qe, ke, ve = args
        qh = qe.transpose(1, 0, 2)
        kb = ke.transpose(1, 0, 2).reshape(MOBA_HEADS, nb, MOBA_BLOCK, HEAD_DIM)
        vb = ve.transpose(1, 0, 2).reshape(MOBA_HEADS, nb, MOBA_BLOCK, HEAD_DIM)
        kmean = jnp.mean(kb.astype(jnp.float32), axis=2)

        def per_qblock(i):
            start = i * Q_BLOCK
            qb = lax.dynamic_slice_in_dim(qh, start, Q_BLOCK, axis=1)
            pos = start + jnp.arange(Q_BLOCK)
            cur = start // MOBA_BLOCK
            gate = jnp.einsum('hqd,hnd->hqn', qb.astype(jnp.float32), kmean)
            gate = jnp.where(jnp.arange(nb) < cur, gate, NEG)
            _, sel = lax.top_k(gate, topk)
            k_sel = kb[heads, sel]
            v_sel = vb[heads, sel]
            k_own = lax.dynamic_index_in_dim(kb, cur, axis=1, keepdims=False)
            v_own = lax.dynamic_index_in_dim(vb, cur, axis=1, keepdims=False)
            s_sel = jnp.einsum('hqd,hqnkd->hqnk', qb, k_sel, preferred_element_type=jnp.float32) * scale
            s_sel = jnp.where((sel < cur)[..., None], s_sel, NEG)
            s_own = jnp.einsum('hqd,hkd->hqk', qb, k_own, preferred_element_type=jnp.float32) * scale
            own_pos = cur * MOBA_BLOCK + jnp.arange(MOBA_BLOCK)
            s_own = jnp.where(own_pos[None, None, :] <= pos[None, :, None], s_own, NEG)
            s = jnp.concatenate([s_sel.reshape(MOBA_HEADS, Q_BLOCK, topk * MOBA_BLOCK), s_own], axis=-1)
            p = jax.nn.softmax(s, axis=-1).astype(ve.dtype)
            p_sel = p[..., :topk * MOBA_BLOCK].reshape(MOBA_HEADS, Q_BLOCK, topk, MOBA_BLOCK)
            p_own = p[..., topk * MOBA_BLOCK:]
            return (jnp.einsum('hqnk,hqnkd->qhd', p_sel, v_sel)
                    + jnp.einsum('hqk,hkd->qhd', p_own, v_own))

        out = lax.map(per_qblock, jnp.arange(Sp // Q_BLOCK))
        return out.reshape(Sp, MOBA_HEADS, HEAD_DIM)

    out = lax.map(per_example, (q, k, v))
    return out[:, :S]

def nsa_attention(q, kv, gates, cmp_pe, cmp_w1, cmp_w2):
    B, S = q.shape[0], q.shape[1]
    G, R, dh = NSA_KV_HEADS, NSA_GROUP, HEAD_DIM
    scale = dh ** -0.5
    ncmp = (S - NSA_CMP_LEN) // NSA_CMP_STRIDE + 1
    win_idx = jnp.arange(ncmp)[:, None] * NSA_CMP_STRIDE + jnp.arange(NSA_CMP_LEN)[None, :]
    blocks = kv[:, :, 0:2][:, win_idx]
    blocks = blocks + cmp_pe.transpose(1, 0, 2)[None, None, :, :, None, :]
    flat = blocks.transpose(0, 1, 3, 4, 2, 5).reshape(B, ncmp, 2, G, NSA_CMP_LEN * dh)
    hid = jax.nn.silu(jnp.einsum('bncgi,cio->bncgo', flat, cmp_w1))
    kv_c = jnp.einsum('bncgi,cio->bncgo', hid, cmp_w2)
    k_c, v_c = kv_c[:, :, 0], kv_c[:, :, 1]
    cmp_start = jnp.arange(ncmp) * NSA_CMP_STRIDE
    cmp_end = cmp_start + NSA_CMP_LEN - 1
    nslc = S // NSA_SLC_BLOCK
    slc_start = jnp.arange(nslc) * NSA_SLC_BLOCK
    overlap = ((cmp_start[:, None] < slc_start[None, :] + NSA_SLC_BLOCK)
               & (cmp_end[:, None] >= slc_start[None, :])).astype(jnp.float32)
    topn = min(NSA_TOPN, nslc)
    groups = jnp.arange(G)[:, None, None]

    def per_example(args):
        qe, kve, ge, kce, vce = args
        qg = qe.reshape(S, G, R, dh).transpose(1, 2, 0, 3)
        pos = jnp.arange(S)
        s_c = jnp.einsum('grqd,ngd->grqn', qg, kce, preferred_element_type=jnp.float32) * scale
        cmask = cmp_end[None, :] <= pos[:, None]
        p_c = jax.nn.softmax(jnp.where(cmask, s_c, NEG), axis=-1) * cmask
        o_c = jnp.einsum('grqn,ngd->qgrd', p_c.astype(vce.dtype), vce)
        imp = jnp.einsum('gqn,nj->gqj', p_c.sum(axis=1), overlap)
        cur_blk = pos // NSA_SLC_BLOCK
        j = jnp.arange(nslc)[None, :]
        forced = (j == 0) | (j == cur_blk[:, None]) | (j == cur_blk[:, None] - 1)
        imp = jnp.where(forced, FORCE, imp)
        imp = jnp.where(j > cur_blk[:, None], NEG, imp)
        _, sel = lax.top_k(imp, topn)
        ksb = kve[:, 2].transpose(1, 0, 2).reshape(G, nslc, NSA_SLC_BLOCK, dh)
        vsb = kve[:, 3].transpose(1, 0, 2).reshape(G, nslc, NSA_SLC_BLOCK, dh)
        kw = jnp.pad(kve[:, 4], ((NSA_WINDOW, 0), (0, 0), (0, 0)))
        vw = jnp.pad(kve[:, 5], ((NSA_WINDOW, 0), (0, 0), (0, 0)))

        def per_qblock(i):
            start = i * Q_BLOCK
            qb = lax.dynamic_slice_in_dim(qg, start, Q_BLOCK, axis=2)
            qpos = start + jnp.arange(Q_BLOCK)
            selb = lax.dynamic_slice_in_dim(sel, start, Q_BLOCK, axis=1)
            k_sel = ksb[groups, selb]
            v_sel = vsb[groups, selb]
            s_s = jnp.einsum('grqd,gqnkd->grqnk', qb, k_sel, preferred_element_type=jnp.float32) * scale
            key_pos = selb[..., None] * NSA_SLC_BLOCK + jnp.arange(NSA_SLC_BLOCK)
            s_s = jnp.where((key_pos <= qpos[None, :, None, None])[:, None], s_s, NEG)
            p_s = jax.nn.softmax(s_s.reshape(G, R, Q_BLOCK, topn * NSA_SLC_BLOCK), axis=-1)
            p_s = p_s.reshape(G, R, Q_BLOCK, topn, NSA_SLC_BLOCK).astype(v_sel.dtype)
            o_s = jnp.einsum('grqnk,gqnkd->qgrd', p_s, v_sel)
            k_w = lax.dynamic_slice_in_dim(kw, start, NSA_WINDOW + Q_BLOCK, axis=0)
            v_w = lax.dynamic_slice_in_dim(vw, start, NSA_WINDOW + Q_BLOCK, axis=0)
            wpos = start - NSA_WINDOW + jnp.arange(NSA_WINDOW + Q_BLOCK)
            wmask = ((wpos[None, :] <= qpos[:, None]) & (wpos[None, :] > qpos[:, None] - NSA_WINDOW)
                     & (wpos[None, :] >= 0))
            s_w = jnp.einsum('grqd,kgd->grqk', qb, k_w, preferred_element_type=jnp.float32) * scale
            p_w = jax.nn.softmax(jnp.where(wmask, s_w, NEG), axis=-1).astype(v_w.dtype)
            o_w = jnp.einsum('grqk,kgd->qgrd', p_w, v_w)
            return o_s, o_w

        o_s, o_w = lax.map(per_qblock, jnp.arange(S // Q_BLOCK))
        o_s = o_s.reshape(S, G, R, dh)
        o_w = o_w.reshape(S, G, R, dh)
        gg = ge.reshape(S, G, R, 3)
        o = gg[..., 0:1] * o_c + gg[..., 1:2] * o_s + gg[..., 2:3] * o_w
        return o.reshape(S, NSA_HEADS, dh)

    return lax.map(per_example, (q, kv, gates, k_c, v_c))

def gla_attention(q, k, v, log_a):
    B, S, H = q.shape[0], q.shape[1], q.shape[2]
    nc = S // GLA_CHUNK

    def chunks(t):
        return t.reshape(B, nc, GLA_CHUNK, H, t.shape[-1]).transpose(1, 0, 3, 2, 4)

    qc, kc, vc, ac = chunks(q * (GLA_DK ** -0.5)), chunks(k), chunks(v), chunks(log_a)
    causal = jnp.tril(jnp.ones((GLA_CHUNK, GLA_CHUNK), dtype=bool))

    def step(state, inp):
        qi, ki, vi, ai = inp
        qf, kf, vf = qi.astype(jnp.float32), ki.astype(jnp.float32), vi.astype(jnp.float32)
        b = jnp.cumsum(ai.astype(jnp.float32), axis=2)
        diff = b[:, :, :, None, :] - b[:, :, None, :, :]
        decay = jnp.exp(jnp.where(causal[None, None, :, :, None], diff, -jnp.inf))
        attn = jnp.einsum('bhtd,bhsd,bhtsd->bhts', qf, kf, decay)
        o = (jnp.einsum('bhts,bhse->bhte', attn, vf)
             + jnp.einsum('bhtd,bhde->bhte', qf * jnp.exp(b), state))
        b_last = b[:, :, -1:, :]
        state = (jnp.exp(b_last[:, :, 0, :, None]) * state
                 + jnp.einsum('bhsd,bhse->bhde', kf * jnp.exp(b_last - b), vf))
        return state, o

    state0 = jnp.zeros((B, H, GLA_DK, GLA_DV), jnp.float32)
    _, o = lax.scan(step, state0, (qc, kc, vc, ac))
    return o.transpose(1, 0, 3, 2, 4).reshape(B, S, H, GLA_DV).astype(v.dtype)

def hier_moe(h, rg_w, rg_b, re_w, re_b, w_gate, w_up, w_down):
    B, S, D = h.shape
    T = B * S
    ht = h.reshape(T, D)
    g_logits = (ht @ rg_w).astype(jnp.float32) + rg_b.astype(jnp.float32)
    grp = jnp.argmax(g_logits, axis=-1)
    p_grp = jnp.take_along_axis(jax.nn.softmax(g_logits, axis=-1), grp[:, None], axis=1)[:, 0]
    e_logits = ((ht @ re_w).astype(jnp.float32) + re_b.astype(jnp.float32)).reshape(T, MOE_GROUPS, MOE_EXPERTS_PER_GROUP)
    e_in = jnp.take_along_axis(e_logits, grp[:, None, None], axis=1)[:, 0]
    top_v, top_i = lax.top_k(e_in, MOE_TOPK)
    w = jax.nn.softmax(top_v, axis=-1) * p_grp[:, None]
    expert = grp[:, None] * MOE_EXPERTS_PER_GROUP + top_i
    A = T * MOE_TOPK
    e_flat = expert.reshape(A)
    w_flat = w.reshape(A)
    tok = jnp.arange(A) // MOE_TOPK
    order = jnp.argsort(e_flat)
    e_sorted = e_flat[order]
    counts = jax.ops.segment_sum(jnp.ones((A,), jnp.int32), e_flat, num_segments=MOE_EXPERTS)
    starts = jnp.cumsum(counts) - counts
    padded = (counts + MOE_ROW_BLOCK - 1) // MOE_ROW_BLOCK * MOE_ROW_BLOCK
    pends = jnp.cumsum(padded)
    pstarts = pends - padded
    dest = pstarts[e_sorted] + (jnp.arange(A) - starts[e_sorted])
    P = (A + MOE_EXPERTS * (MOE_ROW_BLOCK - 1) + MOE_ROW_BLOCK - 1) // MOE_ROW_BLOCK * MOE_ROW_BLOCK
    nblk = P // MOE_ROW_BLOCK
    row_tok = jnp.zeros((P,), jnp.int32).at[dest].set(tok[order])
    row_w = jnp.zeros((P,), jnp.float32).at[dest].set(w_flat[order])
    blk_e = jnp.clip(jnp.searchsorted(pends, jnp.arange(nblk) * MOE_ROW_BLOCK, side='right'), 0, MOE_EXPERTS - 1)

    def expert_block(args):
        toks, e = args
        xb = ht[toks]
        return (jax.nn.silu(xb @ w_gate[e]) * (xb @ w_up[e])) @ w_down[e]

    y_rows = lax.map(expert_block, (row_tok.reshape(nblk, MOE_ROW_BLOCK), blk_e)).reshape(P, D)
    y_rows = y_rows * row_w[:, None].astype(y_rows.dtype)
    y = jax.ops.segment_sum(y_rows, row_tok, num_segments=T)
    return y.reshape(B, S, D)

def hybrid_layer(x, norm1_g, w_in, nsa_cmp_pe, nsa_cmp_w1, nsa_cmp_w2, gla_wa, gla_ba, gla_norm_g,
                 w_br_moba, w_br_nsa, w_br_gla, w_out, norm2_g, router_group_w, router_group_b,
                 router_expert_w, router_expert_b, expert_w_gate, expert_w_up, expert_w_down):
    B, S = x.shape[0], x.shape[1]
    h = rmsnorm(x, norm1_g)
    proj = h @ w_in
    offsets = [int(o) for o in np.cumsum(IN_SPLITS)[:-1]]
    (mq, mk, mv, nq, nkv, ng, gq, gk, gv, ga, gg, mg) = jnp.split(proj, offsets, axis=-1)
    o_m = moba_attention(mq.reshape(B, S, MOBA_HEADS, HEAD_DIM), mk.reshape(B, S, MOBA_HEADS, HEAD_DIM),
                         mv.reshape(B, S, MOBA_HEADS, HEAD_DIM)).reshape(B, S, MOBA_WIDTH)
    o_n = nsa_attention(nq.reshape(B, S, NSA_HEADS, HEAD_DIM), nkv.reshape(B, S, 6, NSA_KV_HEADS, HEAD_DIM),
                        jax.nn.sigmoid(ng.reshape(B, S, NSA_HEADS, 3)),
                        nsa_cmp_pe, nsa_cmp_w1, nsa_cmp_w2).reshape(B, S, NSA_WIDTH)
    log_a = jax.nn.log_sigmoid((ga @ gla_wa + gla_ba).astype(jnp.float32)) / GLA_TAU
    o_g = gla_attention(gq.reshape(B, S, GLA_HEADS, GLA_DK), gk.reshape(B, S, GLA_HEADS, GLA_DK),
                        gv.reshape(B, S, GLA_HEADS, GLA_DV), log_a.reshape(B, S, GLA_HEADS, GLA_DK))
    o_g = (rmsnorm(o_g, gla_norm_g) * jax.nn.silu(gg.reshape(B, S, GLA_HEADS, GLA_DV))).reshape(B, S, GLA_WIDTH)
    gates = jax.nn.sigmoid(mg.reshape(B, S, N_BRANCH, D_MODEL))
    merged = (gates[:, :, 0] * (o_m @ w_br_moba) + gates[:, :, 1] * (o_n @ w_br_nsa)
              + gates[:, :, 2] * (o_g @ w_br_gla))
    x = x + merged @ w_out
    x = x + hier_moe(rmsnorm(x, norm2_g), router_group_w, router_group_b, router_expert_w, router_expert_b,
                     expert_w_gate, expert_w_up, expert_w_down)
    return x

def setup_inputs(seed: int = 0) -> dict:
    key = jax.random.key(seed)
    ks = jax.random.split(key, 24)
    L = DEPTH

    def nrm(k, shape, scale):
        return jax.random.normal(k, shape, jnp.float32) * scale

    return {
        'x': nrm(ks[0], (BATCH, SEQ, D_MODEL), 1.0),
        'norm1_g': 1.0 + nrm(ks[1], (L, D_MODEL), 0.02),
        'w_in': nrm(ks[2], (L, D_MODEL, IN_WIDTH), D_MODEL ** -0.5),
        'nsa_cmp_pe': nrm(ks[3], (L, 2, NSA_CMP_LEN, HEAD_DIM), 0.1),
        'nsa_cmp_w1': nrm(ks[4], (L, 2, NSA_CMP_LEN * HEAD_DIM, HEAD_DIM), (NSA_CMP_LEN * HEAD_DIM) ** -0.5),
        'nsa_cmp_w2': nrm(ks[5], (L, 2, HEAD_DIM, HEAD_DIM), HEAD_DIM ** -0.5),
        'gla_wa': nrm(ks[6], (L, GLA_RANK, GLA_KEY_WIDTH), GLA_RANK ** -0.5),
        'gla_ba': nrm(ks[7], (L, GLA_KEY_WIDTH), 0.02),
        'gla_norm_g': 1.0 + nrm(ks[8], (L, GLA_DV), 0.02),
        'w_br_moba': nrm(ks[9], (L, MOBA_WIDTH, D_MODEL), MOBA_WIDTH ** -0.5),
        'w_br_nsa': nrm(ks[10], (L, NSA_WIDTH, D_MODEL), NSA_WIDTH ** -0.5),
        'w_br_gla': nrm(ks[11], (L, GLA_WIDTH, D_MODEL), GLA_WIDTH ** -0.5),
        'w_out': nrm(ks[12], (L, D_MODEL, D_MODEL), D_MODEL ** -0.5),
        'norm2_g': 1.0 + nrm(ks[13], (L, D_MODEL), 0.02),
        'router_group_w': nrm(ks[14], (L, D_MODEL, MOE_GROUPS), D_MODEL ** -0.5),
        'router_group_b': nrm(ks[15], (L, MOE_GROUPS), 0.01),
        'router_expert_w': nrm(ks[16], (L, D_MODEL, MOE_EXPERTS), D_MODEL ** -0.5),
        'router_expert_b': nrm(ks[17], (L, MOE_EXPERTS), 0.01),
        'expert_w_gate': nrm(ks[18], (L, MOE_EXPERTS, D_MODEL, MOE_FF), D_MODEL ** -0.5),
        'expert_w_up': nrm(ks[19], (L, MOE_EXPERTS, D_MODEL, MOE_FF), D_MODEL ** -0.5),
        'expert_w_down': nrm(ks[20], (L, MOE_EXPERTS, MOE_FF, D_MODEL), MOE_FF ** -0.5),
        'final_norm_g': 1.0 + nrm(ks[21], (D_MODEL,), 0.02),
    }

def reference(x, norm1_g, w_in, nsa_cmp_pe, nsa_cmp_w1, nsa_cmp_w2, gla_wa, gla_ba, gla_norm_g,
              w_br_moba, w_br_nsa, w_br_gla, w_out, norm2_g, router_group_w, router_group_b,
              router_expert_w, router_expert_b, expert_w_gate, expert_w_up, expert_w_down, final_norm_g):
    for l in range(DEPTH):
        x = hybrid_layer(x, norm1_g[l], w_in[l], nsa_cmp_pe[l], nsa_cmp_w1[l], nsa_cmp_w2[l],
                         gla_wa[l], gla_ba[l], gla_norm_g[l], w_br_moba[l], w_br_nsa[l], w_br_gla[l],
                         w_out[l], norm2_g[l], router_group_w[l], router_group_b[l],
                         router_expert_w[l], router_expert_b[l], expert_w_gate[l], expert_w_up[l],
                         expert_w_down[l])
    return rmsnorm(x, final_norm_g)


_drawn_inputs = setup_inputs


def setup_inputs(seed=0):
    import zlib

    import numpy as np

    out = dict(_drawn_inputs(seed))
    spreads = {}
    factors = {'gla_ba': 8.0,
     'gla_norm_g': 15.165,
     'router_group_b': 64.0,
     'router_expert_b': 24.459,
     'final_norm_g': 7.653,
     'nsa_cmp_pe': 5.072,
     'norm2_g': 3.544}
    for name, (base, spread) in spreads.items():
        noise = np.random.default_rng([zlib.crc32(name.encode()), seed]).standard_normal(out[name].shape)
        drawn = base * np.exp(spread * noise) if base else spread * noise
        out[name] = __import__('jax').numpy.asarray(drawn.astype(out[name].dtype))
    for name, factor in factors.items():
        out[name] = (out[name] * factor).astype(out[name].dtype)
    return out
```

```python
from contextlib import ExitStack

import concourse.bass as bass
from concourse import mybir
from concourse.alu_op_type import AluOpType as ALU

F32 = mybir.dt.float32
I32 = mybir.dt.int32
ACT = mybir.ActivationFunctionType
AX_X = mybir.AxisListType.X

P = 128
T = 256
TT = T // P
D = 2048
KT = D // P
HD = 128
SCALE = HD ** -0.5
NEG = -1e30
EPS = 1e-6
TAU = 16.0
CMP_LEN, CMP_STRIDE = 32, 16
NCMP = (T - CMP_LEN) // CMP_STRIDE + 1
MH = NH = 8
KVH = 2
GH, GDV = 4, 256
LEVELS = 8
NE, GROUPS = 32, 4
EPG = NE // GROUPS
FF = 512
FT = FF // P
SLOTS = 64
NPAIR = NE // 2
W = 512

C_MQ, C_MK, C_MV, C_NQ, C_NKV = 0, 1024, 2048, 3072, 4096
C_NG = C_NKV + 1536
C_GQ = C_NG + 24
C_GK = C_GQ + 512
C_GV = C_GK + 512
C_GA = C_GV + 1024
C_GG = C_GA + 16
C_MG = C_GG + 1024

G_CMP = 14
N_FM = 10
N_GROUP = 18
B_GQ, B_GK, B_MQ, B_MK, B_NQ, B_KCMP, B_VCMP, B_KSLC, B_KWIN = 0, 4, 8, 16, 24, 32, 34, 36, 38
BRANCH_ORDER = (0, 2, 1)
CW = 256
N_CG = D // CW
UNITS = MH + 2 * NH


def unit_of(u):
    return ("moba", u) if u < MH else (("slc", "win")[(u - MH) % 2], (u - MH) // 2)


def schedule():
    steps = []
    nxt = [0]

    def unit_step(last):
        i = nxt[0]
        if i - 2 >= last:
            return
        if i >= 2:
            steps.append(("V", i - 2))
        if 1 <= i < last + 1:
            steps.append(("T", i - 1))
        if i < last:
            steps.append(("S", i))
        nxt[0] += 1

    for n in (10, 11):
        steps.extend(("tm", n, tt) for tt in range(TT))
    for n in (12, 13):
        for tt in range(TT):
            steps.append(("tm", n, tt))
            unit_step(MH)
    steps.append(("cmp1",))
    for i, tt in enumerate(range(TT)):
        steps.append(("tm", 15, tt))
        unit_step(MH)
        steps.append(("cmp2",) if i == 0 else ("cmp3",))
    for n in (16, 17):
        for tt in range(TT):
            steps.append(("tm", n, tt))
            unit_step(MH)
            steps.append(("gpv", 2 * (n - 16) + tt))
    while nxt[0] - 2 < MH:
        unit_step(MH)
    nxt[0] = MH
    steps.append(("gnorm",))
    first = [True]
    for m in range(N_CG):
        for part in range(4):
            steps.append(("mg", m, part))
            i = nxt[0]
            if i - 2 < UNITS and (part % 2 == 0 or m < 2):
                if i - 2 >= MH:
                    steps.append(("V", i - 2))
                if i - 1 >= MH and i - 1 < UNITS:
                    steps.append(("T", i - 1))
                if i < UNITS:
                    steps.append(("S", i))
                nxt[0] += 1
            if m == N_CG - 1:
                steps.append(("gtr", part))
    assert nxt[0] - 2 >= UNITS
    return steps


def build(nc, x, norm1_g, w_in, cmp_pe, cmp_w1, cmp_w2, gla_wa, gla_ba, gla_norm_g, w_br_moba, w_br_nsa,
          w_br_gla, w_out, norm2_g, rg_w, rg_b, re_w, re_b, e_gate, e_up, e_down, final_g, out):
    SCHED = schedule()
    with ExitStack() as ctx:
        def sb(name, shape, dt=F32):
            return ctx.enter_context(nc.sbuf_tensor(name, shape, dt))

        def sem(name):
            return ctx.enter_context(nc.semaphore(name))

        xs = sb("xs", [P, TT, D])
        hbuf = sb("hbuf", [P, KT * T])
        arena = sb("arena", [P, 40960])
        ident = sb("ident", [P, P])
        small = sb("small", [P, 5840])
        ps = ctx.enter_context(nc.psum_tensor("ps", [P, 8, 512], F32))

        def ar(a, n):
            return arena[:, a:a + n]

        def sm(a, n, parts=P):
            return small[0:parts, a:a + n]

        hT = hbuf[:, :].rearrange("p (k t) -> p k t", k=KT)
        h2 = hbuf[:, :].rearrange("p (a d) -> p a d", a=TT)
        SLOT = KT * W
        FM0 = 2 * SLOT
        TM0 = FM0 + 40 * T
        TMP0 = TM0 + 7 * TT * W
        slot = [ar(s * SLOT, SLOT).rearrange("p (k n) -> p k n", k=KT) for s in range(2)]
        cmpw = ar((G_CMP % 2) * SLOT, SLOT).rearrange("p (c l o) -> p c l o", c=2, l=CMP_LEN)
        mgw = [ar(s * SLOT, KT * CW).rearrange("p (k n) -> p k n", k=KT) for s in range(2)]
        brw = [ar(s * SLOT + KT * CW, 8 * CW).rearrange("p (k n) -> p k n", k=8) for s in range(2)]
        fm_flat = ar(FM0, 40 * T)
        fm = fm_flat.rearrange("p (b t) -> p b t", t=T)
        mv = ar(TM0, 2048).rearrange("p (a n) -> p a n", a=TT)
        gv = ar(TM0 + 2048, 2048).rearrange("p (a n) -> p a n", a=TT)
        gg = ar(TM0 + 4096, 2048).rearrange("p (a n) -> p a n", a=TT)
        kv35 = ar(TM0 + 6144, 1024).rearrange("p (a n) -> p a n", a=TT)
        oraw = ar(38912, 2048).rearrange("p (i n) -> p i n", i=2 * GH)
        merged = ar(TM0, KT * T).rearrange("p (k t) -> p k t", k=KT)
        ogT = ar(TM0 + 4096, 2048).rearrange("p (b t) -> p b t", t=T)
        xn = ar(FM0, 2 * D).rearrange("p (a d) -> p a d", a=TT)
        gb = ar(TMP0, 1024)
        gd = ar(TMP0 + 1024, 1024)
        gG = [ar(TMP0 + 2048 + 1024 * i, 1024) for i in range(2)]
        lmask = ar(TMP0 + 4224, 896).rearrange("p (l t) -> p l t", t=P)
        aP = [ar(TMP0 + 384 * i, 384) for i in range(2)]
        aPT = [ar(TMP0 + 768 + 384 * i, 384) for i in range(2)]
        cP = [ar(TMP0 + 1536 + 32 * i, 30).rearrange("p (a n) -> p a n", a=TT) for i in range(2)]
        cPT = [arena[0:NCMP, TMP0 + 1600 + 256 * i:TMP0 + 1856 + 256 * i] for i in range(2)]
        flat = ar(TMP0 + 2112, 1920).rearrange("p (c l n) -> p c l n", c=2, l=CMP_LEN)
        sg = [ar(TMP0 + 4096 + 512 * i, 512) for i in range(2)]
        wsm = sm(0, KT * 40).rearrange("p (k n) -> p k n", k=KT)
        g1row, perow, barow = sm(640, P, KT), sm(768, P, 64), sm(896, P, GH)
        gA = sm(0, TT * 512).rearrange("p (a h t) -> p a h t", a=TT, h=GH)
        gAoff = sm(1024, 512).rearrange("p (h t) -> p h t", h=GH)
        ng = sm(1536, 48).rearrange("p (a n) -> p a n", a=TT)
        ga = sm(1584, 32).rearrange("p (a n) -> p a n", a=TT)
        gaT = sm(1616, 256, 16)
        wa = sm(1872, 512, 16)
        junk256 = sm(1872, 256)
        causal = sm(2384, P)
        cadd = sm(2512, 30).rearrange("p (a n) -> p a n", a=TT)
        cmul = sm(2542, 30).rearrange("p (a n) -> p a n", a=TT)
        g1T, peT, baT = sm(2572, KT), sm(2588, 64), sm(2652, GH)
        w2 = sm(2656, 256).rearrange("p (c n) -> p c n", c=2)
        gng = sm(2912, 256)
        hidT = sm(3168, 60).rearrange("p (c n) -> p c n", c=2)
        kcT = sm(3228, 30)
        vc = sm(3258, 256, NCMP).rearrange("p (g n) -> p g n", g=KVH)
        ssx, rx = sm(3514, 4), sm(3518, 4)
        ssg, rg = sm(3522, 8), sm(3530, 8)
        mx = [sm(3540 + 4 * i, 4) for i in range(2)]
        nb = [sm(3548 + 4 * i, 4) for i in range(2)]
        su = [sm(3556 + 4 * i, 4) for i in range(2)]
        rr = [sm(3564 + 4 * i, 4) for i in range(2)]
        ss2, r2 = sm(5824, 4), sm(5828, 4)
        npass_f = sm(5832, 4)
        npass_i = npass_f[:, 0:1].bitcast(I32)
        g2b = sm(0, D)
        xgT = sm(0, 2048).rearrange("p (k s) -> p k s", k=KT)
        osb = sm(2048, 2048)
        gusb = sm(4096, 512)
        hmid = sm(4608, 256).rearrange("p (j s) -> p j s", j=FT)
        Sb = sm(4864, 256).rearrange("p (a s) -> p a s", a=TT)
        Gb = sm(5120, 256).rearrange("p (a s) -> p a s", a=TT)
        STb = sm(5376, 256)
        iota = sm(5632, SLOTS)
        posm = sm(5696, 64).rearrange("p (a e) -> p a e", a=TT)
        wgt = sm(5760, 64).rearrange("p (a e) -> p a e", a=TT)
        rw = sm(2816, KT * 36).rearrange("p (k n) -> p k n", k=KT)
        tri, ones = sm(2048, P), sm(2176, P)
        rbb = sm(2304, 36)
        jm = sm(2340, NE)
        lg = sm(2372, 72).rearrange("p (a n) -> p a n", a=TT)
        em = sm(2444, 64).rearrange("p (a n) -> p a n", a=TT)
        oh1 = sm(2508, 64).rearrange("p (a n) -> p a n", a=TT)
        t64 = sm(2572, 64).rearrange("p (a n) -> p a n", a=TT)
        oh2 = sm(2636, 64).rearrange("p (a n) -> p a n", a=TT)
        goh = sm(2700, 8).rearrange("p (a n) -> p a n", a=TT)
        t8 = sm(2708, 8).rearrange("p (a n) -> p a n", a=TT)
        rs = sm(2716, 40).rearrange("p (i a) -> p i a", a=TT)
        M = sm(3392, 64).rearrange("p (a n) -> p a n", a=TT)
        h2T = ar(0, KT * T).rearrange("p (k t) -> p k t", k=KT)
        UN = SLOT
        unit_g = [ar(u * UN, UN // 2).rearrange("p (j f) -> p j f", j=8) for u in range(4)]
        unit_u = [ar(u * UN + UN // 2, UN // 2).rearrange("p (j f) -> p j f", j=8) for u in range(4)]
        wd = ar(4 * UN, UN).rearrange("p (j n) -> p j n", j=FT)
        gfb = ar(0, D)

        s_x = [sem(f"s_x{t}") for t in range(TT)]
        s_rows, s_wsm, s_const = sem("s_rows"), sem("s_wsm"), sem("s_const")
        s_ident, s_masks = sem("s_ident"), sem("s_masks")
        s_ssx, s_ms, s_sq = sem("s_ssx"), sem("s_ms"), sem("s_sq")
        s_dve, s_act, s_pl = sem("s_dve"), sem("s_act"), sem("s_pl")
        s_xn, s_rowT, s_rowC = sem("s_xn"), sem("s_rowT"), sem("s_rowC")
        s_xT, s_hA, s_hD = sem("s_xT"), sem("s_hA"), sem("s_hD")
        s_smp, s_sma, s_gaT, s_gaTc, s_z = sem("s_smp"), sem("s_sma"), sem("s_gaT"), sem("s_gaTc"), sem("s_z")
        s_y, s_e, s_m, s_ln = sem("s_y"), sem("s_e"), sem("s_m"), sem("s_ln")
        s_w = [sem(f"s_w{s}") for s in range(2)]
        s_proj, s_ev = sem("s_proj"), sem("s_ev")
        s_gD, s_gE, s_gG, s_lv, s_gA = sem("s_gD"), sem("s_gE"), sem("s_gG"), sem("s_lv"), sem("s_gA")
        s_S, s_nb, s_exp, s_P, s_T, s_PT, s_V, s_O = (
            sem(n) for n in ("s_S", "s_nb", "s_exp", "s_P", "s_T", "s_PT", "s_V", "s_O"))
        s_flat, s_cmp1, s_hid, s_cmp2, s_kvc = (
            sem(n) for n in ("s_flat", "s_cmp1", "s_hid", "s_cmp2", "s_kvc"))
        s_gpv, s_gsq, s_gcp, s_gms, s_grt, s_on, s_gtr, s_ogT = (
            sem(n) for n in ("s_gpv", "s_gsq", "s_gcp", "s_gms", "s_grt", "s_on", "s_gtr", "s_ogT"))
        s_mg, s_sig, s_mrg = sem("s_mg"), sem("s_sig"), sem("s_mrg")
        s_wo, s_x2 = sem("s_wo"), sem("s_x2")
        s_g2, s_rw = sem("s_g2"), sem("s_rw")
        s_ss2, s_ms2, s_sq2, s_h2 = sem("s_ss2"), sem("s_ms2"), sem("s_sq2"), sem("s_h2")
        s_h2t, s_h2A, s_h2D, s_lgt, s_rc = sem("s_h2t"), sem("s_h2A"), sem("s_h2D"), sem("s_lgt"), sem("s_rc")
        s_re, s_rex, s_M, s_pos, s_route = sem("s_re"), sem("s_rex"), sem("s_M"), sem("s_pos"), sem("s_route")
        s_u = [sem(f"s_u{u}") for u in range(4)]
        s_wd = sem("s_wd")
        s_gu0, s_gu, s_gus, s_xg, s_xgA, s_xgD = (
            sem(n) for n in ("s_gu0", "s_gu", "s_gus", "s_xg", "s_xgA", "s_xgD"))
        s_G, s_Sm, s_tr, s_silu, s_mid, s_ST, s_STc = (
            sem(n) for n in ("s_G", "s_Sm", "s_tr", "s_silu", "s_mid", "s_ST", "s_STc"))
        s_dn, s_osb, s_sc, s_add = sem("s_dn"), sem("s_osb"), sem("s_sc"), sem("s_add")
        s_gf, s_ssf, s_msf, s_sqf, s_y1, s_out = (
            sem(n) for n in ("s_gf", "s_ssf", "s_msf", "s_sqf", "s_y1", "s_out"))

        x_v = x.rearrange("b (a p) d -> (b a) p d", p=P)
        out_v = out.rearrange("b (a p) d -> (b a) p d", p=P)
        win_v = w_in[0].rearrange("(k p) n -> p k n", p=P)
        wout_v = w_out[0].rearrange("(k p) n -> p k n", p=P)
        br_v = [w[0].rearrange("(k p) n -> p k n", p=P) for w in (w_br_moba, w_br_nsa, w_br_gla)]
        cmpw1_v = cmp_w1[0].rearrange("c (l d) o -> c d l o", d=HD)
        gate_v = e_gate.rearrange("a e (p j) f -> (a e) p j f", j=KT)
        up_v = e_up.rearrange("a e (p j) f -> (a e) p j f", j=KT)
        down_v = e_down.rearrange("a e (p j) n -> (a e) p j n", j=FT)

        cols = {0: C_GQ, 1: C_GK, 6: C_NQ, 7: C_NQ + W, 8: C_NKV, 10: C_MV, 11: C_MV + W, 12: C_GV,
                13: C_GV + W, 16: C_GG, 17: C_GG + W}
        split_cols = {9: (C_NKV + 512, C_NKV + 1024), 15: (C_NKV + 768, C_NKV + 1280)}

        block = ctx.enter_context(nc.Block())

        @block.sync
        def _(sp):
            for t in range(TT):
                sp.dma_start(xs[:, t, :], x_v[t]).then_inc(s_x[t], 16)
            sp.dma_start(g1row, norm1_g[0].rearrange("(k p) -> k p", p=P)).then_inc(s_rows, 16)
            sp.dma_start(perow, cmp_pe[0].rearrange("c l d -> (c l) d")).then_inc(s_rows, 16)
            sp.dma_start(barow, gla_ba[0].rearrange("(h p) -> h p", p=P)).then_inc(s_rows, 16)
            sp.dma_start(wsm[:, :, 0:24], win_v[:, :, C_NG:C_NG + 24]).then_inc(s_wsm, 16)
            sp.dma_start(wsm[:, :, 24:40], win_v[:, :, C_GA:C_GA + 16]).then_inc(s_wsm, 16)

            def load_group(n, col):
                for h in range(2):
                    sp.dma_start(slot[n % 2][:, 8 * h:8 * h + 8, :],
                                 win_v[:, 8 * h:8 * h + 8, col]).then_inc(s_w[n % 2], 16)

            for n in (0, 1):
                load_group(n, slice(cols[n], cols[n] + W))
            sp.dma_start(wa, gla_wa[0]).then_inc(s_const, 16)
            sp.dma_start(w2, cmp_w2[0].rearrange("c d o -> d c o")).then_inc(s_const, 16)
            sp.dma_start(gng, gla_norm_g[0].partition_broadcast(P)).then_inc(s_const, 16)
            with sp.Fori(0, 2) as j:
                for b in range(2):
                    sp.wait_ge(s_proj, 2 * j + b + 1)
                    load_group(b, bass.ds(j * (2 * W) + b * W, W))
            for n in range(6, N_GROUP):
                sp.wait_ge(s_proj, n - 1)
                if n == G_CMP:
                    for c in range(2):
                        sp.dma_start(cmpw[:, c], cmpw1_v[c]).then_inc(s_w[n % 2], 16)
                elif n in split_cols:
                    for h, c in enumerate(split_cols[n]):
                        sp.dma_start(slot[n % 2][:, :, CW * h:CW * h + CW],
                                     win_v[:, :, c:c + CW]).then_inc(s_w[n % 2], 16)
                else:
                    load_group(n, slice(cols[n], cols[n] + W))

            def load_gate_step(s, branch, cg):
                sp.dma_start(mgw[s], win_v[:, :, bass.ds(C_MG + branch * D + cg * CW, CW)]).then_inc(s_w[s], 16)
                sp.dma_start(brw[s], br_v[branch][:, :, bass.ds(cg * CW, CW)]).then_inc(s_w[s], 16)

            for m in range(2):
                sp.wait_ge(s_proj, 17 + m)
                load_gate_step(m, BRANCH_ORDER[0], m)
            with sp.Fori(1, N_CG // 2) as j:
                for s in range(2):
                    sp.wait_ge(s_mg, 2 * j + s - 1)
                    load_gate_step(s, BRANCH_ORDER[0], 2 * j + s)
            for bi in (1, 2):
                with sp.Fori(0, N_CG // 2) as j:
                    for s in range(2):
                        sp.wait_ge(s_mg, N_CG * bi + 2 * j + s - 1)
                        load_gate_step(s, BRANCH_ORDER[bi], 2 * j + s)

            def load_out(s, g):
                for h in range(2):
                    sp.dma_start(slot[s][:, 8 * h:8 * h + 8, :],
                                 wout_v[:, 8 * h:8 * h + 8, bass.ds(g * W, W)]).then_inc(s_w[s], 16)

            def load_gu(u, e, h):
                sp.dma_start(unit_g[u], gate_v[bass.ds(e, 1), :, 8 * h:8 * h + 8].rearrange(
                    "e p j f -> (e p) j f")).then_inc(s_u[u], 16)
                sp.dma_start(unit_u[u], up_v[bass.ds(e, 1), :, 8 * h:8 * h + 8].rearrange(
                    "e p j f -> (e p) j f")).then_inc(s_u[u], 16)

            def load_down(e):
                for h in range(2):
                    sp.dma_start(wd[:, 2 * h:2 * h + 2], down_v[bass.ds(e, 1), :, 2 * h:2 * h + 2].rearrange(
                        "e p j n -> (e p) j n")).then_inc(s_wd, 16)

            for g in range(2):
                sp.wait_ge(s_mg, 3 * N_CG - 1 + g)
                load_out(g, g)
            sp.dma_start(g2b, norm2_g[0].partition_broadcast(P)).then_inc(s_g2, 16)
            sp.dma_start(rw[:, :, 0:GROUPS], rg_w[0].rearrange("(k p) n -> p k n", p=P)).then_inc(s_rw, 16)
            sp.dma_start(rw[:, :, GROUPS:36], re_w[0].rearrange("(k p) n -> p k n", p=P)).then_inc(s_rw, 16)
            sp.dma_start(rbb[:, 0:GROUPS], rg_b[0].partition_broadcast(P)).then_inc(s_rw, 16)
            sp.dma_start(rbb[:, GROUPS:36], re_b[0].partition_broadcast(P)).then_inc(s_rw, 16)
            for g in range(2, 4):
                sp.wait_ge(s_wo, g - 1)
                load_out(g % 2, g)
            load_gu(2, 0, 0)
            load_down(0)
            sp.wait_ge(s_wo, 4)
            load_gu(3, 0, 1)

            sp.wait_ge(s_route, 1)

            def load_expert(e, n, par):
                for h in range(2):
                    u = (2, 0)[par] + h
                    load_gu(u, e, h)

            npass = sp.value_load(npass_i[0:1, 0:1], min_val=1, max_val=T // SLOTS)

            for h in range(2):
                load_gu(h, 1, h)

            def rest_of(n, e0):
                for q in range(2):
                    for h in range(2):
                        sp.wait_ge(s_gu0 if h == 0 else s_gu, n + q + 1)
                        load_gu((2, 0)[q] + h, e0 + 2 + q, h)
                    sp.wait_ge(s_dn, n + q + 1)
                    load_down(e0 + 1 + q)

            with sp.Fori(0, NE // 2 - 1) as i:
                rest_of(2 * i, 2 * i)
            sp.wait_ge(s_dn, NE - 1)
            load_down(NE - 1)
            with sp.If(npass > 1):
                with sp.Fori(1, npass) as q:
                    base = q * NE
                    for h in range(2):
                        sp.wait_ge(s_gu0 if h == 0 else s_gu, base - 1)
                        load_gu(2 + h, 0, h)
                    sp.wait_ge(s_dn, base)
                    load_down(0)
                    for h in range(2):
                        sp.wait_ge(s_gu, base)
                        load_gu(h, 1, h)
                    with sp.Fori(0, NE // 2 - 1) as i:
                        rest_of(base + 2 * i, 2 * i)
                    sp.wait_ge(s_dn, base + NE - 1)
                    load_down(NE - 1)

            sp.wait_ge(s_gu, npass * NE)
            sp.dma_start(gfb, final_g.partition_broadcast(P)).then_inc(s_gf, 16)
            for t in range(TT):
                sp.wait_ge(s_y1, t + 1)
                sp.dma_start(out_v[t], h2[:, t, :]).then_inc(s_out, 16)
            sp.wait_ge(s_out, 16 * TT)

        @block.gpsimd
        def _(pool):
            done = [0]

            def link(ins):
                done[0] += 1
                ins.then_inc(s_pl, 1)
                pool.wait_ge(s_pl, done[0])

            link(nc.gpsimd.memset(ident[:, :], 0.0))
            nc.gpsimd.affine_select(out=ident[:, :], in_=ident[:, :], compare_op=ALU.not_equal, fill=1.0,
                                    base=0, pattern=[[-1, P]], channel_multiplier=1).then_inc(s_ident, 1)
            link(nc.gpsimd.memset(causal, 0.0))
            nc.gpsimd.affine_select(out=causal, in_=causal, compare_op=ALU.is_ge, fill=NEG, base=0,
                                    pattern=[[-1, P]], channel_multiplier=1).then_inc(s_masks, 1)
            link(nc.gpsimd.memset(cadd, 0.0))
            link(nc.gpsimd.memset(cmul, 1.0))
            for t in range(TT):
                for m, fill in ((cadd, NEG), (cmul, 0.0)):
                    nc.gpsimd.affine_select(out=m[:, t], in_=m[:, t], compare_op=ALU.is_ge, fill=fill,
                                            base=t * P - CMP_LEN + 1, pattern=[[-CMP_STRIDE, NCMP]],
                                            channel_multiplier=1).then_inc(s_masks, 1)
            link(nc.gpsimd.memset(lmask, 0.0))
            for lv in range(LEVELS - 1):
                H = 1 << lv
                v = lmask[:, lv].rearrange("p (n two r) -> p n two r", two=2, r=H)[:, :, 1, :]
                link(nc.gpsimd.memset(v, 1.0))
                link(nc.gpsimd.affine_select(out=v, in_=v, compare_op=ALU.is_ge, fill=0.0, base=0,
                                             pattern=[[-2 * H, P // (2 * H)], [0, H]], channel_multiplier=1))
                nc.gpsimd.affine_select(out=v, in_=v, compare_op=ALU.is_ge, fill=0.0, base=H - 1,
                                        pattern=[[2 * H, P // (2 * H)], [0, H]],
                                        channel_multiplier=-1).then_inc(s_masks, 1)
            pool.wait_ge(s_mg, 3 * N_CG)
            nc.gpsimd.iota(jm, pattern=[[1, NE]], base=-64, channel_multiplier=0,
                           allow_small_or_imprecise_dtypes=True).then_inc(s_rc, 1)
            nc.gpsimd.iota(iota, pattern=[[1, SLOTS]], base=0,
                           channel_multiplier=0, allow_small_or_imprecise_dtypes=True).then_inc(s_rc, 1)
            nc.gpsimd.memset(ones, 1.0).then_inc(s_rc, 1)
            link(nc.gpsimd.memset(tri, 1.0))
            nc.gpsimd.affine_select(out=tri, in_=tri, compare_op=ALU.is_gt, fill=0.0, base=0,
                                    pattern=[[1, P]], channel_multiplier=-1).then_inc(s_rc, 1)

        N_MASKS = 1 + 2 * TT + LEVELS - 1

        @block.tensor
        def _(pe):
            mm = nc.tensor.matmul

            pe.wait_ge(s_ident, 1)
            pe.wait_ge(s_rows, 48)
            nc.tensor.transpose(ps[:, 0, 0:KT], g1row, ident[0:KT, 0:KT])
            nc.tensor.transpose(ps[:, 0, 16:80], perow, ident[0:64, 0:64])
            nc.tensor.transpose(ps[:, 0, 80:84], barow, ident[0:GH, 0:GH]).then_inc(s_rowT, 1)
            pe.wait_ge(s_xn, TT)
            for i in range(KT // 2):
                if i >= 4:
                    pe.wait_ge(s_hA if i % 2 else s_hD, (i - 4) // 2 + 1)
                for k in (2 * i, 2 * i + 1):
                    for t in range(TT):
                        last = nc.tensor.transpose(ps[:, 4 + i % 4, (k % 2) * T + t * P:(k % 2) * T + t * P + P],
                                                   xn[:, t, k * P:k * P + P], ident[:, :])
                last.then_inc(s_xT, 1)
            pe.wait_ge(s_hA, KT // 4)
            pe.wait_ge(s_hD, KT // 4)

            pe.wait_ge(s_wsm, 32)
            for t in range(TT):
                for k in range(KT):
                    last = mm(ps[:, 4, 64 * t:64 * t + 40], hT[:, k, t * P:t * P + P], wsm[:, k, :],
                              start=k == 0, stop=k == KT - 1)
            last.then_inc(s_smp, 1)

            def fm_chunk(n, s, b):
                o = ps[:, 2 * s + b // 2, (b % 2) * T:(b % 2) * T + T]
                for k in range(KT):
                    last = mm(o, slot[s][:, k, b * P:b * P + P], hT[:, k, :], start=k == 0, stop=k == KT - 1)
                return last

            def fm_group(n, s):
                pe.wait_ge(s_w[s], 32 * ((n - s) // 2 + 1) if isinstance(n, int) else (n - s) * 16 + 32)
                if not isinstance(n, int) or n >= 2:
                    pe.wait_ge(s_ev, n - 1)
                for b in range(4):
                    last = fm_chunk(n, s, b)
                last.then_inc(s_proj, 1)

            fm_group(0, 0)
            pe.wait_ge(s_sma, 1)
            for t in range(TT):
                last = nc.tensor.transpose(ps[0:16, 5, t * P:t * P + P], ga[:, t, :], ident[:, :])
            last.then_inc(s_gaT, 1)
            pe.wait_ge(s_const, 48)
            pe.wait_ge(s_gaTc, 1)
            for h in range(GH):
                last = mm(ps[:, 6 + h // 2, (h % 2) * T:(h % 2) * T + T], wa[:, h * P:h * P + P], gaT,
                          start=True, stop=True)
            last.then_inc(s_z, 1)
            fm_group(1, 1)

            pe.wait_ge(s_ev, 2)
            for t in range(TT):
                for h in range(GH):
                    last = mm(ps[:, 4 + t, h * P:h * P + P], fm[:, B_GK + h, t * P:t * P + P],
                              fm[:, B_GQ + h, t * P:t * P + P], start=True, stop=True)
            last.then_inc(s_lv, 1)

            def level(buf, count):
                pe.wait_ge(s_gG, count)
                pe.wait_ge(s_gA, count)
                g = gG[buf].rearrange("p (h t) -> p h t", h=GH)
                for t in range(TT):
                    for h in range(GH):
                        last = mm(ps[:, 4 + t, h * P:h * P + P], g[:, h, t * P:t * P + P],
                                  g[:, h, t * P:t * P + P], start=True, stop=True)
                last.then_inc(s_lv, 1)

            with pe.Fori(0, 3) as j:
                for b in range(2):
                    fm_group(j * 2 + (2 + b), b)
                    level(b, j * 2 + (1 + b))
            fm_group(8, 0)
            level(0, 7)
            fm_group(9, 1)
            pe.wait_ge(s_gG, 8)
            pe.wait_ge(s_gA, 8)
            g = gG[1].rearrange("p (h t) -> p h t", h=GH)
            for h in range(GH):
                last = mm(ps[:, 4, h * P:h * P + P], g[:, h, 0:P], g[:, h, P:T], start=True, stop=True)
            last.then_inc(s_lv, 1)

            def scores(u):
                kind, h = unit_of(u)
                g = h // (NH // KVH)
                q = fm[:, (B_MQ if kind == "moba" else B_NQ) + h]
                k = fm[:, {"moba": B_MK + h, "slc": B_KSLC + g, "win": B_KWIN + g}[kind]]
                if u >= 1:
                    pe.wait_ge(s_exp, u)
                if u == 0:
                    pe.wait_ge(s_ev, N_FM)
                mm(ps[:, 6, 0:P], q[:, 0:P], k[:, 0:P], start=True, stop=False)
                mm(ps[:, 6, 0:P], ident[:, :], causal, start=False, stop=True)
                mm(ps[:, 6, P:3 * P], q[:, P:T], k, start=True, stop=False)
                last = mm(ps[:, 6, 2 * P:3 * P], ident[:, :], causal, start=False, stop=True)
                if kind == "slc":
                    pe.wait_ge(s_kvc, 1)
                    for t in range(TT):
                        o = ps[:, 6, 384 + 16 * t:384 + 16 * t + NCMP]
                        mm(o, q[:, t * P:t * P + P], kcT[:, g * NCMP:(g + 1) * NCMP], start=True, stop=False)
                        last = mm(o, ident[:, :], cadd[:, t], start=False, stop=True)
                last.then_inc(s_S, 1)

            def turn(u):
                kind, h = unit_of(u)
                pe.wait_ge(s_P, u + 1)
                for b in range(3):
                    last = nc.tensor.transpose(ps[:, 7, b * P:b * P + P], aP[u % 2][:, b * P:b * P + P], ident[:, :])
                if kind == "slc":
                    for t in range(TT):
                        last = nc.tensor.transpose(ps[0:NCMP, 5, t * P:t * P + P], cP[h % 2][:, t], ident[:, :])
                last.then_inc(s_T, 1)

            def values(u):
                kind, h = unit_of(u)
                g = h // (NH // KVH)
                o = ps[:, 4, (h % 2) * T:(h % 2) * T + T]
                pe.wait_ge(s_PT, u + 1)
                if kind != "win":
                    hh = h if kind == "moba" else MH + h
                    if hh >= 1:
                        pe.wait_ge(s_O, hh)
                    if hh == 0:
                        pe.wait_ge(s_gA, 9)
                if kind == "moba":
                    v = mv[:, :, h * HD:h * HD + HD]
                    if h % 4 == 0:
                        pe.wait_ge(s_ev, 11 + h // 4)
                elif kind == "slc":
                    v = kv35[:, :, g * HD:g * HD + HD]
                    mm(o, vc[:, g], cPT[h % 2], start=True, stop=False)
                    if h == 0:
                        pe.wait_ge(s_ev, 16)
                else:
                    v = kv35[:, :, CW + g * HD:CW + g * HD + HD]
                pt = aPT[u % 2]
                mm(o, v[:, 0], pt[:, 0:T], start=kind == "moba", stop=False)
                last = mm(o[:, P:T], v[:, 1], pt[:, T:T + P], start=False, stop=kind != "slc")
                last.then_inc(s_V, 1)

            def gla_values(h):
                if h == 0:
                    pe.wait_ge(s_gA, 9)
                    pe.wait_ge(s_ev, 14)
                else:
                    pe.wait_ge(s_gcp, h)
                vh = gv[:, :, h * GDV:(h + 1) * GDV]
                mm(ps[:, 5, 0:GDV], gA[:, 0, h], vh[:, 0], start=True, stop=True)
                mm(ps[:, 5, GDV:2 * GDV], gAoff[:, h], vh[:, 0], start=True, stop=False)
                mm(ps[:, 5, GDV:2 * GDV], gA[:, 1, h], vh[:, 1], start=False, stop=True).then_inc(s_gpv, 1)

            def gate_part(s, part, wait_n, br, br_block, first_wait=None):
                b = part % 2
                if part < 2:
                    for k in range(KT):
                        last = mm(ps[:, 2 * s, b * T:b * T + T], mgw[s][:, k, b * P:b * P + P], hT[:, k, :],
                                  start=k == 0, stop=k == KT - 1)
                else:
                    for k in range(8):
                        last = mm(ps[:, 2 * s + 1, b * T:b * T + T], brw[s][:, k, b * P:b * P + P],
                                  br[:, br_block + k, :], start=k == 0, stop=k == 7)
                if part == 3:
                    last.then_inc(s_mg, 1)

            seen_loads = {s: 9 for s in range(2)}
            for step in SCHED:
                if step[0] == "tm":
                    _, n, t = step
                    s = n % 2
                    if t == 0:
                        pe.wait_ge(s_w[s], 32 * (n // 2 + 1))
                        pe.wait_ge(s_ev, n - 1)
                    if n == 16 and t == 0:
                        pe.wait_ge(s_kvc, 1)
                    for k in range(KT):
                        last = mm(ps[:, 2 * s + t, :], hT[:, k, t * P:t * P + P], slot[s][:, k, :],
                                  start=k == 0, stop=k == KT - 1)
                    if t == 1:
                        last.then_inc(s_proj, 1)
                elif step[0] == "cmp1":
                    pe.wait_ge(s_w[0], 32 * (G_CMP // 2 + 1))
                    pe.wait_ge(s_ev, G_CMP - 1)
                    pe.wait_ge(s_flat, 1)
                    for c in range(2):
                        for l in range(CMP_LEN):
                            last = mm(ps[:, 0, 32 * c:32 * c + 30], cmpw[:, c, l], flat[:, c, l],
                                      start=l == 0, stop=l == CMP_LEN - 1)
                    last.then_inc(s_proj, 1)
                elif step[0] == "cmp2":
                    pe.wait_ge(s_ev, 15)
                    mm(ps[:, 1, 0:30], w2[:, 0], hidT[:, 0], start=True, stop=True)
                    for g in range(KVH):
                        last = mm(ps[0:NCMP, 1, 64 + P * g:64 + P * g + P], hidT[:, 1, g * NCMP:(g + 1) * NCMP],
                                  w2[:, 1], start=True, stop=True)
                    last.then_inc(s_cmp2, 1)
                elif step[0] == "S":
                    scores(step[1])
                elif step[0] == "T":
                    turn(step[1])
                elif step[0] == "V":
                    values(step[1])
                elif step[0] == "gpv":
                    gla_values(step[1])
                elif step[0] == "gtr":
                    h = step[1]
                    pe.wait_ge(s_on, 2 * h + 2)
                    if h >= 1:
                        pe.wait_ge(s_ogT, h)
                    for eh in range(2):
                        for t in range(TT):
                            last = nc.tensor.transpose(ps[:, 5, eh * T + t * P:eh * T + t * P + P],
                                                       oraw[:, 2 * h + t, eh * P:eh * P + P], ident[:, :])
                    last.then_inc(s_gtr, 1)
                elif step[0] == "mg":
                    _, m, part = step
                    s = m % 2
                    if part == 0:
                        pe.wait_ge(s_w[s], 32 * (9 + m // 2 + 1))
                        if m < 2:
                            pe.wait_ge(s_ev, 17 + m)
                        else:
                            pe.wait_ge(s_mrg, m - 1)
                    if part == 2 and m == 0:
                        pe.wait_ge(s_O, MH)
                    gate_part(s, part, None, fm, B_MQ)

            for bi in (1, 2):
                if bi == 1:
                    pe.wait_ge(s_ogT, GH)
                else:
                    pe.wait_ge(s_O, MH + NH)
                with pe.Fori(0, N_CG // 2) as j:
                    for s in range(2):
                        pe.wait_ge(s_w[s], j * 32 + 32 * (9 + 4 * bi + 1))
                        pe.wait_ge(s_mrg, j * 2 + (N_CG * bi + s - 1))
                        for part in range(4):
                            if bi == 1:
                                gate_part(s, part, None, ogT, 0)
                            else:
                                gate_part(s, part, None, fm, B_NQ)

            pe.wait_ge(s_mrg, 3 * N_CG)
            with pe.Fori(0, 2) as j:
                for s in range(2):
                    pe.wait_ge(s_w[s], j * 32 + 32 * (9 + 12 + 1))
                    pe.wait_ge(s_x2, j * 2 + s + 1)
                    for t in range(TT):
                        for k in range(KT):
                            last = mm(ps[:, 2 * s + t, :], merged[:, k, t * P:t * P + P], slot[s][:, k, :],
                                      start=k == 0, stop=k == KT - 1)
                    last.then_inc(s_wo, 1)

            pe.wait_ge(s_h2, TT)
            for i in range(KT // 2):
                if i >= 4:
                    pe.wait_ge(s_h2A if i % 2 else s_h2D, (i - 4) // 2 + 1)
                for k in (2 * i, 2 * i + 1):
                    for t in range(TT):
                        last = nc.tensor.transpose(ps[:, 4 + i % 4, (k % 2) * T + t * P:(k % 2) * T + t * P + P],
                                                   h2[:, t, k * P:k * P + P], ident[:, :])
                last.then_inc(s_h2t, 1)
            pe.wait_ge(s_h2A, KT // 4)
            pe.wait_ge(s_h2D, KT // 4)
            pe.wait_ge(s_rw, 64)
            for t in range(TT):
                for k in range(KT):
                    last = mm(ps[:, 0, 64 * t:64 * t + 36], h2T[:, k, t * P:t * P + P], rw[:, k, :],
                              start=k == 0, stop=k == KT - 1)
            last.then_inc(s_lgt, 1)
            pe.wait_ge(s_rc, 4)
            pe.wait_ge(s_M, 1)
            mm(ps[:, 1, 0:NE], tri, M[:, 0], start=True, stop=True)
            mm(ps[:, 1, NE:2 * NE], ones, M[:, 0], start=True, stop=False)
            mm(ps[:, 1, NE:2 * NE], tri, M[:, 1], start=False, stop=True)
            mm(ps[:, 1, 2 * NE:3 * NE], ones, M[:, 0], start=True, stop=False)
            mm(ps[:, 1, 2 * NE:3 * NE], ones, M[:, 1], start=False, stop=True).then_inc(s_pos, 1)
            pe.wait_ge(s_route, 1)
            npass = pe.value_load(npass_i[0:1, 0:1], min_val=1, max_val=T // SLOTS)

            def gather(m, half):
                for k in range(8 * half, 8 * half + 8):
                    o = ps[:, 2 + k // 4, (k % 4) * P:(k % 4 + 1) * P]
                    for t in range(TT):
                        last = mm(o, h2[:, t, :].rearrange("p (c k) -> p k c", k=KT)[:, k], Gb[:, t],
                                  start=t == 0, stop=t == TT - 1)
                last.then_inc(s_xg, 1)

            def scatter(m, t):
                if t == 0:
                    pe.wait_ge(s_osb, m * 2 + 2)
                for c in range(4):
                    if t == 1:
                        pe.wait_ge(s_add, m * 8 + (c + 2))
                    mm(ps[:, 2 + c, :], STb[:, t * P:t * P + P], osb[:, c * W:c * W + W],
                       start=True, stop=True).then_inc(s_sc, 1)

            def gate_up(n, par, uses, m):
                for h in range(2):
                    u = (2, 0)[par] + h
                    pe.wait_ge(s_u[u], uses * 32 + 32)
                    if h == 0 and par == 0:
                        pe.wait_ge(s_xgA, m + 1)
                        pe.wait_ge(s_xgD, m + 1)
                        pe.wait_ge(s_STc, m + 1)
                    for j in range(8):
                        k = 8 * h + j
                        xk = xgT[:, k, par * SLOTS:par * SLOTS + SLOTS]
                        mm(ps[0:SLOTS, 0, :], xk, unit_g[u][:, j], start=k == 0, stop=k == KT - 1)
                        a = mm(ps[SLOTS:P, 0, :], xk, unit_u[u][:, j], start=k == 0, stop=k == KT - 1)
                    a.then_inc(s_gu0 if h == 0 else s_gu, 1)

            def turn_gate_up(n):
                pe.wait_ge(s_gus, n + 1)
                for j in range(FT):
                    a = nc.tensor.transpose(ps[:, 1, j * P:j * P + P],
                                            gusb.rearrange("p (c j) -> p j c", j=FT)[:, j], ident[:, :])
                a.then_inc(s_tr, 1)

            def down(n):
                pe.wait_ge(s_mid, n + 1)
                pe.wait_ge(s_wd, n * 32 + 32)
                for c in range(2):
                    for j in range(FT):
                        mm(ps[0:SLOTS, 6 + c, :], hmid[:, j], wd[:, j, c * W:c * W + W],
                           start=j == 0, stop=j == FT - 1)
                        a = mm(ps[SLOTS:P, 6 + c, :], hmid[:, j], wd[:, j, 1024 + c * W:1024 + c * W + W],
                               start=j == 0, stop=j == FT - 1)
                a.then_inc(s_dn, 1)

            def pair(m, uses, first, last_of_pass):
                n = m * 2
                gate_up(n, 0, uses, m)
                if not first:
                    scatter(m - 1, 0)
                turn_gate_up(n)
                if not first:
                    scatter(m - 1, 1)
                down(n)
                gate_up(n + 1, 1, uses, m)
                if not last_of_pass:
                    pe.wait_ge(s_G, m + 2)
                    pe.wait_ge(s_add, m * 8 + 1)
                    gather(m + 1, 0)
                turn_gate_up(n + 1)
                if not last_of_pass:
                    gather(m + 1, 1)
                pe.wait_ge(s_Sm, m + 1)
                for t in range(TT):
                    a = nc.tensor.transpose(ps[:, 0, t * P:t * P + P], Sb[:, t], ident[:, :])
                a.then_inc(s_ST, 1)
                pe.wait_ge(s_osb, n + 1)
                down(n + 1)

            with pe.Fori(0, npass) as q:
                base = q * NPAIR
                pe.wait_ge(s_G, base + 1)
                pe.wait_ge(s_add, q * (8 * NPAIR) + 1)
                for half in range(2):
                    gather(base, half)
                pair(base, q * NPAIR, True, False)
                with pe.Fori(1, NPAIR - 1) as i:
                    pair(base + i, q * NPAIR + i, False, False)
                pair(base + (NPAIR - 1), q * NPAIR + (NPAIR - 1), False, True)
                for t in range(TT):
                    scatter(base + (NPAIR - 1), t)

        @block.scalar
        def _(act):
            done = [0]

            def link(ins):
                done[0] += 1
                ins.then_inc(s_act, 1)
                act.wait_ge(s_act, done[0])

            A = nc.scalar.activation
            for t in range(TT):
                act.wait_ge(s_x[t], 16)
                A(ar(TM0 + 2048 * t, D), xs[:, t, :], ACT.Square, accum_out=ssx[:, t:t + 1]).then_inc(s_ssx, 1)
            act.wait_ge(s_ms, 1)
            A(rx[:, 0:TT], ssx[:, 2:2 + TT], ACT.Sqrt).then_inc(s_sq, 1)
            act.wait_ge(s_rowT, 1)
            A(small[:, 2572:2572 + 84], ps[:, 0, 0:84], ACT.Copy).then_inc(s_rowC, 1)
            act.wait_ge(s_rowC, 1)
            for i in range(1, KT // 2, 2):
                act.wait_ge(s_xT, i + 1)
                for k in (2 * i, 2 * i + 1):
                    ins = nc.scalar.mul(hT[:, k, :], ps[:, 4 + i % 4, (k % 2) * T:(k % 2) * T + T], g1T[:, k:k + 1])
                ins.then_inc(s_hA, 1)
            act.wait_ge(s_smp, 1)
            smp = ps[:, 4, 0:128].rearrange("p (a n) -> p a n", a=TT)
            A(ng, smp[:, :, 0:24], ACT.Sigmoid)
            A(ga, smp[:, :, 24:40], ACT.Copy).then_inc(s_sma, 1)
            act.wait_ge(s_gaT, 1)
            A(gaT, ps[0:16, 5, 0:T], ACT.Copy).then_inc(s_gaTc, 1)

            def evac_fm(n, s):
                act.wait_ge(s_proj, n + 1)
                A(fm_flat[:, bass.ds(n * 1024, 1024)], ps[:, 2 * s:2 * s + 2, :].rearrange("p a n -> p (a n)"),
                  ACT.Copy).then_inc(s_ev, 1)

            act.wait_ge(s_y, 1)
            A(gG[0], gG[0], ACT.Exp, scale=-1.0).then_inc(s_e, 1)
            act.wait_ge(s_e, 1)
            A(gG[0], gG[0], ACT.Ln, bias=1.0).then_inc(s_ln, 1)
            evac_fm(0, 0)
            evac_fm(1, 1)

            def level_exp(count):
                act.wait_ge(s_gD, count)
                A(gd, gd, ACT.Exp, scale=1.0 / TAU).then_inc(s_gE, 1)

            level_exp(1)
            with act.Fori(0, 3) as j:
                for b in range(2):
                    evac_fm(j * 2 + (2 + b), b)
                    level_exp(j * 2 + (2 + b))
            evac_fm(8, 0)
            level_exp(8)
            evac_fm(9, 1)

            for step in SCHED:
                if step[0] == "tm" and step[2] == 1:
                    n = step[1]
                    s = n % 2
                    act.wait_ge(s_proj, n + 1)
                    dst = {10: mv[:, :, 0:W], 11: mv[:, :, W:2 * W], 12: gv[:, :, 0:W], 13: gv[:, :, W:2 * W],
                           15: kv35, 16: gg[:, :, 0:W], 17: gg[:, :, W:2 * W]}[n]
                    A(dst, ps[:, 2 * s:2 * s + 2, :], ACT.Silu if n in (16, 17) else ACT.Copy).then_inc(s_ev, 1)
                elif step[0] == "cmp1":
                    act.wait_ge(s_proj, G_CMP + 1)
                    A(hidT, ps[:, 0, 0:64].rearrange("p (c n) -> p c n", c=2)[:, :, 0:30], ACT.Silu).then_inc(s_ev, 1)
                elif step[0] == "cmp3":
                    act.wait_ge(s_cmp2, 1)
                    A(kcT, ps[:, 1, 0:30], ACT.Copy)
                    A(vc, ps[0:NCMP, 1, 64:64 + 2 * P].rearrange("p (g n) -> p g n", g=KVH), ACT.Copy).then_inc(s_kvc, 1)
                elif step[0] == "S":
                    u = step[1]
                    kind, h = unit_of(u)
                    act.wait_ge(s_nb, u + 1)
                    b = nb[u % 2]
                    A(aP[u % 2][:, 0:P], ps[:, 6, 0:P], ACT.Exp, bias=b[:, 0:1], scale=SCALE,
                      accum_out=su[u % 2][:, 0:1])
                    last = A(aP[u % 2][:, P:3 * P], ps[:, 6, P:3 * P], ACT.Exp, bias=b[:, 1:2], scale=SCALE,
                             accum_out=su[u % 2][:, 1:2])
                    if kind == "slc":
                        for t in range(TT):
                            last = A(cP[h % 2][:, t], ps[:, 6, 384 + 16 * t:384 + 16 * t + NCMP], ACT.Exp,
                                     bias=b[:, 2 + t:3 + t], scale=SCALE, accum_out=su[u % 2][:, 2 + t:3 + t])
                    last.then_inc(s_exp, 1)
                elif step[0] == "T":
                    u = step[1]
                    kind, h = unit_of(u)
                    act.wait_ge(s_T, u + 1)
                    last = A(aPT[u % 2], ps[:, 7, 0:3 * P], ACT.Copy)
                    if kind == "slc":
                        last = A(cPT[h % 2], ps[0:NCMP, 5, 0:T], ACT.Copy)
                    last.then_inc(s_PT, 1)
                elif step[0] == "gpv":
                    h = step[1]
                    act.wait_ge(s_gcp, h + 1)
                    if h >= 1:
                        act.wait_ge(s_gsq, h)
                    link(A(junk256, oraw[:, 2 * h], ACT.Square, accum_out=ssg[:, 2 * h:2 * h + 1]))
                    A(junk256, oraw[:, 2 * h + 1], ACT.Square, accum_out=ssg[:, 2 * h + 1:2 * h + 2]).then_inc(s_gsq, 1)
                elif step[0] == "gnorm":
                    act.wait_ge(s_gms, 1)
                    A(rg, ssg, ACT.Sqrt).then_inc(s_grt, 1)
                elif step[0] == "gtr":
                    h = step[1]
                    act.wait_ge(s_gtr, h + 1)
                    A(ogT[:, 2 * h:2 * h + 2].rearrange("p b t -> p (b t)"), ps[:, 5, :], ACT.Copy).then_inc(s_ogT, 1)
                elif step[0] == "mg" and step[2] == 3:
                    m = step[1]
                    act.wait_ge(s_mg, m + 1)
                    if m >= 2:
                        act.wait_ge(s_mrg, m - 1)
                    A(sg[m % 2], ps[:, 2 * (m % 2), :], ACT.Sigmoid).then_inc(s_sig, 1)
            with act.Fori(N_CG // 2, 3 * N_CG // 2) as j:
                for s in range(2):
                    act.wait_ge(s_mg, j * 2 + s + 1)
                    act.wait_ge(s_mrg, j * 2 + s - 1)
                    A(sg[s], ps[:, 2 * s, :], ACT.Sigmoid).then_inc(s_sig, 1)

            act.wait_ge(s_x2, 5)
            for t in range(TT):
                A(h2[:, t, :], xs[:, t, :], ACT.Square, accum_out=ss2[:, t:t + 1]).then_inc(s_ss2, 1)
            act.wait_ge(s_ms2, 1)
            A(r2[:, 0:TT], ss2[:, 2:4], ACT.Sqrt).then_inc(s_sq2, 1)
            for i in range(1, KT // 2, 2):
                act.wait_ge(s_h2t, i + 1)
                A(h2T[:, 2 * i:2 * i + 2, :].rearrange("p k t -> p (k t)"), ps[:, 4 + i % 4, :], ACT.Copy).then_inc(s_h2A, 1)
            act.wait_ge(s_re, 1)
            A(t8, t8, ACT.Exp)
            A(rs[:, 5], rs[:, 5], ACT.Exp).then_inc(s_rex, 1)
            act.wait_ge(s_route, 1)
            npass = act.value_load(npass_i[0:1, 0:1], min_val=1, max_val=T // SLOTS)

            def copy_xg(m):
                act.wait_ge(s_xg, m * 2 + 1)
                A(xgT[:, 0:8].rearrange("p k s -> p (k s)"), ps[:, 2:4, :].rearrange("p a n -> p (a n)"),
                  ACT.Copy).then_inc(s_xgA, 1)

            def copy_gu(n):
                act.wait_ge(s_gu, n + 1)
                A(gusb, ps[:, 0, :], ACT.Copy).then_inc(s_gus, 1)

            def silu(n):
                act.wait_ge(s_tr, n + 1)
                tr = ps[:, 1, :].rearrange("p (j two s) -> p j two s", two=2, s=SLOTS)
                A(hmid, tr[:, :, 0], ACT.Silu).then_inc(s_silu, 1)

            def copy_out(n, par):
                act.wait_ge(s_dn, n + 1)
                o = osb[par * SLOTS:par * SLOTS + SLOTS]
                A(o[:, 0:1024], ps[0:SLOTS, 6:8, :].rearrange("p a n -> p (a n)"), ACT.Copy)
                A(o[:, 1024:D], ps[SLOTS:P, 6:8, :].rearrange("p a n -> p (a n)"), ACT.Copy).then_inc(s_osb, 1)

            def pair(m, last_of_pass):
                n = m * 2
                copy_gu(n)
                silu(n)
                copy_out(n, 0)
                copy_gu(n + 1)
                if not last_of_pass:
                    copy_xg(m + 1)
                silu(n + 1)
                act.wait_ge(s_ST, m + 1)
                A(STb, ps[:, 0, 0:T], ACT.Copy).then_inc(s_STc, 1)
                copy_out(n + 1, 1)

            with act.Fori(0, npass) as q:
                base = q * NPAIR
                copy_xg(base)
                with act.Fori(0, NPAIR - 1) as i:
                    pair(base + i, False)
                pair(base + (NPAIR - 1), True)

            act.wait_ge(s_add, npass * (8 * NPAIR) + 1)
            for t in range(TT):
                A(h2[:, t, :], xs[:, t, :], ACT.Square, accum_out=ss2[:, t:t + 1]).then_inc(s_ssf, 1)
            act.wait_ge(s_msf, 1)
            A(r2[:, 0:TT], ss2[:, 2:4], ACT.Sqrt).then_inc(s_sqf, 1)

        @block.vector
        def _(dve):
            done = [0]
            v = nc.vector

            def link(ins):
                done[0] += 1
                ins.then_inc(s_dve, 1)
                dve.wait_ge(s_dve, done[0])

            def rms_scale(ss, r, width, s_in, s_out, s_root, n):
                dve.wait_ge(s_in, n)
                v.tensor_scalar(ss[:, n:2 * n], ss[:, 0:n], 1.0 / width, EPS, ALU.mult, ALU.add).then_inc(s_out, 1)
                dve.wait_ge(s_root, 1)
                link(v.reciprocal(r[:, n:2 * n], r[:, 0:n]))

            rms_scale(ssx, rx, D, s_ssx, s_ms, s_sq, TT)
            for t in range(TT):
                v.tensor_scalar(xn[:, t, :], xs[:, t, :], rx[:, 2 + t:3 + t], None, ALU.mult).then_inc(s_xn, 1)
            dve.wait_ge(s_rowC, 1)
            for i in range(0, KT // 2, 2):
                dve.wait_ge(s_xT, i + 1)
                for k in (2 * i, 2 * i + 1):
                    ins = v.tensor_scalar(hT[:, k, :], ps[:, 4 + i % 4, (k % 2) * T:(k % 2) * T + T],
                                          g1T[:, k:k + 1], None, ALU.mult)
                ins.then_inc(s_hD, 1)
            dve.wait_ge(s_z, 1)
            for h in range(GH):
                ins = v.tensor_scalar(gd[:, h * T:h * T + T], ps[:, 6 + h // 2, (h % 2) * T:(h % 2) * T + T],
                                      baT[:, h:h + 1], None, ALU.add)
            link(ins)
            v.scalar_tensor_tensor(out=gG[0], in0=gd, scalar=-1.0, in1=gd, op0=ALU.mult, op1=ALU.max).then_inc(s_y, 1)
            link(v.tensor_scalar(gG[1], gd, 0.0, None, ALU.min))
            dve.wait_ge(s_ln, 1)
            for h in range(GH):
                q = slice(h * T, h * T + T)
                ins = v.tensor_tensor_scan(gb[:, q], gG[1][:, q], gG[0][:, q], 0.0, ALU.add, ALU.subtract)
            link(ins)

            def halves(ap, H):
                w4 = ap.rearrange("p (n two r) -> p n two r", two=2, r=H)
                return w4[:, :, 0, :], w4[:, :, 1, :]

            qflat, kflat = fm_flat[:, 0:1024], fm_flat[:, 1024:2048]

            def level_diffs(lv):
                H = 1 << lv
                b0, b1 = halves(gb, H)
                ref = b0[:, :, H - 1:H].to_broadcast([P, 1024 // (2 * H), H])
                d0, d1 = halves(gd, H)
                v.tensor_tensor(d0, ref, b0, ALU.subtract)
                v.tensor_tensor(d1, b1, ref, ALU.subtract).then_inc(s_gD, 1)

            def level_product(lv):
                H = 1 << lv
                dve.wait_ge(s_gE, lv + 1)
                d0, d1 = halves(gd, H)
                o0, o1 = halves(gG[lv % 2], H)
                if lv >= 2:
                    dve.wait_ge(s_lv, lv)
                v.tensor_tensor(o0, d0, halves(kflat, H)[0], ALU.mult)
                v.scalar_tensor_tensor(out=o1, in0=d1, scalar=SCALE, in1=halves(qflat, H)[1],
                                       op0=ALU.mult, op1=ALU.mult).then_inc(s_gG, 1)

            level_diffs(0)
            dve.wait_ge(s_ev, 2)
            level_product(0)
            dve.wait_ge(s_lv, 1)
            for t in range(TT):
                ins = v.scalar_tensor_tensor(out=gA[:, t], in0=ps[:, 4 + t, :].rearrange("p (h t) -> p h t", h=GH),
                                             scalar=SCALE, in1=ident[:, :].unsqueeze(1).to_broadcast([P, GH, P]),
                                             op0=ALU.mult, op1=ALU.mult)
            ins.then_inc(s_gA, 1)
            dve.wait_ge(s_gA, 1)
            dve.wait_ge(s_masks, N_MASKS)
            for lv in range(LEVELS):
                if lv + 1 < LEVELS:
                    dve.wait_ge(s_gG, lv + 1)
                    level_diffs(lv + 1)
                    level_product(lv + 1)
                dve.wait_ge(s_lv, lv + 2)
                if lv < LEVELS - 1:
                    dve.wait_ge(s_gA, lv + 1)
                    for t in range(TT):
                        ins = v.copy_predicated(gA[:, t], lmask[:, lv].bitcast(I32).unsqueeze(1).to_broadcast([P, GH, P]),
                                                ps[:, 4 + t, :].rearrange("p (h t) -> p h t", h=GH))
                else:
                    ins = v.tensor_copy(gAoff, ps[:, 4, :].rearrange("p (h t) -> p h t", h=GH))
                ins.then_inc(s_gA, 1)
            dve.wait_ge(s_ev, 9)
            for c in range(2):
                for g in range(KVH):
                    for a in range(2):
                        src = fm[:, B_KCMP + 2 * c + g, 16 * a:16 * a + 240].rearrange("p (n b) -> p b n", b=16)
                        pe_ = peT[:, 32 * c + 16 * a:32 * c + 16 * a + 16].unsqueeze(2).to_broadcast([P, 16, NCMP])
                        ins = v.tensor_tensor(flat[:, c, 16 * a:16 * a + 16, g * NCMP:(g + 1) * NCMP], src, pe_, ALU.add)
            ins.then_inc(s_flat, 1)

            for step in SCHED:
                if step[0] == "S":
                    u = step[1]
                    kind, h = unit_of(u)
                    n = 4 if kind == "slc" else 2
                    m_, b_, s_, r_ = mx[u % 2], nb[u % 2], su[u % 2], rr[u % 2]
                    dve.wait_ge(s_S, u + 1)
                    v.tensor_reduce(m_[:, 0:1], ps[:, 6, 0:P], AX_X, ALU.max)
                    ins = v.tensor_reduce(m_[:, 1:2], ps[:, 6, P:3 * P], AX_X, ALU.max)
                    if kind == "slc":
                        ins = v.tensor_reduce(m_[:, 2:4], ps[:, 6, 384:416].rearrange("p (a n) -> p a n", a=2)[:, :, 0:NCMP],
                                              AX_X, ALU.max)
                    link(ins)
                    v.tensor_scalar(b_[:, 0:n], m_[:, 0:n], -SCALE, 1e28, ALU.mult, ALU.min).then_inc(s_nb, 1)
                    dve.wait_ge(s_exp, u + 1)
                    if kind == "slc":
                        link(v.tensor_scalar(s_[:, 2:4], s_[:, 2:4], 1e-30, None, ALU.max))
                    link(v.reciprocal(r_[:, 0:n], s_[:, 0:n]))
                    if kind != "moba":
                        br = {"slc": 1, "win": 2}[kind]
                        ins = v.tensor_tensor(r_[:, 0:2], r_[:, 0:2], ng[:, :, 3 * h + br], ALU.mult)
                        if kind == "slc":
                            ins = v.tensor_tensor(r_[:, 2:4], r_[:, 2:4], ng[:, :, 3 * h], ALU.mult)
                        link(ins)
                    p_ = aP[u % 2]
                    v.tensor_scalar(p_[:, 0:P], p_[:, 0:P], r_[:, 0:1], None, ALU.mult)
                    ins = v.tensor_scalar(p_[:, P:3 * P], p_[:, P:3 * P], r_[:, 1:2], None, ALU.mult)
                    if kind == "slc":
                        for t in range(TT):
                            ins = v.scalar_tensor_tensor(out=cP[h % 2][:, t], in0=cP[h % 2][:, t],
                                                         scalar=r_[:, 2 + t:3 + t], in1=cmul[:, t],
                                                         op0=ALU.mult, op1=ALU.mult)
                    ins.then_inc(s_P, 1)
                elif step[0] == "V":
                    u = step[1]
                    kind, h = unit_of(u)
                    if kind != "slc":
                        dve.wait_ge(s_V, u + 1)
                        b = (B_MQ if kind == "moba" else B_NQ) + h
                        v.tensor_copy(fm[:, b], ps[:, 4, (h % 2) * T:(h % 2) * T + T]).then_inc(s_O, 1)
                elif step[0] == "gpv":
                    h = step[1]
                    dve.wait_ge(s_gpv, h + 1)
                    v.tensor_copy(oraw[:, 2 * h:2 * h + 2].rearrange("p i n -> p (i n)"), ps[:, 5, :]).then_inc(s_gcp, 1)
                elif step[0] == "gnorm":
                    dve.wait_ge(s_gsq, GH)
                    v.tensor_scalar(ssg, ssg, 1.0 / GDV, EPS, ALU.mult, ALU.add).then_inc(s_gms, 1)
                    dve.wait_ge(s_grt, 1)
                    link(v.reciprocal(rg, rg))
                    for i in range(2 * GH):
                        ins = v.scalar_tensor_tensor(out=oraw[:, i], in0=oraw[:, i], scalar=rg[:, i:i + 1], in1=gng,
                                                     op0=ALU.mult, op1=ALU.mult)
                    link(ins)
                    dve.wait_ge(s_ev, N_GROUP)
                    for i in range(2 * GH):
                        h, t = i // 2, i % 2
                        v.tensor_tensor(oraw[:, i], oraw[:, i], gg[:, t, h * GDV:(h + 1) * GDV],
                                        ALU.mult).then_inc(s_on, 1)
                elif step[0] == "mg" and step[2] == 3:
                    m = step[1]
                    dve.wait_ge(s_sig, m + 1)
                    v.tensor_tensor(merged[:, 2 * m:2 * m + 2].rearrange("p k t -> p (k t)"), sg[m % 2],
                                    ps[:, 2 * (m % 2) + 1, :], ALU.mult).then_inc(s_mrg, 1)
            for bi in (1, 2):
                with dve.Fori(0, N_CG // 2) as j:
                    for s in range(2):
                        dve.wait_ge(s_sig, j * 2 + (N_CG * bi + s + 1))
                        dst = ar(TM0, KT * T)[:, bass.ds(j * (4 * T) + 2 * s * T, 2 * T)]
                        v.tensor_tensor(sg[s], sg[s], ps[:, 2 * s + 1, :], ALU.mult).then_inc(s_dve, 1)
                        dve.wait_ge(s_dve, j * 2 + (done[0] + s + 1))
                        v.tensor_tensor(dst, dst, sg[s], ALU.add).then_inc(s_mrg, 1)
                done[0] += N_CG

            dve.wait_ge(s_mrg, 3 * N_CG)
            v.memset(npass_f[:, 1:2], 0.0).then_inc(s_x2, 1)
            with dve.Fori(0, 2) as j:
                for s in range(2):
                    dve.wait_ge(s_wo, j * 2 + s + 1)
                    dst = xs[:, :, bass.ds(j * (2 * W) + s * W, W)]
                    v.tensor_tensor(dst, dst, ps[:, 2 * s:2 * s + 2, :], ALU.add).then_inc(s_x2, 1)

            rms_scale(ss2, r2, D, s_ss2, s_ms2, s_sq2, TT)
            dve.wait_ge(s_g2, 16)
            for t in range(TT):
                v.scalar_tensor_tensor(out=h2[:, t, :], in0=xs[:, t, :], scalar=r2[:, 2 + t:3 + t], in1=g2b,
                                       op0=ALU.mult, op1=ALU.mult).then_inc(s_h2, 1)
            for i in range(0, KT // 2, 2):
                dve.wait_ge(s_h2t, i + 1)
                v.tensor_copy(h2T[:, 2 * i:2 * i + 2, :].rearrange("p k t -> p (k t)"), ps[:, 4 + i % 4, :]).then_inc(s_h2D, 1)

            def bc(ap, n):
                return ap.unsqueeze(2).to_broadcast([P, TT, n])

            def first_max(vals, mxv, mnv, tmp, oh, n):
                link(v.tensor_reduce(mxv, vals, AX_X, ALU.max))
                link(v.tensor_tensor(oh, vals, bc(mxv, n), ALU.is_equal))
                link(v.tensor_tensor(tmp, oh, jm[:, 0:n].unsqueeze(1).to_broadcast([P, TT, n]), ALU.mult))
                link(v.tensor_reduce(mnv, tmp, AX_X, ALU.min))
                link(v.tensor_tensor(oh, tmp, bc(mnv, n), ALU.is_equal))

            dve.wait_ge(s_lgt, 1)
            dve.wait_ge(s_rc, 4)
            lgp = ps[:, 0, 0:128].rearrange("p (a n) -> p a n", a=TT)[:, :, 0:36]
            link(v.tensor_tensor(lg, lgp, rbb.unsqueeze(1).to_broadcast([P, TT, 36]), ALU.add))
            gl, el = lg[:, :, 0:GROUPS], lg[:, :, GROUPS:36]
            first_max(gl, rs[:, 0], rs[:, 1], t8, goh, GROUPS)
            link(v.tensor_tensor(t8, gl, bc(rs[:, 0], GROUPS), ALU.subtract))
            gx = [goh[:, t].unsqueeze(2).to_broadcast([P, GROUPS, EPG]) for t in range(TT)]
            for t in range(TT):
                ins = v.tensor_tensor(em[:, t].rearrange("p (g e) -> p g e", g=GROUPS),
                                      el[:, t].rearrange("p (g e) -> p g e", g=GROUPS), gx[t], ALU.mult)
            link(ins)
            link(v.tensor_scalar(oh1[:, :, 0:GROUPS], goh, -1.0, -NEG, ALU.add, ALU.mult))
            for t in range(TT):
                ins = v.tensor_tensor(em[:, t].rearrange("p (g e) -> p g e", g=GROUPS),
                                      em[:, t].rearrange("p (g e) -> p g e", g=GROUPS),
                                      oh1[:, t, 0:GROUPS].unsqueeze(2).to_broadcast([P, GROUPS, EPG]), ALU.add)
            link(ins)
            first_max(em, rs[:, 2], rs[:, 3], t64, oh1, NE)
            link(v.scalar_tensor_tensor(out=em, in0=oh1, scalar=10 * NEG, in1=em, op0=ALU.mult, op1=ALU.add))
            first_max(em, rs[:, 4], rs[:, 3], t64, oh2, NE)
            link(v.tensor_tensor(M, oh1, oh2, ALU.add))
            v.tensor_copy(M, M).then_inc(s_M, 1)
            v.tensor_tensor(rs[:, 5], rs[:, 4], rs[:, 2], ALU.subtract).then_inc(s_re, 1)
            dve.wait_ge(s_rex, 1)
            link(v.tensor_reduce(rs[:, 6], t8, AX_X, ALU.add))
            link(v.tensor_scalar(rs[:, 7], rs[:, 5], 1.0, None, ALU.add))
            link(v.tensor_tensor(rs[:, 6], rs[:, 6], rs[:, 7], ALU.mult))
            link(v.reciprocal(rs[:, 8], rs[:, 6]))
            link(v.tensor_tensor(rs[:, 9], rs[:, 8], rs[:, 5], ALU.mult))
            link(v.tensor_tensor(oh1, oh1, bc(rs[:, 8], NE), ALU.mult))
            link(v.tensor_tensor(oh2, oh2, bc(rs[:, 9], NE), ALU.mult))
            link(v.tensor_tensor(wgt, oh1, oh2, ALU.add))
            dve.wait_ge(s_pos, 1)
            link(v.tensor_scalar(t64, M, -1.0, 1e6, ALU.add, ALU.mult))
            link(v.tensor_tensor(posm, ps[:, 1, 0:2 * NE].rearrange("p (a e) -> p a e", a=TT), t64, ALU.add))
            link(v.tensor_reduce(rs[:, 10, 0:1], ps[:, 1, 2 * NE:3 * NE], AX_X, ALU.max))
            link(v.tensor_scalar(rs[:, 11, 0:1], rs[:, 10, 0:1], float(SLOTS), 1.0, ALU.is_gt, ALU.add))
            for k in range(2, T // SLOTS):
                link(v.tensor_scalar(rs[:, 12, 0:1], rs[:, 10, 0:1], float(SLOTS * k), None, ALU.is_gt))
                link(v.tensor_tensor(rs[:, 11, 0:1], rs[:, 11, 0:1], rs[:, 12, 0:1], ALU.add))
            v.tensor_copy(npass_i, rs[:, 11, 0:1]).then_inc(s_route, 1)
            v.memset(npass_f[:, 1:2], 0.0).then_inc(s_add, 1)
            v.memset(npass_f[:, 2:3], 0.0).then_inc(s_STc, 1)
            dve.wait_ge(s_route, 1)
            npass = dve.value_load(npass_i[0:1, 0:1], min_val=1, max_val=T // SLOTS)

            def make_g(e):
                for par in range(2):
                    for t in range(TT):
                        ins = v.tensor_scalar(Gb[:, t, par * SLOTS:par * SLOTS + SLOTS], iota,
                                              posm[:, t, bass.ds(e + par, 1)], None, ALU.is_equal)
                ins.then_inc(s_G, 1)

            def make_s(e):
                for par in range(2):
                    for t in range(TT):
                        ins = v.tensor_scalar(Sb[:, t, par * SLOTS:par * SLOTS + SLOTS], iota,
                                              posm[:, t, bass.ds(e + par, 1)], wgt[:, t, bass.ds(e + par, 1)],
                                              ALU.is_equal, ALU.mult)
                ins.then_inc(s_Sm, 1)

            def copy_xg(m):
                dve.wait_ge(s_xg, m * 2 + 2)
                v.tensor_copy(xgT[:, 8:16].rearrange("p k s -> p (k s)"),
                              ps[:, 4:6, :].rearrange("p a n -> p (a n)")).then_inc(s_xgD, 1)

            def middle(n):
                dve.wait_ge(s_silu, n + 1)
                tr = ps[:, 1, :].rearrange("p (j two s) -> p j two s", two=2, s=SLOTS)
                v.tensor_tensor(hmid, hmid, tr[:, :, 1], ALU.mult).then_inc(s_mid, 1)

            def adds(m, t):
                for c in range(4):
                    dve.wait_ge(s_sc, m * 8 + (4 * t + c + 1))
                    xc = xs[:, t, c * W:c * W + W]
                    v.tensor_tensor(xc, xc, ps[:, 2 + c, :], ALU.add).then_inc(s_add, 1)

            def pair(m, e, first, last_of_pass):
                n = m * 2
                if not last_of_pass:
                    make_g(e + 2)
                if not first:
                    adds(m - 1, 0)
                middle(n)
                if not first:
                    adds(m - 1, 1)
                middle(n + 1)
                if not last_of_pass:
                    copy_xg(m + 1)
                    dve.wait_ge(s_ST, m + 1)
                    make_s(e + 2)

            with dve.Fori(0, npass) as q:
                base = q * NPAIR
                make_g(0)
                make_s(0)
                copy_xg(base)
                pair(base, 0, True, False)
                with dve.Fori(1, NPAIR - 1) as i:
                    pair(base + i, i * 2, False, False)
                pair(base + (NPAIR - 1), NE - 2, False, True)
                for t in range(TT):
                    adds(base + (NPAIR - 1), t)
                v.tensor_scalar(posm, posm, -float(SLOTS), None, ALU.add).then_inc(s_M, 1)
                dve.wait_ge(s_M, q + 2)

            rms_scale(ss2, r2, D, s_ssf, s_msf, s_sqf, TT)
            dve.wait_ge(s_gf, 16)
            for t in range(TT):
                v.scalar_tensor_tensor(out=h2[:, t, :], in0=xs[:, t, :], scalar=r2[:, 2 + t:3 + t], in1=gfb,
                                       op0=ALU.mult, op1=ALU.mult).then_inc(s_y1, 1)


_INS = ['x', 'norm1_g', 'w_in', 'nsa_cmp_pe', 'nsa_cmp_w1', 'nsa_cmp_w2', 'gla_wa', 'gla_ba', 'gla_norm_g',
        'w_br_moba', 'w_br_nsa', 'w_br_gla', 'w_out', 'norm2_g', 'router_group_w', 'router_group_b',
        'router_expert_w', 'router_expert_b', 'expert_w_gate', 'expert_w_up', 'expert_w_down', 'final_norm_g']
_OUTS = [((1, 256, 2048), 'float32')]


def kernel(**inputs):
    import numpy as _np
    import concourse.bacc as _bacc
    from concourse import mybir as _mybir
    from concourse.bass_utils import run_bass_kernel_spmd as _run

    nc = _bacc.Bacc("TRN2", target_bir_lowering=False, num_devices=1, dynamic_dma_scratch_size=1024)
    arrays, args = {}, []
    for name in _INS:
        a = _np.ascontiguousarray(inputs[name])
        arrays[f"in_{name}_dram"] = a
        args.append(nc.dram_tensor(f"in_{name}_dram", a.shape, _mybir.dt.from_np(a.dtype), kind="ExternalInput").ap())
    for i, (shape, dtype) in enumerate(_OUTS):
        dt = _mybir.dt.from_np(_np.dtype(dtype))
        args.append(nc.dram_tensor(f"out_{i}_dram", shape, dt, kind="ExternalOutput").ap())
    build(nc, *args)
    r = _run(nc, [arrays], core_ids=[0])
    return r.results[0]["out_0_dram"]
```

```python
from contextlib import ExitStack

import concourse.bass as bass
from concourse import mybir
from concourse.alu_op_type import AluOpType as ALU

F32 = mybir.dt.float32
F32R = mybir.dt.float32r
I32 = mybir.dt.int32
ACT = mybir.ActivationFunctionType
AX_X = mybir.AxisListType.X

P = 128
T = 256
TT = T // P
D = 2048
KT = D // P
HD = 128
SCALE = HD ** -0.5
NEG = -1e30
EPS = 1e-6
TAU = 16.0
CMP_LEN, CMP_STRIDE = 32, 16
NCMP = (T - CMP_LEN) // CMP_STRIDE + 1
MH = NH = 8
KVH = 2
GH, GDV = 4, 256
LEVELS = 8
NE, GROUPS = 32, 4
EPG = NE // GROUPS
FF = 512
FT = FF // P
SLOTS = 64
NPAIR = NE // 2
W = 512

C_MQ, C_MK, C_MV, C_NQ, C_NKV = 0, 1024, 2048, 3072, 4096
C_NG = C_NKV + 1536
C_GQ = C_NG + 24
C_GK = C_GQ + 512
C_GV = C_GK + 512
C_GA = C_GV + 1024
C_GG = C_GA + 16
C_MG = C_GG + 1024

UK, CW = 8, 256
USIZE = UK * CW
N_CG = D // CW
FM_COLS = ([C_GQ, C_GQ + CW, C_GK, C_GK + CW] + [C_MQ + CW * i for i in range(8)]
           + [C_NQ + CW * i for i in range(4)]
           + [C_NKV, C_NKV + CW, C_NKV + 2 * CW, C_NKV + 4 * CW])
TM_COLS = ([C_MV + CW * i for i in range(4)] + [C_GV + CW * i for i in range(4)]
           + [C_NKV + 3 * CW, C_NKV + 5 * CW] + [C_GG + CW * i for i in range(4)])
N_FM, N_TM = len(FM_COLS), len(TM_COLS)
N_GROUP = N_FM + N_TM
G_LOOP = 15
TM_KS, TM_VW, TM_GG = 8, 9, 10
CMP_AFTER = 10
N_CMPU = 4
U_TM = 2 * N_FM
U_MG = U_TM + 2 * N_TM
U_WO = U_MG + 9 * N_CG
U_END = U_WO + 2 * N_CG
U_CMP = U_TM + 2 * CMP_AFTER
B_GQ, B_GK, B_MQ, B_MK, B_NQ, B_KCMP, B_VCMP, B_KSLC, B_KWIN = 0, 4, 8, 16, 24, 32, 34, 36, 38
BRANCH_ORDER = (0, 2, 1)
UNITS = MH + 2 * NH


def unit_of(u):
    return ("moba", u) if u < MH else (("slc", "win")[(u - MH) % 2], (u - MH) // 2)


def schedule():
    steps = []
    count = [0]

    def attention(first, end):
        i = count[0]
        if i >= end + 2:
            return
        if i - 2 >= first:
            steps.append(("V", i - 2))
        if first <= i - 1 < end:
            steps.append(("T", i - 1))
        if i < end:
            steps.append(("S", i))
        count[0] += 1

    for g in range(G_LOOP, N_FM):
        steps += [("fm", g, 0), ("fm", g, 1)]
        if g == G_LOOP:
            steps.append(("gat",))
        if g == G_LOOP + 1:
            steps.append(("z",))
    steps.append(("diag",))
    for g in range(N_TM):
        if g == CMP_AFTER:
            steps.append(("cmp1",))
        for half in range(2):
            steps.append(("tm", g, half))
            if g >= 8:
                attention(0, MH)
            if g == CMP_AFTER and half == 0:
                steps.append(("cmp2",))
        if g < LEVELS:
            steps.append(("level", g))
        if g == LEVELS - 1:
            steps.append(("flat",))
        if g >= TM_GG:
            steps.append(("gpv", g - TM_GG))
    while count[0] < MH + 2:
        attention(0, MH)
    steps.append(("osplit", 0))
    count[0] = MH
    for m in range(N_CG):
        for part in range(3):
            steps.append(("mg", m, part))
            attention(MH, UNITS)
            if m == N_CG - 2 and part == 0:
                steps.append(("gms",))
            if m == N_CG - 2 and part > 0:
                steps.append(("gnorm", part - 1))
            if m == N_CG - 1 and part < 2:
                steps.append(("gnorm", part + 2))
            if m == N_CG - 1 and part > 0:
                steps.append(("gtr", 2 * part - 2))
                steps.append(("gtr", 2 * part - 1))
    assert count[0] >= UNITS + 2
    steps.append(("osplit", 1))
    steps.append(("osplit", 2))
    return steps


def build(nc, x, norm1_g, w_in, cmp_pe, cmp_w1, cmp_w2, gla_wa, gla_ba, gla_norm_g, w_br_moba, w_br_nsa,
          w_br_gla, w_out, norm2_g, rg_w, rg_b, re_w, re_b, e_gate, e_up, e_down, final_g, out):
    SCHED = schedule()
    with ExitStack() as ctx:
        def sb(name, shape, dt=F32):
            return ctx.enter_context(nc.sbuf_tensor(name, shape, dt))

        def sem(name):
            return ctx.enter_context(nc.semaphore(name))

        XS0, HB0 = 0, TT * D
        ID0 = HB0 + KT * T
        SM0 = ID0 + P
        AR0 = SM0 + 5840
        SLAB = AR0 + 40960
        base_bytes = (nc.sbuf_base + 31) // 32 * 32
        sb("slab", [P, SLAB])

        def r32(name, a, n):
            return nc.alloc_sbuf_tensor_at(name, [P, n], F32R, offset=base_bytes + 4 * a)

        ps = ctx.enter_context(nc.psum_tensor("ps", [P, 8, 512], F32))

        buffers = {}

        def at(a, n, parts=P):
            skip = a % 8
            if (a, n) not in buffers:
                buffers[a, n] = nc.alloc_sbuf_tensor_at(f"at{a}_{n}", [P, skip + n], F32,
                                                        offset=base_bytes + 4 * (a - skip))
            return buffers[a, n][0:parts, skip:skip + n]

        def ar(a, n, parts=P):
            return at(AR0 + a, n, parts)

        def sm(a, n, parts=P):
            return at(SM0 + a, n, parts)

        ident = at(ID0, P)
        xs = at(XS0, TT * D).rearrange("p (a d) -> p a d", a=TT)
        h2 = at(HB0, TT * D).rearrange("p (a d) -> p a d", a=TT)
        hThi = r32("hThi", HB0, KT * T)[:, :].rearrange("p (k t) -> p k t", k=KT)
        hTlo = r32("hTlo", XS0, KT * T)[:, :].rearrange("p (k t) -> p k t", k=KT)
        RAW0 = 6 * USIZE
        FM0 = RAW0 + 3 * USIZE
        TM0 = FM0 + 40 * T
        TMP0 = TM0 + N_TM * TT * CW
        whi = r32("whi", AR0, 3 * USIZE)[:, :].rearrange("p (s k n) -> p s k n", s=3, k=UK)
        wlo = r32("wlo", AR0 + 3 * USIZE, 3 * USIZE)[:, :].rearrange("p (s k n) -> p s k n", s=3, k=UK)
        raw = ar(RAW0, 3 * USIZE).rearrange("p (s k n) -> p s k n", s=3, k=UK)
        raw_cmp = ar(RAW0, 3 * USIZE).rearrange("p (s l o) -> p s l o", s=3, l=USIZE // HD)
        fm_flat = ar(FM0, 40 * T)
        fm = fm_flat.rearrange("p (b t) -> p b t", t=T)
        mv = ar(TM0, 2048).rearrange("p (a n) -> p a n", a=TT)
        gv = ar(TM0 + 2048, 2048).rearrange("p (a n) -> p a n", a=TT)
        gg = ar(TM0 + 4096, 2048).rearrange("p (a n) -> p a n", a=TT)
        kv35 = ar(TM0 + 6144, 1024).rearrange("p (a n) -> p a n", a=TT)
        merged_flat = ar(TM0, KT * T)
        merged_lo = r32("merged_lo", AR0 + TM0, KT * T)
        merged_hi = r32("merged_hi", AR0 + FM0 + 24 * T, KT * T)
        ogT = ar(TM0 + 4096, 2048).rearrange("p (b t) -> p b t", t=T)
        xn = ar(FM0, 2 * D).rearrange("p (a d) -> p a d", a=TT)
        wsm_hi = r32("wsm_hi", AR0 + TMP0 + 2048, KT * 40)[:, :].rearrange("p (k n) -> p k n", k=KT)
        wsm_lo = r32("wsm_lo", AR0 + TMP0 + 2048 + KT * 40, KT * 40)[:, :].rearrange("p (k n) -> p k n", k=KT)
        osrc = [fm_flat[:, B_MQ * T:(B_MQ + 8) * T], ar(TM0 + 4096, 2048), fm_flat[:, B_NQ * T:(B_NQ + 8) * T]]
        ohi_a, olo_a = r32("ohi_a", AR0 + FM0, 2048), r32("olo_a", AR0 + FM0 + B_MK * T, 2048)
        ohi_b, olo_b = r32("ohi_b", AR0 + FM0 + B_KCMP * T, 2048), r32("olo_b", AR0 + TMP0, 2048)
        ohi, olo = [ohi_a, ohi_b, ohi_a], [olo_a, olo_b, olo_a]
        gb = ar(TMP0, 1024)
        gd = ar(TMP0 + 1024, 1024)
        gG = [ar(TMP0 + 2048 + 1024 * i, 1024) for i in range(2)]
        lmask = ar(TMP0 + 4224, 896).rearrange("p (l t) -> p l t", t=P)
        aP = [ar(TMP0 + 384 * i, 384) for i in range(2)]
        aPT = [ar(TMP0 + 768 + 384 * i, 384) for i in range(2)]
        cP = [ar(TMP0 + 1536 + 32 * i, 30).rearrange("p (a n) -> p a n", a=TT) for i in range(2)]
        cPT = [ar(TMP0 + 1600 + 256 * i, 256, NCMP) for i in range(2)]
        flat = ar(TMP0 + 2112, 1920).rearrange("p (c l n) -> p c l n", c=2, l=CMP_LEN)
        sg = [ar(TMP0 + 4096 + 512 * i, 512) for i in range(2)]
        wsm = sm(0, KT * 40).rearrange("p (k n) -> p k n", k=KT)
        g1row, perow, barow = sm(640, P, KT), sm(768, P, 64), sm(896, P, GH)
        gA = sm(0, TT * 512).rearrange("p (a h t) -> p a h t", a=TT, h=GH)
        gAoff = sm(1024, 512).rearrange("p (h t) -> p h t", h=GH)
        ng = sm(1536, 48).rearrange("p (a n) -> p a n", a=TT)
        ga = sm(1584, 32).rearrange("p (a n) -> p a n", a=TT)
        gaT = sm(1616, 256, 16)
        wa = sm(1872, 512, 16)
        junk256 = sm(1872, 256)
        causal = sm(2384, P)
        cadd = sm(2512, 30).rearrange("p (a n) -> p a n", a=TT)
        cmul = sm(2542, 30).rearrange("p (a n) -> p a n", a=TT)
        cols3 = sm(2572, 84)
        g1T, peT, baT = cols3[:, 0:KT], cols3[:, KT:KT + 64], cols3[:, KT + 64:KT + 64 + GH]
        w2 = sm(2656, 256).rearrange("p (c n) -> p c n", c=2)
        gng = sm(2912, 256)
        hidT = sm(3168, 60).rearrange("p (c n) -> p c n", c=2)
        kcT = sm(3228, 30)
        vc = sm(3258, 256, NCMP).rearrange("p (g n) -> p g n", g=KVH)
        ssx, rx = sm(3514, 4), sm(3518, 4)
        ssg, rg = sm(3522, 8), sm(3530, 8)
        mx = [sm(3540 + 4 * i, 4) for i in range(2)]
        nb = [sm(3548 + 4 * i, 4) for i in range(2)]
        su = [sm(3556 + 4 * i, 4) for i in range(2)]
        rr = [sm(3564 + 4 * i, 4) for i in range(2)]
        oraw = sm(3584, 2048).rearrange("p (i n) -> p i n", i=2 * GH)
        ss2, r2 = sm(5824, 4), sm(5828, 4)
        npass_f = sm(5832, 4)
        npass_i = npass_f[:, 0:1].bitcast(I32)
        xgT = sm(0, 2048).rearrange("p (k s) -> p k s", k=KT)
        osb = sm(2048, 2048)
        gusb = sm(4096, 512)
        hmid = sm(4608, 256).rearrange("p (j s) -> p j s", j=FT)
        Sb = sm(4864, 256).rearrange("p (a s) -> p a s", a=TT)
        Gb = sm(5120, 256).rearrange("p (a s) -> p a s", a=TT)
        STb = sm(5376, 256)
        iota = sm(5632, SLOTS)
        posm = sm(5696, 64).rearrange("p (a e) -> p a e", a=TT)
        wgt = sm(5760, 64).rearrange("p (a e) -> p a e", a=TT)
        g2b = sm(0, D)
        h2T = sm(0, KT * T).rearrange("p (k t) -> p k t", k=KT)
        rw = sm(4096, KT * 36).rearrange("p (k n) -> p k n", k=KT)
        tri, ones = sm(4672, P), sm(4800, P)
        rbb = sm(4928, 36)
        jm = sm(4964, NE)
        lg = sm(4996, 72).rearrange("p (a n) -> p a n", a=TT)
        em = sm(5068, 64).rearrange("p (a n) -> p a n", a=TT)
        oh1 = sm(5132, 64).rearrange("p (a n) -> p a n", a=TT)
        t64 = sm(5196, 64).rearrange("p (a n) -> p a n", a=TT)
        oh2 = sm(5260, 64).rearrange("p (a n) -> p a n", a=TT)
        goh = sm(5324, 8).rearrange("p (a n) -> p a n", a=TT)
        t8 = sm(5332, 8).rearrange("p (a n) -> p a n", a=TT)
        rs = sm(5340, 40).rearrange("p (i a) -> p i a", a=TT)
        M = sm(5380, 64).rearrange("p (a n) -> p a n", a=TT)
        UN = KT * W
        unit_g = [ar(u * UN, UN // 2).rearrange("p (j f) -> p j f", j=8) for u in range(4)]
        unit_u = [ar(u * UN + UN // 2, UN // 2).rearrange("p (j f) -> p j f", j=8) for u in range(4)]
        wd = ar(4 * UN, UN).rearrange("p (j n) -> p j n", j=FT)
        gfb = ar(0, D)

        s_x = [sem(f"s_x{t}") for t in range(TT)]
        s_rows, s_wsm, s_const = sem("s_rows"), sem("s_wsm"), sem("s_const")
        s_ident, s_masks = sem("s_ident"), sem("s_masks")
        s_ssx, s_ms, s_sq = sem("s_ssx"), sem("s_ms"), sem("s_sq")
        s_dve, s_act, s_pl, s_tmp = sem("s_dve"), sem("s_act"), sem("s_pl"), sem("s_tmp")
        s_xn, s_rowT, s_rowC = sem("s_xn"), sem("s_rowT"), sem("s_rowC")
        s_xT, s_hhi, s_hlo = sem("s_xT"), sem("s_hhi"), sem("s_hlo")
        s_wsh, s_wsl = sem("s_wsh"), sem("s_wsl")
        s_smp, s_sma, s_gaT, s_gaTc, s_z = sem("s_smp"), sem("s_sma"), sem("s_gaT"), sem("s_gaTc"), sem("s_z")
        s_y, s_e, s_ln = sem("s_y"), sem("s_e"), sem("s_ln")
        s_raw = [sem(f"s_raw{i}") for i in range(3)]
        s_hi, s_lo, s_use, s_cmpu = sem("s_hi"), sem("s_lo"), sem("s_use"), sem("s_cmpu")
        s_ev = sem("s_ev")
        s_gD, s_gE, s_gG, s_lv, s_gA = sem("s_gD"), sem("s_gE"), sem("s_gG"), sem("s_lv"), sem("s_gA")
        s_S, s_nb, s_exp, s_P, s_T, s_PT, s_V, s_O = (
            sem(n) for n in ("s_S", "s_nb", "s_exp", "s_P", "s_T", "s_PT", "s_V", "s_O"))
        s_flat, s_hid, s_cmp2, s_kvc = (sem(n) for n in ("s_flat", "s_hid", "s_cmp2", "s_kvc"))
        s_gpv, s_gsq, s_gcp, s_gms, s_grt, s_on, s_gtr, s_ogT = (
            sem(n) for n in ("s_gpv", "s_gsq", "s_gcp", "s_gms", "s_grt", "s_on", "s_gtr", "s_ogT"))
        s_ohi, s_olo = sem("s_ohi"), sem("s_olo")
        s_sig, s_mrg, s_mhi, s_mlo = sem("s_sig"), sem("s_mrg"), sem("s_mhi"), sem("s_mlo")
        s_xr, s_x2 = sem("s_xr"), sem("s_x2")
        s_g2, s_rw = sem("s_g2"), sem("s_rw")
        s_ss2, s_ms2, s_sq2, s_h2 = sem("s_ss2"), sem("s_ms2"), sem("s_sq2"), sem("s_h2")
        s_h2t, s_h2A, s_h2D, s_lgt, s_rc = sem("s_h2t"), sem("s_h2A"), sem("s_h2D"), sem("s_lgt"), sem("s_rc")
        s_re, s_rex, s_M, s_pos, s_route = sem("s_re"), sem("s_rex"), sem("s_M"), sem("s_pos"), sem("s_route")
        s_u = [sem(f"s_u{u}") for u in range(4)]
        s_wd = sem("s_wd")
        s_gu0, s_gu, s_gus, s_xg, s_xgA, s_xgD = (
            sem(n) for n in ("s_gu0", "s_gu", "s_gus", "s_xg", "s_xgA", "s_xgD"))
        s_G, s_Sm, s_tr, s_silu, s_mid, s_ST, s_STc = (
            sem(n) for n in ("s_G", "s_Sm", "s_tr", "s_silu", "s_mid", "s_ST", "s_STc"))
        s_dn, s_osb, s_sc, s_add = sem("s_dn"), sem("s_osb"), sem("s_sc"), sem("s_add")
        s_gf, s_ssf, s_msf, s_sqf, s_y1, s_out = (
            sem(n) for n in ("s_gf", "s_ssf", "s_msf", "s_sqf", "s_y1", "s_out"))

        x_v = x.rearrange("b (a p) d -> (b a) p d", p=P)
        out_v = out.rearrange("b (a p) d -> (b a) p d", p=P)
        win_v = w_in[0].rearrange("(k p) n -> p k n", p=P)
        wout_v = w_out[0].rearrange("(k p) n -> p k n", p=P)
        br_v = [w[0].rearrange("(k p) n -> p k n", p=P) for w in (w_br_moba, w_br_nsa, w_br_gla)]
        cmpw1_v = cmp_w1[0].rearrange("c (l d) o -> c d l o", d=HD)
        gate_v = e_gate.rearrange("a e (p j) f -> (a e) p j f", j=KT)
        up_v = e_up.rearrange("a e (p j) f -> (a e) p j f", j=KT)
        down_v = e_down.rearrange("a e (p j) n -> (a e) p j n", j=FT)

        def slot_of(u):
            return u % 3

        block = ctx.enter_context(nc.Block())

        @block.sync
        def _(sp):
            for t in range(TT):
                sp.dma_start(xs[:, t, :], x_v[t]).then_inc(s_x[t], 16)
            sp.dma_start(g1row, norm1_g[0].rearrange("(k p) -> k p", p=P)).then_inc(s_rows, 16)
            sp.dma_start(perow, cmp_pe[0].rearrange("c l d -> (c l) d")).then_inc(s_rows, 16)
            sp.dma_start(barow, gla_ba[0].rearrange("(h p) -> h p", p=P)).then_inc(s_rows, 16)
            sp.dma_start(wsm[:, :, 0:24], win_v[:, :, C_NG:C_NG + 24]).then_inc(s_wsm, 16)
            sp.dma_start(wsm[:, :, 24:40], win_v[:, :, C_GA:C_GA + 16]).then_inc(s_wsm, 16)

            def load_unit(slot, src):
                sp.dma_start(raw[:, slot], src).then_inc(s_raw[slot], 16)

            def win_unit(col, half):
                return win_v[:, UK * half:UK * half + UK, col]

            for u in range(U_TM + 2 * CMP_AFTER):
                g, half = u // 2, u % 2
                col = (FM_COLS + TM_COLS)[g]
                if u >= 3:
                    sp.wait_ge(s_lo, u - 2)
                load_unit(u % 3, win_unit(slice(col, col + CW), half))
                if u == 2:
                    sp.dma_start(wa, gla_wa[0]).then_inc(s_const, 16)
                    sp.dma_start(w2, cmp_w2[0].rearrange("c d o -> d c o")).then_inc(s_const, 16)
                    sp.dma_start(gng, gla_norm_g[0].partition_broadcast(P)).then_inc(s_const, 16)
            for i in range(N_CMPU):
                if i < 3:
                    sp.wait_ge(s_lo, U_CMP + i - 2)
                else:
                    sp.wait_ge(s_cmpu, i - 2)
                sp.dma_start(raw_cmp[:, (U_CMP + i) % 3], cmpw1_v[i // 2][:, 16 * (i % 2):16 * (i % 2) + 16]
                             ).then_inc(s_raw[(U_CMP + i) % 3], 16)
            for u in range(U_CMP, U_MG):
                g, half = u // 2, u % 2
                col = (FM_COLS + TM_COLS)[g]
                if u < U_CMP + 3:
                    sp.wait_ge(s_cmpu, u - U_CMP + N_CMPU - 2)
                else:
                    sp.wait_ge(s_lo, u - 2)
                load_unit((u + N_CMPU) % 3, win_unit(slice(col, col + CW), half))

            for bi, branch in enumerate(BRANCH_ORDER):
                with sp.Fori(1, N_CG + 1) as m1:
                    for i in range(3):
                        sp.wait_ge(s_lo, m1 * 3 + (U_MG + 3 * N_CG * bi + i - 5))
                        if i < 2:
                            load_unit((U_MG + N_CMPU + i) % 3,
                                      win_unit(bass.ds(m1 * CW + (C_MG + branch * D - CW), CW), i))
                        else:
                            load_unit((U_MG + N_CMPU + i) % 3, br_v[branch][:, :, bass.ds(m1 * CW - CW, CW)])

            def load_out(u, slot, col, half):
                sp.wait_ge(s_lo, u - 2)
                load_unit(slot, wout_v[:, UK * half:UK * half + UK, col])

            for i in range(6):
                load_out(U_WO + i, (U_WO + N_CMPU + i) % 3, slice(i // 2 * CW, i // 2 * CW + CW), i % 2)
                if i == 2:
                    sp.wait_ge(s_use, U_WO)
                    for t in range(TT):
                        sp.dma_start(xs[:, t, :], x_v[t]).then_inc(s_xr, 16)
            with sp.Fori(1, 2) as j:
                for i in range(6):
                    load_out(j * 6 + (U_WO + i), (U_WO + N_CMPU + i) % 3,
                             bass.ds(j * (3 * CW) + i // 2 * CW, CW), i % 2)
            for i in range(12, 16):
                load_out(U_WO + i, (U_WO + N_CMPU + i) % 3, slice(i // 2 * CW, i // 2 * CW + CW), i % 2)
            sp.dma_start(g2b, norm2_g[0].partition_broadcast(P)).then_inc(s_g2, 16)
            sp.dma_start(rw[:, :, 0:GROUPS], rg_w[0].rearrange("(k p) n -> p k n", p=P)).then_inc(s_rw, 16)
            sp.dma_start(rw[:, :, GROUPS:36], re_w[0].rearrange("(k p) n -> p k n", p=P)).then_inc(s_rw, 16)
            sp.dma_start(rbb[:, 0:GROUPS], rg_b[0].partition_broadcast(P)).then_inc(s_rw, 16)
            sp.dma_start(rbb[:, GROUPS:36], re_b[0].partition_broadcast(P)).then_inc(s_rw, 16)

            def load_gu(u, e, h):
                sp.dma_start(unit_g[u], gate_v[bass.ds(e, 1), :, 8 * h:8 * h + 8].rearrange(
                    "e p j f -> (e p) j f")).then_inc(s_u[u], 16)
                sp.dma_start(unit_u[u], up_v[bass.ds(e, 1), :, 8 * h:8 * h + 8].rearrange(
                    "e p j f -> (e p) j f")).then_inc(s_u[u], 16)

            def load_down(e):
                for h in range(2):
                    sp.dma_start(wd[:, 2 * h:2 * h + 2], down_v[bass.ds(e, 1), :, 2 * h:2 * h + 2].rearrange(
                        "e p j n -> (e p) j n")).then_inc(s_wd, 16)

            load_down(0)
            sp.wait_ge(s_use, U_END)
            for h in range(2):
                load_gu(2 + h, 0, h)
            for h in range(2):
                load_gu(h, 1, h)
            sp.wait_ge(s_route, 1)
            npass = sp.value_load(npass_i[0:1, 0:1], min_val=1, max_val=T // SLOTS)

            def rest_of(n, e0):
                for q in range(2):
                    for h in range(2):
                        sp.wait_ge(s_gu0 if h == 0 else s_gu, n + q + 1)
                        load_gu((2, 0)[q] + h, e0 + 2 + q, h)
                    sp.wait_ge(s_dn, n + q + 1)
                    load_down(e0 + 1 + q)

            with sp.Fori(0, NE // 2 - 1) as i:
                rest_of(2 * i, 2 * i)
            sp.wait_ge(s_dn, NE - 1)
            load_down(NE - 1)
            with sp.If(npass > 1):
                with sp.Fori(1, npass) as q:
                    base = q * NE
                    for h in range(2):
                        sp.wait_ge(s_gu0 if h == 0 else s_gu, base - 1)
                        load_gu(2 + h, 0, h)
                    sp.wait_ge(s_dn, base)
                    load_down(0)
                    for h in range(2):
                        sp.wait_ge(s_gu, base)
                        load_gu(h, 1, h)
                    with sp.Fori(0, NE // 2 - 1) as i:
                        rest_of(base + 2 * i, 2 * i)
                    sp.wait_ge(s_dn, base + NE - 1)
                    load_down(NE - 1)

            sp.wait_ge(s_gu, npass * NE)
            sp.dma_start(gfb, final_g.partition_broadcast(P)).then_inc(s_gf, 16)
            for t in range(TT):
                sp.wait_ge(s_y1, t + 1)
                sp.dma_start(out_v[t], h2[:, t, :]).then_inc(s_out, 16)
            sp.wait_ge(s_out, 16 * TT)

        @block.gpsimd
        def _(pool):
            done = [0]

            def link(ins):
                done[0] += 1
                ins.then_inc(s_pl, 1)
                pool.wait_ge(s_pl, done[0])

            link(nc.gpsimd.memset(ident, 0.0))
            nc.gpsimd.affine_select(out=ident, in_=ident, compare_op=ALU.not_equal, fill=1.0,
                                    base=0, pattern=[[-1, P]], channel_multiplier=1).then_inc(s_ident, 1)
            link(nc.gpsimd.memset(causal, 0.0))
            nc.gpsimd.affine_select(out=causal, in_=causal, compare_op=ALU.is_ge, fill=NEG, base=0,
                                    pattern=[[-1, P]], channel_multiplier=1).then_inc(s_masks, 1)
            link(nc.gpsimd.memset(cadd, 0.0))
            link(nc.gpsimd.memset(cmul, 1.0))
            for t in range(TT):
                for m, fill in ((cadd, NEG), (cmul, 0.0)):
                    nc.gpsimd.affine_select(out=m[:, t], in_=m[:, t], compare_op=ALU.is_ge, fill=fill,
                                            base=t * P - CMP_LEN + 1, pattern=[[-CMP_STRIDE, NCMP]],
                                            channel_multiplier=1).then_inc(s_masks, 1)
            link(nc.gpsimd.memset(lmask, 0.0))
            for lv in range(LEVELS - 1):
                H = 1 << lv
                v = lmask[:, lv].rearrange("p (n two r) -> p n two r", two=2, r=H)[:, :, 1, :]
                link(nc.gpsimd.memset(v, 1.0))
                link(nc.gpsimd.affine_select(out=v, in_=v, compare_op=ALU.is_ge, fill=0.0, base=0,
                                             pattern=[[-2 * H, P // (2 * H)], [0, H]], channel_multiplier=1))
                nc.gpsimd.affine_select(out=v, in_=v, compare_op=ALU.is_ge, fill=0.0, base=H - 1,
                                        pattern=[[2 * H, P // (2 * H)], [0, H]],
                                        channel_multiplier=-1).then_inc(s_masks, 1)
            pool.wait_ge(s_use, U_WO)
            nc.gpsimd.iota(jm, pattern=[[1, NE]], base=-64, channel_multiplier=0,
                           allow_small_or_imprecise_dtypes=True).then_inc(s_rc, 1)
            nc.gpsimd.iota(iota, pattern=[[1, SLOTS]], base=0,
                           channel_multiplier=0, allow_small_or_imprecise_dtypes=True).then_inc(s_rc, 1)
            nc.gpsimd.memset(ones, 1.0).then_inc(s_rc, 1)
            link(nc.gpsimd.memset(tri, 1.0))
            nc.gpsimd.affine_select(out=tri, in_=tri, compare_op=ALU.is_gt, fill=0.0, base=0,
                                    pattern=[[1, P]], channel_multiplier=-1).then_inc(s_rc, 1)

        N_MASKS = 1 + 2 * TT + LEVELS - 1

        @block.tensor
        def _(pe):
            mm = nc.tensor.matmul

            pe.wait_ge(s_ident, 1)
            pe.wait_ge(s_rows, 48)
            nc.tensor.transpose(ps[:, 3, 0:KT], g1row, ident[0:KT, 0:KT])
            nc.tensor.transpose(ps[:, 3, 16:80], perow, ident[0:64, 0:64])
            nc.tensor.transpose(ps[:, 3, 80:84], barow, ident[0:GH, 0:GH]).then_inc(s_rowT, 1)
            pe.wait_ge(s_xn, TT)
            for i in range(KT // 2):
                if i >= 4:
                    pe.wait_ge(s_hlo, i - 3)
                for k in (2 * i, 2 * i + 1):
                    for t in range(TT):
                        last = nc.tensor.transpose(ps[:, 4 + i % 4, (k % 2) * T + t * P:(k % 2) * T + t * P + P],
                                                   xn[:, t, k * P:k * P + P], ident)
                last.then_inc(s_xT, 1)
            pe.wait_ge(s_hlo, KT // 2)

            def mm3(o, ah, al, bh, bl, start, stop):
                mm(o, ah, bh, start=start, stop=False)
                mm(o, ah, bl, start=False, stop=False)
                return mm(o, al, bh, start=False, stop=stop)

            pe.wait_ge(s_wsl, 1)
            for t in range(TT):
                q = slice(t * P, t * P + P)
                for k in range(KT):
                    last = mm3(ps[:, 3, 64 * t:64 * t + 40], hThi[:, k, q], hTlo[:, k, q], wsm_hi[:, k], wsm_lo[:, k],
                               k == 0, k == KT - 1)
            last.then_inc(s_smp, 1)

            def fm_unit(slot, bank, half, ah=None, al=None, whole=False):
                ah = hThi if ah is None else ah
                al = hTlo if al is None else al
                for b in range(2):
                    for k in range(UK):
                        kk = UK * half + k
                        o = ps[:, bank, b * T:b * T + T]
                        q = slice(b * P, b * P + P)
                        last = mm3(o, whi[:, slot, k, q], wlo[:, slot, k, q], ah[:, kk], al[:, kk],
                                   b == 0 and k == 0 and half == 0,
                                   b == 1 and k == UK - 1 and (half == 1 or whole))
                return last.then_inc(s_use, 1)

            def tm_unit(slot, bank, half, ah, al):
                for t in range(TT):
                    for k in range(UK):
                        kk = UK * half + k
                        q = slice(t * P, t * P + P)
                        last = mm3(ps[:, bank, t * CW:t * CW + CW], ah[:, kk, q], al[:, kk, q],
                                   whi[:, slot, k], wlo[:, slot, k],
                                   t == 0 and k == 0 and half == 0, t == 1 and k == UK - 1 and half == 1)
                return last.then_inc(s_use, 1)

            def fm_group_half(g, gi, half):
                pe.wait_ge(s_lo, g * 2 + (half + 1))
                if half == 0 and not (isinstance(g, int) and g < 3):
                    pe.wait_ge(s_ev, g - 2)
                fm_unit((2 * gi + half) % 3, gi % 3, half)

            for g in range(3):
                for half in range(2):
                    fm_group_half(g, g, half)
            with pe.Fori(1, G_LOOP // 3) as j:
                for gi in range(3):
                    for half in range(2):
                        fm_group_half(j * 3 + gi, gi, half)

            def scores(u):
                kind, h = unit_of(u)
                g = h // (NH // KVH)
                q = fm[:, (B_MQ if kind == "moba" else B_NQ) + h]
                k = fm[:, {"moba": B_MK + h, "slc": B_KSLC + g, "win": B_KWIN + g}[kind]]
                if u >= 1:
                    pe.wait_ge(s_exp, u)
                if u == 0:
                    pe.wait_ge(s_ev, N_FM)
                mm(ps[:, 6, 0:P], q[:, 0:P], k[:, 0:P], start=True, stop=False)
                mm(ps[:, 6, 0:P], ident, causal, start=False, stop=True)
                mm(ps[:, 6, P:3 * P], q[:, P:T], k, start=True, stop=False)
                last = mm(ps[:, 6, 2 * P:3 * P], ident, causal, start=False, stop=True)
                if kind == "slc":
                    pe.wait_ge(s_kvc, 1)
                    for t in range(TT):
                        o = ps[:, 6, 384 + 16 * t:384 + 16 * t + NCMP]
                        mm(o, q[:, t * P:t * P + P], kcT[:, g * NCMP:(g + 1) * NCMP], start=True, stop=False)
                        last = mm(o, ident, cadd[:, t], start=False, stop=True)
                last.then_inc(s_S, 1)

            def turn(u):
                kind, h = unit_of(u)
                pe.wait_ge(s_P, u + 1)
                for b in range(3):
                    last = nc.tensor.transpose(ps[:, 7, b * P:b * P + P], aP[u % 2][:, b * P:b * P + P], ident)
                if kind == "slc":
                    for t in range(TT):
                        last = nc.tensor.transpose(ps[0:NCMP, 5, t * P:t * P + P], cP[h % 2][:, t], ident)
                last.then_inc(s_T, 1)

            def values(u):
                kind, h = unit_of(u)
                g = h // (NH // KVH)
                o = ps[:, 4, (h % 2) * T:(h % 2) * T + T]
                pe.wait_ge(s_PT, u + 1)
                if kind != "win":
                    hh = h if kind == "moba" else MH + h
                    if hh >= 1:
                        pe.wait_ge(s_O, hh)
                    if hh == 0:
                        pe.wait_ge(s_gA, 9)
                if kind == "moba":
                    v = mv[:, :, h * HD:h * HD + HD]
                    if h == 0:
                        pe.wait_ge(s_ev, N_FM + 4)
                elif kind == "slc":
                    v = kv35[:, :, g * HD:g * HD + HD]
                    mm(o, vc[:, g], cPT[h % 2], start=True, stop=False)
                    if h == 0:
                        pe.wait_ge(s_ev, N_FM + TM_VW + 1)
                else:
                    v = kv35[:, :, CW + g * HD:CW + g * HD + HD]
                pt = aPT[u % 2]
                mm(o, v[:, 0], pt[:, 0:T], start=kind == "moba", stop=False)
                last = mm(o[:, P:T], v[:, 1], pt[:, T:T + P], start=False, stop=kind != "slc")
                last.then_inc(s_V, 1)

            def gla_values(h):
                if h == 0:
                    pe.wait_ge(s_gA, 9)
                    pe.wait_ge(s_ev, N_FM + 8)
                else:
                    pe.wait_ge(s_gcp, h)
                vh = gv[:, :, h * GDV:(h + 1) * GDV]
                mm(ps[:, 5, 0:GDV], gA[:, 0, h], vh[:, 0], start=True, stop=True)
                mm(ps[:, 5, GDV:2 * GDV], gAoff[:, h], vh[:, 0], start=True, stop=False)
                mm(ps[:, 5, GDV:2 * GDV], gA[:, 1, h], vh[:, 1], start=False, stop=True).then_inc(s_gpv, 1)

            def level(lv):
                pe.wait_ge(s_gG, lv + 1)
                pe.wait_ge(s_gA, lv + 1)
                g = gG[lv % 2].rearrange("p (h t) -> p h t", h=GH)
                if lv < LEVELS - 1:
                    for t in range(TT):
                        for h in range(GH):
                            last = mm(ps[:, 4 + t, h * P:h * P + P], g[:, h, t * P:t * P + P],
                                      g[:, h, t * P:t * P + P], start=True, stop=True)
                else:
                    for h in range(GH):
                        last = mm(ps[:, 4, h * P:h * P + P], g[:, h, 0:P], g[:, h, P:T], start=True, stop=True)
                last.then_inc(s_lv, 1)

            def mg_unit(u, slot, s, part, oh, ol):
                pe.wait_ge(s_lo, u + 1)
                if part < 2:
                    fm_unit(slot, 2 * s, part)
                else:
                    v8 = "p (b t) -> p b t"
                    fm_unit(slot, 2 * s + 1, 0, oh[:, :].rearrange(v8, t=T), ol[:, :].rearrange(v8, t=T), whole=True)

            for step in SCHED:
                if step[0] == "fm":
                    fm_group_half(step[1], step[1], step[2])
                elif step[0] == "gat":
                    pe.wait_ge(s_sma, 1)
                    for t in range(TT):
                        last = nc.tensor.transpose(ps[0:16, 3, t * P:t * P + P], ga[:, t, :], ident)
                    last.then_inc(s_gaT, 1)
                elif step[0] == "z":
                    pe.wait_ge(s_const, 48)
                    pe.wait_ge(s_gaTc, 1)
                    for h in range(GH):
                        last = mm(ps[:, 6 + h // 2, (h % 2) * T:(h % 2) * T + T], wa[:, h * P:h * P + P], gaT,
                                  start=True, stop=True)
                    last.then_inc(s_z, 1)
                elif step[0] == "diag":
                    for t in range(TT):
                        for h in range(GH):
                            last = mm(ps[:, 4 + t, h * P:h * P + P], fm[:, B_GK + h, t * P:t * P + P],
                                      fm[:, B_GQ + h, t * P:t * P + P], start=True, stop=True)
                    last.then_inc(s_lv, 1)
                elif step[0] == "level":
                    level(step[1])
                elif step[0] == "tm":
                    _, g, half = step
                    G = N_FM + g
                    pe.wait_ge(s_lo, 2 * G + half + 1)
                    if half == 0:
                        pe.wait_ge(s_ev, G - 2)
                        if g == CMP_AFTER + 1:
                            pe.wait_ge(s_kvc, 1)
                    tm_unit((2 * G + half) % 3, G % 3, half, hThi, hTlo)
                elif step[0] == "cmp1":
                    pe.wait_ge(s_flat, 1)
                    for i in range(N_CMPU):
                        r = U_CMP + i
                        pe.wait_ge(s_raw[r % 3], 16 * (r // 3 + 1))
                        c = i // 2
                        for l in range(16):
                            last = mm(ps[:, 3, 32 * c:32 * c + 30], raw_cmp[:, r % 3, l], flat[:, c, 16 * (i % 2) + l],
                                      start=i % 2 == 0 and l == 0, stop=i % 2 == 1 and l == 15)
                        last.then_inc(s_cmpu, 1)
                elif step[0] == "cmp2":
                    pe.wait_ge(s_hid, 1)
                    mm(ps[:, 3, 0:30], w2[:, 0], hidT[:, 0], start=True, stop=True)
                    for g in range(KVH):
                        last = mm(ps[0:NCMP, 3, 64 + P * g:64 + P * g + P], hidT[:, 1, g * NCMP:(g + 1) * NCMP],
                                  w2[:, 1], start=True, stop=True)
                    last.then_inc(s_cmp2, 1)
                elif step[0] == "S":
                    scores(step[1])
                elif step[0] == "T":
                    turn(step[1])
                elif step[0] == "V":
                    values(step[1])
                elif step[0] == "gpv":
                    gla_values(step[1])
                elif step[0] == "gtr":
                    h = step[1]
                    pe.wait_ge(s_on, GH)
                    if h >= 1:
                        pe.wait_ge(s_ogT, h)
                    for eh in range(2):
                        for t in range(TT):
                            last = nc.tensor.transpose(ps[:, 5, eh * T + t * P:eh * T + t * P + P],
                                                       oraw[:, 2 * h + t, eh * P:eh * P + P], ident)
                    last.then_inc(s_gtr, 1)
                elif step[0] == "mg":
                    _, m, part = step
                    if part == 0:
                        if m < 2:
                            pe.wait_ge(s_ev, N_GROUP)
                            pe.wait_ge(s_kvc, 1)
                        else:
                            pe.wait_ge(s_mrg, m - 1)
                    if part == 2 and m == 0:
                        pe.wait_ge(s_olo, 1)
                    mg_unit(U_MG + 3 * m + part, slot_of(U_MG + part), m % 2, part, ohi[0], olo[0])

            for bi in (1, 2):
                def gate_step(m, s):
                    pe.wait_ge(s_mrg, m - 1)
                    for part in range(3):
                        mg_unit(m * 3 + (U_MG + part), slot_of(U_MG + part), s, part, ohi[bi], olo[bi])

                pe.wait_ge(s_olo, bi + 1)
                with pe.Fori(bi * (N_CG // 2), (bi + 1) * (N_CG // 2)) as j:
                    for s in range(2):
                        gate_step(j * 2 + s, s)

            mh = merged_hi[:, :].rearrange("p (k t) -> p k t", k=KT)
            ml = merged_lo[:, :].rearrange("p (k t) -> p k t", k=KT)
            pe.wait_ge(s_mlo, N_CG)
            pe.wait_ge(s_mrg, 3 * N_CG)

            def out_group(g, gi):
                for half in range(2):
                    pe.wait_ge(s_lo, g * 2 + (U_WO + half + 1))
                    if half == 0 and not (isinstance(g, int) and g < 3):
                        pe.wait_ge(s_x2, g - 2)
                    tm_unit(slot_of(U_WO + 2 * gi + half), gi, half, mh, ml)

            for g in range(3):
                out_group(g, g)
            with pe.Fori(1, 2) as j:
                for gi in range(3):
                    out_group(j * 3 + gi, gi)
            for g in (6, 7):
                out_group(g, g - 6)

            pe.wait_ge(s_h2, TT)
            for i in range(KT // 2):
                if i >= 4:
                    pe.wait_ge(s_h2A if i % 2 else s_h2D, (i - 4) // 2 + 1)
                for k in (2 * i, 2 * i + 1):
                    for t in range(TT):
                        last = nc.tensor.transpose(ps[:, 4 + i % 4, (k % 2) * T + t * P:(k % 2) * T + t * P + P],
                                                   h2[:, t, k * P:k * P + P], ident)
                last.then_inc(s_h2t, 1)
            pe.wait_ge(s_h2A, KT // 4)
            pe.wait_ge(s_h2D, KT // 4)
            pe.wait_ge(s_rw, 64)
            for t in range(TT):
                for k in range(KT):
                    last = mm(ps[:, 0, 64 * t:64 * t + 36], h2T[:, k, t * P:t * P + P], rw[:, k, :],
                              start=k == 0, stop=k == KT - 1)
            last.then_inc(s_lgt, 1)
            pe.wait_ge(s_rc, 4)
            pe.wait_ge(s_M, 1)
            mm(ps[:, 1, 0:NE], tri, M[:, 0], start=True, stop=True)
            mm(ps[:, 1, NE:2 * NE], ones, M[:, 0], start=True, stop=False)
            mm(ps[:, 1, NE:2 * NE], tri, M[:, 1], start=False, stop=True)
            mm(ps[:, 1, 2 * NE:3 * NE], ones, M[:, 0], start=True, stop=False)
            mm(ps[:, 1, 2 * NE:3 * NE], ones, M[:, 1], start=False, stop=True).then_inc(s_pos, 1)
            pe.wait_ge(s_route, 1)
            npass = pe.value_load(npass_i[0:1, 0:1], min_val=1, max_val=T // SLOTS)

            def gather(m, half):
                for k in range(8 * half, 8 * half + 8):
                    o = ps[:, 2 + k // 4, (k % 4) * P:(k % 4 + 1) * P]
                    for t in range(TT):
                        last = mm(o, h2[:, t, :].rearrange("p (c k) -> p k c", k=KT)[:, k], Gb[:, t],
                                  start=t == 0, stop=t == TT - 1)
                last.then_inc(s_xg, 1)

            def scatter(m, t):
                if t == 0:
                    pe.wait_ge(s_osb, m * 2 + 2)
                for c in range(4):
                    if t == 1:
                        pe.wait_ge(s_add, m * 8 + (c + 2))
                    mm(ps[:, 2 + c, :], STb[:, t * P:t * P + P], osb[:, c * W:c * W + W],
                       start=True, stop=True).then_inc(s_sc, 1)

            def gate_up(n, par, uses, m):
                for h in range(2):
                    u = (2, 0)[par] + h
                    pe.wait_ge(s_u[u], uses * 32 + 32)
                    if h == 0 and par == 0:
                        pe.wait_ge(s_xgA, m + 1)
                        pe.wait_ge(s_xgD, m + 1)
                        pe.wait_ge(s_STc, m + 1)
                    for j in range(8):
                        k = 8 * h + j
                        xk = xgT[:, k, par * SLOTS:par * SLOTS + SLOTS]
                        mm(ps[0:SLOTS, 0, :], xk, unit_g[u][:, j], start=k == 0, stop=k == KT - 1)
                        a = mm(ps[SLOTS:P, 0, :], xk, unit_u[u][:, j], start=k == 0, stop=k == KT - 1)
                    a.then_inc(s_gu0 if h == 0 else s_gu, 1)

            def turn_gate_up(n):
                pe.wait_ge(s_gus, n + 1)
                for j in range(FT):
                    a = nc.tensor.transpose(ps[:, 1, j * P:j * P + P],
                                            gusb.rearrange("p (c j) -> p j c", j=FT)[:, j], ident)
                a.then_inc(s_tr, 1)

            def down(n):
                pe.wait_ge(s_mid, n + 1)
                pe.wait_ge(s_wd, n * 32 + 32)
                for c in range(2):
                    for j in range(FT):
                        mm(ps[0:SLOTS, 6 + c, :], hmid[:, j], wd[:, j, c * W:c * W + W],
                           start=j == 0, stop=j == FT - 1)
                        a = mm(ps[SLOTS:P, 6 + c, :], hmid[:, j], wd[:, j, 1024 + c * W:1024 + c * W + W],
                               start=j == 0, stop=j == FT - 1)
                a.then_inc(s_dn, 1)

            def pair(m, uses, first, last_of_pass):
                n = m * 2
                gate_up(n, 0, uses, m)
                if not first:
                    scatter(m - 1, 0)
                turn_gate_up(n)
                if not first:
                    scatter(m - 1, 1)
                down(n)
                gate_up(n + 1, 1, uses, m)
                if not last_of_pass:
                    pe.wait_ge(s_G, m + 2)
                    pe.wait_ge(s_add, m * 8 + 1)
                    gather(m + 1, 0)
                turn_gate_up(n + 1)
                if not last_of_pass:
                    gather(m + 1, 1)
                pe.wait_ge(s_Sm, m + 1)
                for t in range(TT):
                    a = nc.tensor.transpose(ps[:, 0, t * P:t * P + P], Sb[:, t], ident)
                a.then_inc(s_ST, 1)
                pe.wait_ge(s_osb, n + 1)
                down(n + 1)

            with pe.Fori(0, npass) as q:
                base = q * NPAIR
                pe.wait_ge(s_G, base + 1)
                pe.wait_ge(s_add, q * (8 * NPAIR) + 1)
                for half in range(2):
                    gather(base, half)
                pair(base, q * NPAIR, True, False)
                with pe.Fori(1, NPAIR - 1) as i:
                    pair(base + i, q * NPAIR + i, False, False)
                pair(base + (NPAIR - 1), q * NPAIR + (NPAIR - 1), False, True)
                for t in range(TT):
                    scatter(base + (NPAIR - 1), t)

        @block.scalar
        def _(act):
            done = [0]

            def link(ins):
                done[0] += 1
                ins.then_inc(s_act, 1)
                act.wait_ge(s_act, done[0])

            A = nc.scalar.activation
            for t in range(TT):
                act.wait_ge(s_x[t], 16)
                A(ar(TM0 + 2048 * t, D), xs[:, t, :], ACT.Square, accum_out=ssx[:, t:t + 1]).then_inc(s_ssx, 1)
            act.wait_ge(s_ms, 1)
            A(rx[:, 0:TT], ssx[:, 2:2 + TT], ACT.Sqrt).then_inc(s_sq, 1)
            act.wait_ge(s_rowT, 1)
            A(cols3, ps[:, 3, 0:84], ACT.Copy).then_inc(s_rowC, 1)
            act.wait_ge(s_rowC, 1)
            act.wait_ge(s_wsm, 32)
            A(wsm_hi, wsm, ACT.Copy).then_inc(s_wsh, 1)
            for i in range(KT // 2):
                act.wait_ge(s_xT, i + 1)
                for k in (2 * i, 2 * i + 1):
                    ins = nc.scalar.mul(hThi[:, k, :], ps[:, 4 + i % 4, (k % 2) * T:(k % 2) * T + T], g1T[:, k:k + 1])
                ins.then_inc(s_hhi, 1)

            def high_part(u, slot, rslot, uses):
                act.wait_ge(s_raw[rslot], uses * 16 + 16)
                if not (isinstance(u, int) and u < 3):
                    act.wait_ge(s_use, u - 2)
                A(whi[:, slot], raw[:, rslot], ACT.Copy).then_inc(s_hi, 1)

            def high_part_at(u):
                r = u + (N_CMPU if u >= U_CMP else 0)
                high_part(u, u % 3, r % 3, r // 3)

            def evac_fm(g, gi):
                act.wait_ge(s_use, g * 2 + 2)
                A(fm_flat[:, bass.ds(g * 512, 512)], ps[:, gi, :], ACT.Copy).then_inc(s_ev, 1)

            high_part_at(0)
            high_part_at(1)
            high_part_at(2)
            act.wait_ge(s_smp, 1)
            smp = ps[:, 3, 0:128].rearrange("p (a n) -> p a n", a=TT)
            A(ng, smp[:, :, 0:24], ACT.Sigmoid)
            A(ga, smp[:, :, 24:40], ACT.Copy).then_inc(s_sma, 1)
            for g in range(3):
                for half in range(2):
                    if 2 * g + half + 2 > 2:
                        high_part_at(2 * g + half + 2)
                evac_fm(g, g)
            with act.Fori(1, G_LOOP // 3) as j:
                for gi in range(3):
                    for half in range(2):
                        i = 2 * gi + half + 2
                        high_part(j * 6 + i, i % 3, i % 3, j * 2 + i // 3)
                    evac_fm(j * 3 + gi, gi)

            for step in SCHED:
                if step[0] in ("fm", "tm", "mg"):
                    u = {"fm": 2 * step[1] + step[2], "tm": U_TM + 2 * step[1] + step[2],
                         "mg": U_MG + 3 * step[1] + step[2]}[step[0]]
                    if not U_CMP <= u + 2 < U_CMP + 2:
                        high_part_at(u + 2)
                if step[0] == "fm" and step[2] == 1:
                    evac_fm(step[1], step[1] % 3)
                elif step[0] == "gat":
                    act.wait_ge(s_gaT, 1)
                    A(gaT, ps[0:16, 3, 0:T], ACT.Copy).then_inc(s_gaTc, 1)
                elif step[0] == "z":
                    act.wait_ge(s_y, 1)
                    A(gG[0], gG[0], ACT.Exp, scale=-1.0).then_inc(s_e, 1)
                    act.wait_ge(s_e, 1)
                    A(gG[0], gG[0], ACT.Ln, bias=1.0).then_inc(s_ln, 1)
                elif step[0] in ("diag", "level"):
                    lv = 0 if step[0] == "diag" else step[1] + 1
                    if lv < LEVELS:
                        act.wait_ge(s_gD, lv + 1)
                        A(gd, gd, ACT.Exp, scale=1.0 / TAU).then_inc(s_gE, 1)
                elif step[0] == "tm" and step[2] == 1:
                    g = step[1]
                    G = N_FM + g
                    act.wait_ge(s_use, 2 * G + 2)
                    dst, c = ((mv, g) if g < 4 else (gv, g - 4) if g < 8 else (kv35, g - 8) if g < TM_GG
                              else (gg, g - TM_GG))
                    A(dst[:, :, c * CW:c * CW + CW], ps[:, G % 3, :].rearrange("p (a n) -> p a n", a=TT),
                      ACT.Silu if g >= TM_GG else ACT.Copy).then_inc(s_ev, 1)
                elif step[0] == "cmp1":
                    act.wait_ge(s_cmpu, N_CMPU)
                    A(hidT, ps[:, 3, 0:64].rearrange("p (c n) -> p c n", c=2)[:, :, 0:30], ACT.Silu).then_inc(s_hid, 1)
                    high_part_at(U_CMP)
                    high_part_at(U_CMP + 1)
                elif step[0] == "cmp2":
                    act.wait_ge(s_cmp2, 1)
                    A(kcT, ps[:, 3, 0:30], ACT.Copy)
                    A(vc, ps[0:NCMP, 3, 64:64 + 2 * P].rearrange("p (g n) -> p g n", g=KVH), ACT.Copy).then_inc(s_kvc, 1)
                elif step[0] == "S":
                    u = step[1]
                    kind, h = unit_of(u)
                    act.wait_ge(s_nb, u + 1)
                    b = nb[u % 2]
                    A(aP[u % 2][:, 0:P], ps[:, 6, 0:P], ACT.Exp, bias=b[:, 0:1], scale=SCALE,
                      accum_out=su[u % 2][:, 0:1])
                    last = A(aP[u % 2][:, P:3 * P], ps[:, 6, P:3 * P], ACT.Exp, bias=b[:, 1:2], scale=SCALE,
                             accum_out=su[u % 2][:, 1:2])
                    if kind == "slc":
                        for t in range(TT):
                            last = A(cP[h % 2][:, t], ps[:, 6, 384 + 16 * t:384 + 16 * t + NCMP], ACT.Exp,
                                     bias=b[:, 2 + t:3 + t], scale=SCALE, accum_out=su[u % 2][:, 2 + t:3 + t])
                    last.then_inc(s_exp, 1)
                elif step[0] == "T":
                    u = step[1]
                    kind, h = unit_of(u)
                    act.wait_ge(s_T, u + 1)
                    last = A(aPT[u % 2], ps[:, 7, 0:3 * P], ACT.Copy)
                    if kind == "slc":
                        last = A(cPT[h % 2], ps[0:NCMP, 5, 0:T], ACT.Copy)
                    last.then_inc(s_PT, 1)
                elif step[0] == "gpv":
                    h = step[1]
                    act.wait_ge(s_gcp, h + 1)
                    if h >= 1:
                        act.wait_ge(s_gsq, h)
                    link(A(junk256, oraw[:, 2 * h], ACT.Square, accum_out=ssg[:, 2 * h:2 * h + 1]))
                    A(junk256, oraw[:, 2 * h + 1], ACT.Square, accum_out=ssg[:, 2 * h + 1:2 * h + 2]).then_inc(s_gsq, 1)
                elif step[0] == "gms":
                    act.wait_ge(s_gms, 1)
                    A(rg, ssg, ACT.Sqrt).then_inc(s_grt, 1)
                elif step[0] == "gtr":
                    h = step[1]
                    act.wait_ge(s_gtr, h + 1)
                    A(ogT[:, 2 * h:2 * h + 2].rearrange("p b t -> p (b t)"), ps[:, 5, :], ACT.Copy).then_inc(s_ogT, 1)
                elif step[0] == "osplit":
                    b = step[1]
                    if b == 1:
                        act.wait_ge(s_ogT, GH)
                    else:
                        act.wait_ge(s_O, MH if b == 0 else MH + NH)
                    if b == 2:
                        act.wait_ge(s_use, U_MG + 3 * N_CG)
                    A(ohi[b][:, :], osrc[b], ACT.Copy).then_inc(s_ohi, 1)
                elif step[0] == "mg" and step[2] == 2:
                    m = step[1]
                    act.wait_ge(s_use, U_MG + 3 * m + 3)
                    if m >= 2:
                        act.wait_ge(s_mrg, m - 1)
                    A(sg[m % 2], ps[:, 2 * (m % 2), :], ACT.Sigmoid).then_inc(s_sig, 1)

            for bi in (1, 2):
                with act.Fori(bi * (N_CG // 2), (bi + 1) * (N_CG // 2)) as j:
                    for s in range(2):
                        m = j * 2 + s
                        for part in range(3):
                            i = 3 * s + part + 2
                            high_part(j * 6 + (U_MG + i), (U_MG + i) % 3, (U_MG + N_CMPU + i) % 3,
                                      j * 2 + (U_MG + N_CMPU + i) // 3)
                        act.wait_ge(s_use, m * 3 + (U_MG + 3))
                        act.wait_ge(s_mrg, m - 1)
                        A(sg[s], ps[:, 2 * s, :], ACT.Sigmoid).then_inc(s_sig, 1)
                        if bi == 2:
                            act.wait_ge(s_mrg, m + 1)
                            q = bass.ds(j * 1024 + (s * 512 - N_CG * 2 * 512), 512)
                            A(merged_hi[:, q], merged_flat[:, q], ACT.Copy).then_inc(s_mhi, 1)
            for u in range(U_WO, U_END - 2):
                high_part_at(u + 2)
            act.wait_ge(s_x2, N_CG)
            for t in range(TT):
                A(h2[:, t, :], xs[:, t, :], ACT.Square, accum_out=ss2[:, t:t + 1]).then_inc(s_ss2, 1)
            act.wait_ge(s_ms2, 1)
            A(r2[:, 0:TT], ss2[:, 2:4], ACT.Sqrt).then_inc(s_sq2, 1)
            for i in range(1, KT // 2, 2):
                act.wait_ge(s_h2t, i + 1)
                A(h2T[:, 2 * i:2 * i + 2, :].rearrange("p k t -> p (k t)"), ps[:, 4 + i % 4, :], ACT.Copy).then_inc(s_h2A, 1)
            act.wait_ge(s_re, 1)
            A(t8, t8, ACT.Exp)
            A(rs[:, 5], rs[:, 5], ACT.Exp).then_inc(s_rex, 1)
            act.wait_ge(s_route, 1)
            npass = act.value_load(npass_i[0:1, 0:1], min_val=1, max_val=T // SLOTS)

            def copy_xg(m):
                act.wait_ge(s_xg, m * 2 + 1)
                A(xgT[:, 0:8].rearrange("p k s -> p (k s)"), ps[:, 2:4, :].rearrange("p a n -> p (a n)"),
                  ACT.Copy).then_inc(s_xgA, 1)

            def copy_gu(n):
                act.wait_ge(s_gu, n + 1)
                A(gusb, ps[:, 0, :], ACT.Copy).then_inc(s_gus, 1)

            def silu(n):
                act.wait_ge(s_tr, n + 1)
                tr = ps[:, 1, :].rearrange("p (j two s) -> p j two s", two=2, s=SLOTS)
                A(hmid, tr[:, :, 0], ACT.Silu).then_inc(s_silu, 1)

            def copy_out(n, par):
                act.wait_ge(s_dn, n + 1)
                o = osb[par * SLOTS:par * SLOTS + SLOTS]
                A(o[:, 0:1024], ps[0:SLOTS, 6:8, :].rearrange("p a n -> p (a n)"), ACT.Copy)
                A(o[:, 1024:D], ps[SLOTS:P, 6:8, :].rearrange("p a n -> p (a n)"), ACT.Copy).then_inc(s_osb, 1)

            def pair(m, last_of_pass):
                n = m * 2
                copy_gu(n)
                silu(n)
                copy_out(n, 0)
                copy_gu(n + 1)
                if not last_of_pass:
                    copy_xg(m + 1)
                silu(n + 1)
                act.wait_ge(s_ST, m + 1)
                A(STb, ps[:, 0, 0:T], ACT.Copy).then_inc(s_STc, 1)
                copy_out(n + 1, 1)

            with act.Fori(0, npass) as q:
                base = q * NPAIR
                copy_xg(base)
                with act.Fori(0, NPAIR - 1) as i:
                    pair(base + i, False)
                pair(base + (NPAIR - 1), True)

            act.wait_ge(s_add, npass * (8 * NPAIR) + 1)
            for t in range(TT):
                A(h2[:, t, :], xs[:, t, :], ACT.Square, accum_out=ss2[:, t:t + 1]).then_inc(s_ssf, 1)
            act.wait_ge(s_msf, 1)
            A(r2[:, 0:TT], ss2[:, 2:4], ACT.Sqrt).then_inc(s_sqf, 1)

        @block.vector
        def _(dve):
            done = [0]
            v = nc.vector

            def link(ins):
                done[0] += 1
                ins.then_inc(s_dve, 1)
                dve.wait_ge(s_dve, done[0])

            def rms_scale(ss, r, width, s_in, s_out, s_root, n):
                dve.wait_ge(s_in, n)
                v.tensor_scalar(ss[:, n:2 * n], ss[:, 0:n], 1.0 / width, EPS, ALU.mult, ALU.add).then_inc(s_out, 1)
                dve.wait_ge(s_root, 1)
                link(v.reciprocal(r[:, n:2 * n], r[:, 0:n]))

            rms_scale(ssx, rx, D, s_ssx, s_ms, s_sq, TT)
            for t in range(TT):
                v.tensor_scalar(xn[:, t, :], xs[:, t, :], rx[:, 2 + t:3 + t], None, ALU.mult).then_inc(s_xn, 1)
            dve.wait_ge(s_wsh, 1)
            v.tensor_tensor(wsm_lo, wsm, wsm_hi.bitcast(F32), ALU.subtract).then_inc(s_wsl, 1)
            dve.wait_ge(s_rowC, 1)
            for i in range(KT // 2):
                dve.wait_ge(s_hhi, i + 1)
                for k in (2 * i, 2 * i + 1):
                    ins = v.scalar_tensor_tensor(out=hTlo[:, k, :], in0=ps[:, 4 + i % 4, (k % 2) * T:(k % 2) * T + T],
                                                 scalar=g1T[:, k:k + 1], in1=hThi[:, k, :].bitcast(F32),
                                                 op0=ALU.mult, op1=ALU.subtract)
                ins.then_inc(s_hlo, 1)

            def rest(u, slot, rslot):
                dve.wait_ge(s_hi, u + 1)
                v.tensor_tensor(wlo[:, slot], raw[:, rslot], whi[:, slot].bitcast(F32), ALU.subtract).then_inc(s_lo, 1)

            def rest_at(u):
                rest(u, u % 3, (u + (N_CMPU if u >= U_CMP else 0)) % 3)

            for u in range(2 * G_LOOP // 5 + 2):
                rest_at(u)
            with dve.Fori(1, G_LOOP // 3) as j:
                for i in range(2, 8):
                    rest(j * 6 + i, i % 3, i % 3)

            def halves(ap, H):
                w4 = ap.rearrange("p (n two r) -> p n two r", two=2, r=H)
                return w4[:, :, 0, :], w4[:, :, 1, :]

            qflat, kflat = fm_flat[:, 0:1024], fm_flat[:, 1024:2048]

            def level_diffs(lv):
                H = 1 << lv
                b0, b1 = halves(gb, H)
                ref = b0[:, :, H - 1:H].to_broadcast([P, 1024 // (2 * H), H])
                d0, d1 = halves(gd, H)
                v.tensor_tensor(d0, ref, b0, ALU.subtract)
                v.tensor_tensor(d1, b1, ref, ALU.subtract).then_inc(s_gD, 1)

            def level_product(lv):
                H = 1 << lv
                dve.wait_ge(s_gE, lv + 1)
                d0, d1 = halves(gd, H)
                o0, o1 = halves(gG[lv % 2], H)
                if lv >= 2:
                    dve.wait_ge(s_lv, lv)
                v.tensor_tensor(o0, d0, halves(kflat, H)[0], ALU.mult)
                v.scalar_tensor_tensor(out=o1, in0=d1, scalar=SCALE, in1=halves(qflat, H)[1],
                                       op0=ALU.mult, op1=ALU.mult).then_inc(s_gG, 1)

            for step in SCHED:
                if step[0] in ("fm", "tm", "mg"):
                    u = {"fm": 2 * step[1] + step[2], "tm": U_TM + 2 * step[1] + step[2],
                         "mg": U_MG + 3 * step[1] + step[2]}[step[0]]
                    if not U_CMP <= u + 2 < U_CMP + 2:
                        rest_at(u + 2)
                if step[0] == "cmp1":
                    rest_at(U_CMP)
                    rest_at(U_CMP + 1)
                elif step[0] == "z":
                    dve.wait_ge(s_z, 1)
                    for h in range(GH):
                        ins = v.tensor_scalar(gd[:, h * T:h * T + T], ps[:, 6 + h // 2, (h % 2) * T:(h % 2) * T + T],
                                              baT[:, h:h + 1], None, ALU.add)
                    link(ins)
                    v.scalar_tensor_tensor(out=gG[0], in0=gd, scalar=-1.0, in1=gd, op0=ALU.mult,
                                           op1=ALU.max).then_inc(s_y, 1)
                    link(v.tensor_scalar(gG[1], gd, 0.0, None, ALU.min))
                    dve.wait_ge(s_ln, 1)
                    for h in range(GH):
                        q = slice(h * T, h * T + T)
                        ins = v.tensor_tensor_scan(gb[:, q], gG[1][:, q], gG[0][:, q], 0.0, ALU.add, ALU.subtract)
                    link(ins)
                    level_diffs(0)
                elif step[0] == "diag":
                    level_product(0)
                    dve.wait_ge(s_lv, 1)
                    for t in range(TT):
                        ins = v.scalar_tensor_tensor(out=gA[:, t], in0=ps[:, 4 + t, :].rearrange("p (h t) -> p h t", h=GH),
                                                     scalar=SCALE, in1=ident.unsqueeze(1).to_broadcast([P, GH, P]),
                                                     op0=ALU.mult, op1=ALU.mult)
                    ins.then_inc(s_gA, 1)
                    dve.wait_ge(s_masks, N_MASKS)
                    dve.wait_ge(s_gG, 1)
                    level_diffs(1)
                elif step[0] == "level":
                    lv = step[1]
                    if lv + 1 < LEVELS:
                        level_product(lv + 1)
                    if lv + 2 < LEVELS:
                        dve.wait_ge(s_gG, lv + 2)
                        level_diffs(lv + 2)
                    dve.wait_ge(s_lv, lv + 2)
                    dve.wait_ge(s_gA, lv + 1)
                    if lv < LEVELS - 1:
                        for t in range(TT):
                            ins = v.copy_predicated(gA[:, t],
                                                    lmask[:, lv].bitcast(I32).unsqueeze(1).to_broadcast([P, GH, P]),
                                                    ps[:, 4 + t, :].rearrange("p (h t) -> p h t", h=GH))
                    else:
                        ins = v.tensor_copy(gAoff, ps[:, 4, :].rearrange("p (h t) -> p h t", h=GH))
                    ins.then_inc(s_gA, 1)
                elif step[0] == "flat":
                    dve.wait_ge(s_ev, N_FM - 2)
                    for c in range(2):
                        for g in range(KVH):
                            for a in range(2):
                                src = fm[:, B_KCMP + 2 * c + g, 16 * a:16 * a + 240].rearrange("p (n b) -> p b n", b=16)
                                pe_ = peT[:, 32 * c + 16 * a:32 * c + 16 * a + 16].unsqueeze(2).to_broadcast([P, 16, NCMP])
                                ins = v.tensor_tensor(flat[:, c, 16 * a:16 * a + 16, g * NCMP:(g + 1) * NCMP],
                                                      src, pe_, ALU.add)
                    ins.then_inc(s_flat, 1)
                elif step[0] == "S":
                    u = step[1]
                    kind, h = unit_of(u)
                    n = 4 if kind == "slc" else 2
                    m_, b_, s_, r_ = mx[u % 2], nb[u % 2], su[u % 2], rr[u % 2]
                    dve.wait_ge(s_S, u + 1)
                    v.tensor_reduce(m_[:, 0:1], ps[:, 6, 0:P], AX_X, ALU.max)
                    ins = v.tensor_reduce(m_[:, 1:2], ps[:, 6, P:3 * P], AX_X, ALU.max)
                    if kind == "slc":
                        ins = v.tensor_reduce(m_[:, 2:4], ps[:, 6, 384:416].rearrange("p (a n) -> p a n", a=2)[:, :, 0:NCMP],
                                              AX_X, ALU.max)
                    link(ins)
                    v.tensor_scalar(b_[:, 0:n], m_[:, 0:n], -SCALE, 1e28, ALU.mult, ALU.min).then_inc(s_nb, 1)
                    dve.wait_ge(s_exp, u + 1)
                    if kind == "slc":
                        link(v.tensor_scalar(s_[:, 2:4], s_[:, 2:4], 1e-30, None, ALU.max))
                    link(v.reciprocal(r_[:, 0:n], s_[:, 0:n]))
                    if kind != "moba":
                        br = {"slc": 1, "win": 2}[kind]
                        ins = v.tensor_tensor(r_[:, 0:2], r_[:, 0:2], ng[:, :, 3 * h + br], ALU.mult)
                        if kind == "slc":
                            ins = v.tensor_tensor(r_[:, 2:4], r_[:, 2:4], ng[:, :, 3 * h], ALU.mult)
                        link(ins)
                    p_ = aP[u % 2]
                    v.tensor_scalar(p_[:, 0:P], p_[:, 0:P], r_[:, 0:1], None, ALU.mult)
                    ins = v.tensor_scalar(p_[:, P:3 * P], p_[:, P:3 * P], r_[:, 1:2], None, ALU.mult)
                    if kind == "slc":
                        for t in range(TT):
                            ins = v.scalar_tensor_tensor(out=cP[h % 2][:, t], in0=cP[h % 2][:, t],
                                                         scalar=r_[:, 2 + t:3 + t], in1=cmul[:, t],
                                                         op0=ALU.mult, op1=ALU.mult)
                    ins.then_inc(s_P, 1)
                elif step[0] == "V":
                    u = step[1]
                    kind, h = unit_of(u)
                    if kind != "slc":
                        dve.wait_ge(s_V, u + 1)
                        b = (B_MQ if kind == "moba" else B_NQ) + h
                        v.tensor_copy(fm[:, b], ps[:, 4, (h % 2) * T:(h % 2) * T + T]).then_inc(s_O, 1)
                elif step[0] == "gpv":
                    h = step[1]
                    dve.wait_ge(s_gpv, h + 1)
                    v.tensor_copy(oraw[:, 2 * h:2 * h + 2].rearrange("p i n -> p (i n)"), ps[:, 5, :]).then_inc(s_gcp, 1)
                elif step[0] == "gms":
                    dve.wait_ge(s_gsq, GH)
                    v.tensor_scalar(ssg, ssg, 1.0 / GDV, EPS, ALU.mult, ALU.add).then_inc(s_gms, 1)
                    dve.wait_ge(s_grt, 1)
                    link(v.reciprocal(rg, rg))
                elif step[0] == "gnorm":
                    h = step[1]
                    if h == 0:
                        dve.wait_ge(s_ev, N_GROUP)
                    for t in range(TT):
                        i = 2 * h + t
                        ins = v.scalar_tensor_tensor(out=oraw[:, i], in0=oraw[:, i], scalar=rg[:, i:i + 1], in1=gng,
                                                     op0=ALU.mult, op1=ALU.mult)
                    link(ins)
                    for t in range(TT):
                        i = 2 * h + t
                        ins = v.tensor_tensor(oraw[:, i], oraw[:, i], gg[:, t, h * GDV:(h + 1) * GDV], ALU.mult)
                    ins.then_inc(s_on, 1)
                elif step[0] == "osplit":
                    b = step[1]
                    dve.wait_ge(s_ohi, b + 1)
                    v.tensor_tensor(olo[b][:, :], osrc[b], ohi[b][:, :].bitcast(F32), ALU.subtract).then_inc(s_olo, 1)
                elif step[0] == "mg" and step[2] == 2:
                    m = step[1]
                    dve.wait_ge(s_sig, m + 1)
                    v.tensor_tensor(merged_flat[:, 512 * m:512 * m + 512], sg[m % 2],
                                    ps[:, 2 * (m % 2) + 1, :], ALU.mult).then_inc(s_mrg, 1)
            for bi in (1, 2):
                with dve.Fori(bi * (N_CG // 2), (bi + 1) * (N_CG // 2)) as j:
                    for s in range(2):
                        m = j * 2 + s
                        for part in range(3):
                            i = 3 * s + part + 2
                            rest(j * 6 + (U_MG + i), (U_MG + i) % 3, (U_MG + N_CMPU + i) % 3)
                        dve.wait_ge(s_sig, m + 1)
                        q = bass.ds(j * 1024 + (s * 512 - N_CG * bi * 512), 512)
                        v.tensor_tensor(sg[s], sg[s], ps[:, 2 * s + 1, :], ALU.mult).then_inc(s_tmp, 1)
                        dve.wait_ge(s_tmp, m - (N_CG - 1))
                        v.tensor_tensor(merged_flat[:, q], merged_flat[:, q], sg[s], ALU.add).then_inc(s_mrg, 1)
                        if bi == 2:
                            dve.wait_ge(s_mhi, m - (2 * N_CG - 1))
                            v.tensor_tensor(merged_lo[:, q], merged_flat[:, q], merged_hi[:, q].bitcast(F32),
                                            ALU.subtract).then_inc(s_mlo, 1)

            def add_out(g, gi):
                dve.wait_ge(s_use, g * 2 + (U_WO + 2))
                dst = xs[:, :, bass.ds(g * CW, CW)]
                v.tensor_tensor(dst, dst, ps[:, gi, :].rearrange("p (a n) -> p a n", a=TT), ALU.add).then_inc(s_x2, 1)

            for g in range(N_CG):
                for half in range(2):
                    if 2 * g + half + 2 < 2 * N_CG:
                        rest_at(U_WO + 2 * g + half + 2)
                if g == 0:
                    dve.wait_ge(s_xr, 16 * TT)
                add_out(g, g % 3)

            rms_scale(ss2, r2, D, s_ss2, s_ms2, s_sq2, TT)
            dve.wait_ge(s_g2, 16)
            for t in range(TT):
                v.scalar_tensor_tensor(out=h2[:, t, :], in0=xs[:, t, :], scalar=r2[:, 2 + t:3 + t], in1=g2b,
                                       op0=ALU.mult, op1=ALU.mult).then_inc(s_h2, 1)
            for i in range(0, KT // 2, 2):
                dve.wait_ge(s_h2t, i + 1)
                v.tensor_copy(h2T[:, 2 * i:2 * i + 2, :].rearrange("p k t -> p (k t)"), ps[:, 4 + i % 4, :]).then_inc(s_h2D, 1)

            def bc(ap, n):
                return ap.unsqueeze(2).to_broadcast([P, TT, n])

            def first_max(vals, mxv, mnv, tmp, oh, n):
                link(v.tensor_reduce(mxv, vals, AX_X, ALU.max))
                link(v.tensor_tensor(oh, vals, bc(mxv, n), ALU.is_equal))
                link(v.tensor_tensor(tmp, oh, jm[:, 0:n].unsqueeze(1).to_broadcast([P, TT, n]), ALU.mult))
                link(v.tensor_reduce(mnv, tmp, AX_X, ALU.min))
                link(v.tensor_tensor(oh, tmp, bc(mnv, n), ALU.is_equal))

            dve.wait_ge(s_lgt, 1)
            dve.wait_ge(s_rc, 4)
            lgp = ps[:, 0, 0:128].rearrange("p (a n) -> p a n", a=TT)[:, :, 0:36]
            link(v.tensor_tensor(lg, lgp, rbb.unsqueeze(1).to_broadcast([P, TT, 36]), ALU.add))
            gl, el = lg[:, :, 0:GROUPS], lg[:, :, GROUPS:36]
            first_max(gl, rs[:, 0], rs[:, 1], t8, goh, GROUPS)
            link(v.tensor_tensor(t8, gl, bc(rs[:, 0], GROUPS), ALU.subtract))
            gx = [goh[:, t].unsqueeze(2).to_broadcast([P, GROUPS, EPG]) for t in range(TT)]
            for t in range(TT):
                ins = v.tensor_tensor(em[:, t].rearrange("p (g e) -> p g e", g=GROUPS),
                                      el[:, t].rearrange("p (g e) -> p g e", g=GROUPS), gx[t], ALU.mult)
            link(ins)
            link(v.tensor_scalar(oh1[:, :, 0:GROUPS], goh, -1.0, -NEG, ALU.add, ALU.mult))
            for t in range(TT):
                ins = v.tensor_tensor(em[:, t].rearrange("p (g e) -> p g e", g=GROUPS),
                                      em[:, t].rearrange("p (g e) -> p g e", g=GROUPS),
                                      oh1[:, t, 0:GROUPS].unsqueeze(2).to_broadcast([P, GROUPS, EPG]), ALU.add)
            link(ins)
            first_max(em, rs[:, 2], rs[:, 3], t64, oh1, NE)
            link(v.scalar_tensor_tensor(out=em, in0=oh1, scalar=10 * NEG, in1=em, op0=ALU.mult, op1=ALU.add))
            first_max(em, rs[:, 4], rs[:, 3], t64, oh2, NE)
            link(v.tensor_tensor(M, oh1, oh2, ALU.add))
            v.tensor_copy(M, M).then_inc(s_M, 1)
            v.tensor_tensor(rs[:, 5], rs[:, 4], rs[:, 2], ALU.subtract).then_inc(s_re, 1)
            dve.wait_ge(s_rex, 1)
            link(v.tensor_reduce(rs[:, 6], t8, AX_X, ALU.add))
            link(v.tensor_scalar(rs[:, 7], rs[:, 5], 1.0, None, ALU.add))
            link(v.tensor_tensor(rs[:, 6], rs[:, 6], rs[:, 7], ALU.mult))
            link(v.reciprocal(rs[:, 8], rs[:, 6]))
            link(v.tensor_tensor(rs[:, 9], rs[:, 8], rs[:, 5], ALU.mult))
            link(v.tensor_tensor(oh1, oh1, bc(rs[:, 8], NE), ALU.mult))
            link(v.tensor_tensor(oh2, oh2, bc(rs[:, 9], NE), ALU.mult))
            link(v.tensor_tensor(wgt, oh1, oh2, ALU.add))
            dve.wait_ge(s_pos, 1)
            link(v.tensor_scalar(t64, M, -1.0, 1e6, ALU.add, ALU.mult))
            link(v.tensor_tensor(posm, ps[:, 1, 0:2 * NE].rearrange("p (a e) -> p a e", a=TT), t64, ALU.add))
            link(v.tensor_reduce(rs[:, 10, 0:1], ps[:, 1, 2 * NE:3 * NE], AX_X, ALU.max))
            link(v.tensor_scalar(rs[:, 11, 0:1], rs[:, 10, 0:1], float(SLOTS), 1.0, ALU.is_gt, ALU.add))
            for k in range(2, T // SLOTS):
                link(v.tensor_scalar(rs[:, 12, 0:1], rs[:, 10, 0:1], float(SLOTS * k), None, ALU.is_gt))
                link(v.tensor_tensor(rs[:, 11, 0:1], rs[:, 11, 0:1], rs[:, 12, 0:1], ALU.add))
            v.tensor_copy(npass_i, rs[:, 11, 0:1]).then_inc(s_route, 1)
            v.memset(npass_f[:, 1:2], 0.0).then_inc(s_add, 1)
            v.memset(npass_f[:, 2:3], 0.0).then_inc(s_STc, 1)
            dve.wait_ge(s_route, 1)
            npass = dve.value_load(npass_i[0:1, 0:1], min_val=1, max_val=T // SLOTS)

            def make_g(e):
                for par in range(2):
                    for t in range(TT):
                        ins = v.tensor_scalar(Gb[:, t, par * SLOTS:par * SLOTS + SLOTS], iota,
                                              posm[:, t, bass.ds(e + par, 1)], None, ALU.is_equal)
                ins.then_inc(s_G, 1)

            def make_s(e):
                for par in range(2):
                    for t in range(TT):
                        ins = v.tensor_scalar(Sb[:, t, par * SLOTS:par * SLOTS + SLOTS], iota,
                                              posm[:, t, bass.ds(e + par, 1)], wgt[:, t, bass.ds(e + par, 1)],
                                              ALU.is_equal, ALU.mult)
                ins.then_inc(s_Sm, 1)

            def copy_xg(m):
                dve.wait_ge(s_xg, m * 2 + 2)
                v.tensor_copy(xgT[:, 8:16].rearrange("p k s -> p (k s)"),
                              ps[:, 4:6, :].rearrange("p a n -> p (a n)")).then_inc(s_xgD, 1)

            def middle(n):
                dve.wait_ge(s_silu, n + 1)
                tr = ps[:, 1, :].rearrange("p (j two s) -> p j two s", two=2, s=SLOTS)
                v.tensor_tensor(hmid, hmid, tr[:, :, 1], ALU.mult).then_inc(s_mid, 1)

            def adds(m, t):
                for c in range(4):
                    dve.wait_ge(s_sc, m * 8 + (4 * t + c + 1))
                    xc = xs[:, t, c * W:c * W + W]
                    v.tensor_tensor(xc, xc, ps[:, 2 + c, :], ALU.add).then_inc(s_add, 1)

            def pair(m, e, first, last_of_pass):
                n = m * 2
                if not last_of_pass:
                    make_g(e + 2)
                if not first:
                    adds(m - 1, 0)
                middle(n)
                if not first:
                    adds(m - 1, 1)
                middle(n + 1)
                if not last_of_pass:
                    copy_xg(m + 1)
                    dve.wait_ge(s_ST, m + 1)
                    make_s(e + 2)

            with dve.Fori(0, npass) as q:
                base = q * NPAIR
                make_g(0)
                make_s(0)
                copy_xg(base)
                pair(base, 0, True, False)
                with dve.Fori(1, NPAIR - 1) as i:
                    pair(base + i, i * 2, False, False)
                pair(base + (NPAIR - 1), NE - 2, False, True)
                for t in range(TT):
                    adds(base + (NPAIR - 1), t)
                v.tensor_scalar(posm, posm, -float(SLOTS), None, ALU.add).then_inc(s_M, 1)
                dve.wait_ge(s_M, q + 2)

            rms_scale(ss2, r2, D, s_ssf, s_msf, s_sqf, TT)
            dve.wait_ge(s_gf, 16)
            for t in range(TT):
                v.scalar_tensor_tensor(out=h2[:, t, :], in0=xs[:, t, :], scalar=r2[:, 2 + t:3 + t], in1=gfb,
                                       op0=ALU.mult, op1=ALU.mult).then_inc(s_y1, 1)


_INS = ['x', 'norm1_g', 'w_in', 'nsa_cmp_pe', 'nsa_cmp_w1', 'nsa_cmp_w2', 'gla_wa', 'gla_ba', 'gla_norm_g',
        'w_br_moba', 'w_br_nsa', 'w_br_gla', 'w_out', 'norm2_g', 'router_group_w', 'router_group_b',
        'router_expert_w', 'router_expert_b', 'expert_w_gate', 'expert_w_up', 'expert_w_down', 'final_norm_g']
_OUTS = [((1, 256, 2048), 'float32')]


def kernel(**inputs):
    import numpy as _np
    import concourse.bacc as _bacc
    from concourse import mybir as _mybir
    from concourse.bass_utils import run_bass_kernel_spmd as _run

    nc = _bacc.Bacc("TRN2", target_bir_lowering=False, num_devices=1, dynamic_dma_scratch_size=1024)
    arrays, args = {}, []
    for name in _INS:
        a = _np.ascontiguousarray(inputs[name])
        arrays[f"in_{name}_dram"] = a
        args.append(nc.dram_tensor(f"in_{name}_dram", a.shape, _mybir.dt.from_np(a.dtype), kind="ExternalInput").ap())
    for i, (shape, dtype) in enumerate(_OUTS):
        dt = _mybir.dt.from_np(_np.dtype(dtype))
        args.append(nc.dram_tensor(f"out_{i}_dram", shape, dt, kind="ExternalOutput").ap())
    build(nc, *args)
    r = _run(nc, [arrays], core_ids=[0])
    return r.results[0]["out_0_dram"]
```

```python
from contextlib import ExitStack

import concourse.bass as bass
from concourse import mybir
from concourse.alu_op_type import AluOpType as ALU

F32 = mybir.dt.float32
F32R = mybir.dt.float32r
I32 = mybir.dt.int32
ACT = mybir.ActivationFunctionType
AX_X = mybir.AxisListType.X

P = 128
T = 256
TT = T // P
D = 2048
KT = D // P
HD = 128
SCALE = HD ** -0.5
NEG = -1e30
EPS = 1e-6
TAU = 16.0
CMP_LEN, CMP_STRIDE = 32, 16
NCMP = (T - CMP_LEN) // CMP_STRIDE + 1
MH = NH = 8
KVH = 2
GH, GDV = 4, 256
LEVELS = 8
NE, GROUPS = 32, 4
EPG = NE // GROUPS
FF = 512
FT = FF // P
SLOTS = 64
NPAIR = NE // 2
W = 512

C_MQ, C_MK, C_MV, C_NQ, C_NKV = 0, 1024, 2048, 3072, 4096
C_NG = C_NKV + 1536
C_GQ = C_NG + 24
C_GK = C_GQ + 512
C_GV = C_GK + 512
C_GA = C_GV + 1024
C_GG = C_GA + 16
C_MG = C_GG + 1024

UK, CW = 8, 256
USIZE = UK * CW
N_CG = D // CW
FM_COLS = ([C_GQ, C_GQ + CW, C_GK, C_GK + CW] + [C_MQ + CW * i for i in range(8)]
           + [C_NQ + CW * i for i in range(4)]
           + [C_NKV, C_NKV + CW, C_NKV + 2 * CW, C_NKV + 4 * CW])
TM_COLS = ([C_MV + CW * i for i in range(4)] + [C_GV + CW * i for i in range(4)]
           + [C_NKV + 3 * CW, C_NKV + 5 * CW] + [C_GG + CW * i for i in range(4)])
N_FM, N_TM = len(FM_COLS), len(TM_COLS)
N_GROUP = N_FM + N_TM
G_LOOP = 15
TM_KS, TM_VW, TM_GG = 8, 9, 10
CMP_AFTER = 10
N_CMPU = 4
U_TM = 2 * N_FM
U_MG = U_TM + 2 * N_TM
U_WO = U_MG + 9 * N_CG
U_END = U_WO + 2 * N_CG
U_CMP = U_TM + 2 * CMP_AFTER
B_GQ, B_GK, B_MQ, B_MK, B_NQ, B_KCMP, B_VCMP, B_KSLC, B_KWIN = 0, 4, 8, 16, 24, 32, 34, 36, 38
BRANCH_ORDER = (0, 2, 1)


def load_of(u):
    return u + min(max(u - U_CMP, 0), N_CMPU)


UNITS = MH + 2 * NH


def unit_of(u):
    return ("moba", u) if u < MH else (("slc", "win")[(u - MH) % 2], (u - MH) // 2)


def schedule():
    steps = []
    count = [0]

    def attention(first, end):
        i = count[0]
        if i >= end + 2:
            return
        if i - 2 >= first:
            steps.append(("V", i - 2))
        if first <= i - 1 < end:
            steps.append(("T", i - 1))
        if i < end:
            steps.append(("S", i))
        count[0] += 1

    for g in range(G_LOOP, N_FM):
        steps += [("fm", g, 0), ("fm", g, 1)]
        if g == G_LOOP:
            steps.append(("gat",))
        if g == G_LOOP + 1:
            steps.append(("z",))
    steps.append(("diag",))
    for g in range(N_TM):
        for half in range(2):
            steps.append(("tm", g, half))
            if 0 <= 2 * (g - CMP_AFTER) + half < N_CMPU:
                steps.append(("cmp1", 2 * (g - CMP_AFTER) + half))
            if g == CMP_AFTER + 2:
                steps.append(("cmp2", "cmp3")[half:half + 1])
            if g >= 8:
                attention(0, MH)
        if g < LEVELS:
            steps.append(("level", g))
        if g == LEVELS - 1:
            steps.append(("flat",))
        if g >= TM_GG:
            steps.append(("gpv", g - TM_GG))
    while count[0] < MH + 2:
        attention(0, MH)
    steps.append(("osplit", 0))
    count[0] = MH
    for m in range(N_CG):
        for part in range(3):
            steps.append(("mg", m, part))
            attention(MH, UNITS)
            if m == N_CG - 2 and part == 0:
                steps.append(("gms",))
            if m == N_CG - 2 and part > 0:
                steps.append(("gnorm", part - 1))
            if m == N_CG - 1 and part < 2:
                steps.append(("gnorm", part + 2))
            if m == N_CG - 1 and part > 0:
                steps.append(("gtr", 2 * part - 2))
                steps.append(("gtr", 2 * part - 1))
    assert count[0] >= UNITS + 2
    steps.append(("osplit", 1))
    steps.append(("osplit", 2))
    return steps


def build(nc, x, norm1_g, w_in, cmp_pe, cmp_w1, cmp_w2, gla_wa, gla_ba, gla_norm_g, w_br_moba, w_br_nsa,
          w_br_gla, w_out, norm2_g, rg_w, rg_b, re_w, re_b, e_gate, e_up, e_down, final_g, out):
    SCHED = schedule()
    with ExitStack() as ctx:
        def sb(name, shape, dt=F32):
            return ctx.enter_context(nc.sbuf_tensor(name, shape, dt))

        def sem(name):
            return ctx.enter_context(nc.semaphore(name))

        XS0, HB0 = 0, TT * D
        ID0 = HB0 + KT * T
        SM0 = ID0 + P
        AR0 = SM0 + 5840
        SLAB = AR0 + 40960
        base_bytes = (nc.sbuf_base + 31) // 32 * 32
        sb("slab", [P, SLAB])

        def r32(name, a, n):
            return nc.alloc_sbuf_tensor_at(name, [P, n], F32R, offset=base_bytes + 4 * a)

        ps = ctx.enter_context(nc.psum_tensor("ps", [P, 8, 512], F32))

        buffers = {}

        def at(a, n, parts=P):
            skip = a % 8
            if (a, n) not in buffers:
                buffers[a, n] = nc.alloc_sbuf_tensor_at(f"at{a}_{n}", [P, skip + n], F32,
                                                        offset=base_bytes + 4 * (a - skip))
            return buffers[a, n][0:parts, skip:skip + n]

        def ar(a, n, parts=P):
            return at(AR0 + a, n, parts)

        def sm(a, n, parts=P):
            return at(SM0 + a, n, parts)

        ident = at(ID0, P)
        xs = at(XS0, TT * D).rearrange("p (a d) -> p a d", a=TT)
        h2 = at(HB0, TT * D).rearrange("p (a d) -> p a d", a=TT)
        hThi = r32("hThi", HB0, KT * T)[:, :].rearrange("p (k t) -> p k t", k=KT)
        hTlo = r32("hTlo", XS0, KT * T)[:, :].rearrange("p (k t) -> p k t", k=KT)
        RAW0 = 6 * USIZE
        FM0 = RAW0 + 3 * USIZE
        TM0 = FM0 + 40 * T
        TMP0 = TM0 + N_TM * TT * CW
        whi = r32("whi", AR0, 3 * USIZE)[:, :].rearrange("p (s k n) -> p s k n", s=3, k=UK)
        wlo = r32("wlo", AR0 + 3 * USIZE, 3 * USIZE)[:, :].rearrange("p (s k n) -> p s k n", s=3, k=UK)
        raw = ar(RAW0, 3 * USIZE).rearrange("p (s k n) -> p s k n", s=3, k=UK)
        raw_cmp = ar(RAW0, 3 * USIZE).rearrange("p (s l o) -> p s l o", s=3, l=USIZE // HD)
        fm_flat = ar(FM0, 40 * T)
        fm = fm_flat.rearrange("p (b t) -> p b t", t=T)
        mv = ar(TM0, 2048).rearrange("p (a n) -> p a n", a=TT)
        gv = ar(TM0 + 2048, 2048).rearrange("p (a n) -> p a n", a=TT)
        gg = ar(TM0 + 4096, 2048).rearrange("p (a n) -> p a n", a=TT)
        kv35 = ar(TM0 + 6144, 1024).rearrange("p (a n) -> p a n", a=TT)
        merged_flat = ar(TM0, KT * T)
        merged_lo = r32("merged_lo", AR0 + TM0, KT * T)
        merged_hi = r32("merged_hi", AR0 + FM0 + 24 * T, KT * T)
        ogT = ar(TM0 + 4096, 2048).rearrange("p (b t) -> p b t", t=T)
        xn = ar(FM0, 2 * D).rearrange("p (a d) -> p a d", a=TT)
        wsm_hi = r32("wsm_hi", AR0 + TMP0 + 2048, KT * 40)[:, :].rearrange("p (k n) -> p k n", k=KT)
        wsm_lo = r32("wsm_lo", AR0 + TMP0 + 2048 + KT * 40, KT * 40)[:, :].rearrange("p (k n) -> p k n", k=KT)
        osrc = [fm_flat[:, B_MQ * T:(B_MQ + 8) * T], ar(TM0 + 4096, 2048), fm_flat[:, B_NQ * T:(B_NQ + 8) * T]]
        ohi_a, olo_a = r32("ohi_a", AR0 + FM0, 2048), r32("olo_a", AR0 + FM0 + B_MK * T, 2048)
        ohi_b, olo_b = r32("ohi_b", AR0 + FM0 + B_KCMP * T, 2048), r32("olo_b", AR0 + TMP0, 2048)
        ohi, olo = [ohi_a, ohi_b, ohi_a], [olo_a, olo_b, olo_a]
        gb = ar(TMP0, 1024)
        gd = ar(TMP0 + 1024, 1024)
        gG = [ar(TMP0 + 2048 + 1024 * i, 1024) for i in range(2)]
        lmask = ar(TMP0 + 4224, 896).rearrange("p (l t) -> p l t", t=P)
        aP = [ar(TMP0 + 384 * i, 384) for i in range(2)]
        aPT = [ar(TMP0 + 768 + 384 * i, 384) for i in range(2)]
        cP = [ar(TMP0 + 1536 + 32 * i, 30).rearrange("p (a n) -> p a n", a=TT) for i in range(2)]
        cPT = [ar(TMP0 + 1600 + 256 * i, 256, NCMP) for i in range(2)]
        flat = ar(TMP0 + 2112, 2048).rearrange("p (c l n) -> p c l n", c=2, l=CMP_LEN)
        sg = [ar(TMP0 + 4096 + 512 * i, 512) for i in range(2)]
        hid4 = ar(TMP0 + 4608, 256)
        wsm = sm(0, KT * 40).rearrange("p (k n) -> p k n", k=KT)
        g1row, perow, barow = sm(640, P, KT), sm(768, P, 64), sm(896, P, GH)
        gA = sm(0, TT * 512).rearrange("p (a h t) -> p a h t", a=TT, h=GH)
        gAoff = sm(1024, 512).rearrange("p (h t) -> p h t", h=GH)
        ng = sm(1536, 48).rearrange("p (a n) -> p a n", a=TT)
        stack = sm(1584, 32)
        smT = sm(1616, 256, 40)
        wa = sm(1872, 512, 16)
        junk256 = sm(1872, 256)
        causal = sm(2384, P)
        cadd = sm(2512, 30).rearrange("p (a n) -> p a n", a=TT)
        cmul = sm(2542, 30).rearrange("p (a n) -> p a n", a=TT)
        cols3 = sm(2572, 84)
        g1T, peT, baT = cols3[:, 0:KT], cols3[:, KT:KT + 64], cols3[:, KT + 64:KT + 64 + GH]
        w2 = sm(2656, 256).rearrange("p (c n) -> p c n", c=2)
        gng = sm(2912, 256)
        hidT = sm(3168, 60).rearrange("p (c n) -> p c n", c=2)
        kcT = sm(3228, 30)
        vc = sm(3258, 256, NCMP).rearrange("p (g n) -> p g n", g=KVH)
        ssx, rx = sm(3514, 4), sm(3518, 4)
        ssg, rg = sm(3522, 8), sm(3530, 8)
        mx = [sm(3540 + 4 * i, 4) for i in range(2)]
        nb = [sm(3548 + 4 * i, 4) for i in range(2)]
        su = [sm(3556 + 4 * i, 4) for i in range(2)]
        rr = [sm(3564 + 4 * i, 4) for i in range(2)]
        oraw = sm(3584, 2048).rearrange("p (i n) -> p i n", i=2 * GH)
        ss2, r2 = sm(5824, 4), sm(5828, 4)
        npass_f = sm(5832, 4)
        npass_i = npass_f[:, 0:1].bitcast(I32)
        xgT = sm(0, 2048).rearrange("p (k s) -> p k s", k=KT)
        osb = sm(2048, 2048)
        gusb = sm(4096, 512)
        hmid = sm(4608, 256).rearrange("p (j s) -> p j s", j=FT)
        Sb = sm(4864, 256).rearrange("p (a s) -> p a s", a=TT)
        Gb = sm(5120, 256).rearrange("p (a s) -> p a s", a=TT)
        STb = sm(5376, 256)
        iota = sm(5632, SLOTS)
        posm = sm(5696, 64).rearrange("p (a e) -> p a e", a=TT)
        wgt = sm(5760, 64).rearrange("p (a e) -> p a e", a=TT)
        g2b = ar(FM0, D)
        squares, ss2p = sm(5068, CW), sm(5456, TT * N_CG).rearrange("p (a g) -> p a g", a=TT)
        h2T = sm(0, KT * T).rearrange("p (k t) -> p k t", k=KT)
        rw = sm(4096, KT * 36).rearrange("p (k n) -> p k n", k=KT)
        tri, ones = sm(4672, P), sm(4800, P)
        rbb = sm(4928, 36)
        jm = sm(4964, NE)
        lg = sm(4996, 72).rearrange("p (a n) -> p a n", a=TT)
        em = sm(5068, 64).rearrange("p (a n) -> p a n", a=TT)
        oh1 = sm(5132, 64).rearrange("p (a n) -> p a n", a=TT)
        t64 = sm(5196, 64).rearrange("p (a n) -> p a n", a=TT)
        oh2 = sm(5260, 64).rearrange("p (a n) -> p a n", a=TT)
        goh = sm(5324, 8).rearrange("p (a n) -> p a n", a=TT)
        t8 = sm(5332, 8).rearrange("p (a n) -> p a n", a=TT)
        rs = sm(5340, 40).rearrange("p (i a) -> p i a", a=TT)
        M = sm(5380, 64).rearrange("p (a n) -> p a n", a=TT)
        UN = KT * W
        unit_g = [ar(u * UN, UN // 2).rearrange("p (j f) -> p j f", j=8) for u in range(4)]
        unit_u = [ar(u * UN + UN // 2, UN // 2).rearrange("p (j f) -> p j f", j=8) for u in range(4)]
        wd = ar(4 * UN, UN).rearrange("p (j n) -> p j n", j=FT)
        wd_last = ar(2 * UN, UN).rearrange("p (j n) -> p j n", j=FT)
        gfb = ar(3 * UN, D)
        ssfp = sm(0, TT * 4).rearrange("p (a c) -> p a c", a=TT)

        s_x = [sem(f"s_x{t}") for t in range(TT)]
        s_rows, s_wsm, s_const = sem("s_rows"), sem("s_wsm"), sem("s_const")
        s_ident, s_masks = sem("s_ident"), sem("s_masks")
        s_ssx, s_ms, s_sq = sem("s_ssx"), sem("s_ms"), sem("s_sq")
        s_dve, s_act, s_pl, s_tmp = sem("s_dve"), sem("s_act"), sem("s_pl"), sem("s_tmp")
        s_xn, s_rowT, s_rowC = sem("s_xn"), sem("s_rowT"), sem("s_rowC")
        s_xT, s_hhi, s_hlo = sem("s_xT"), sem("s_hhi"), sem("s_hlo")
        s_wsh, s_wsl = sem("s_wsh"), sem("s_wsl")
        s_smp, s_sma, s_gaT, s_gaTc, s_z = sem("s_smp"), sem("s_sma"), sem("s_gaT"), sem("s_gaTc"), sem("s_z")
        s_y, s_e, s_ln = sem("s_y"), sem("s_e"), sem("s_ln")
        s_raw = [sem(f"s_raw{i}") for i in range(3)]
        s_hi, s_lo, s_use, s_cmpu = sem("s_hi"), sem("s_lo"), sem("s_use"), sem("s_cmpu")
        s_ev = sem("s_ev")
        s_gD, s_gE, s_gG, s_lv, s_gA = sem("s_gD"), sem("s_gE"), sem("s_gG"), sem("s_lv"), sem("s_gA")
        s_S, s_nb, s_exp, s_P, s_T, s_PT, s_V, s_O = (
            sem(n) for n in ("s_S", "s_nb", "s_exp", "s_P", "s_T", "s_PT", "s_V", "s_O"))
        s_flat, s_hid4, s_cmps, s_hid, s_cmp2, s_kvc = (
            sem(n) for n in ("s_flat", "s_hid4", "s_cmps", "s_hid", "s_cmp2", "s_kvc"))
        s_gpv, s_gsq, s_gcp, s_gms, s_grt, s_on, s_gtr, s_ogT = (
            sem(n) for n in ("s_gpv", "s_gsq", "s_gcp", "s_gms", "s_grt", "s_on", "s_gtr", "s_ogT"))
        s_ohi, s_olo = sem("s_ohi"), sem("s_olo")
        s_sig, s_mrg, s_mhi, s_mlo = sem("s_sig"), sem("s_mrg"), sem("s_mhi"), sem("s_mlo")
        s_xr, s_x2 = sem("s_xr"), sem("s_x2")
        s_g2, s_rw = sem("s_g2"), sem("s_rw")
        s_ss2, s_ms2, s_sq2, s_h2 = sem("s_ss2"), sem("s_ms2"), sem("s_sq2"), sem("s_h2")
        s_hg, s_ss2p, s_ssfp, s_r2 = sem("s_hg"), sem("s_ss2p"), sem("s_ssfp"), sem("s_r2")
        s_h2t, s_h2A, s_lgt, s_rc = sem("s_h2t"), sem("s_h2A"), sem("s_lgt"), sem("s_rc")
        s_re, s_rex, s_M, s_pos, s_route = sem("s_re"), sem("s_rex"), sem("s_M"), sem("s_pos"), sem("s_route")
        s_u = [sem(f"s_u{u}") for u in range(4)]
        s_wd = [sem(f"s_wd{par}") for par in range(2)]
        s_gu0, s_gu, s_gus, s_xg, s_xgA, s_xgD = (
            sem(n) for n in ("s_gu0", "s_gu", "s_gus", "s_xg", "s_xgA", "s_xgD"))
        s_G, s_Sm, s_tr, s_silu, s_mid, s_ST, s_STc = (
            sem(n) for n in ("s_G", "s_Sm", "s_tr", "s_silu", "s_mid", "s_ST", "s_STc"))
        s_dn, s_osb, s_sc, s_add = sem("s_dn"), sem("s_osb"), sem("s_sc"), sem("s_add")
        s_gf, s_ssf, s_msf, s_sqf, s_y1, s_out = (
            sem(n) for n in ("s_gf", "s_ssf", "s_msf", "s_sqf", "s_y1", "s_out"))

        x_v = x.rearrange("b (a p) d -> (b a) p d", p=P)
        out_v = out.rearrange("b (a p) d -> (b a) p d", p=P)
        win_v = w_in[0].rearrange("(k p) n -> p k n", p=P)
        wout_v = w_out[0].rearrange("(k p) n -> p k n", p=P)
        br_v = [w[0].rearrange("(k p) n -> p k n", p=P) for w in (w_br_moba, w_br_nsa, w_br_gla)]
        cmpw1_v = cmp_w1[0].rearrange("c (l d) o -> c d l o", d=HD)
        gate_v = e_gate.rearrange("a e (p j) f -> (a e) p j f", j=KT)
        up_v = e_up.rearrange("a e (p j) f -> (a e) p j f", j=KT)
        down_v = e_down.rearrange("a e (p j) n -> (a e) p j n", j=FT)

        def slot_of(u):
            return u % 3

        block = ctx.enter_context(nc.Block())

        @block.sync
        def _(sp):
            for t in range(TT):
                sp.dma_start(xs[:, t, :], x_v[t]).then_inc(s_x[t], 16)
            sp.dma_start(g1row, norm1_g[0].rearrange("(k p) -> k p", p=P)).then_inc(s_rows, 16)
            sp.dma_start(perow, cmp_pe[0].rearrange("c l d -> (c l) d")).then_inc(s_rows, 16)
            sp.dma_start(barow, gla_ba[0].rearrange("(h p) -> h p", p=P)).then_inc(s_rows, 16)
            sp.dma_start(wsm[:, :, 0:16], win_v[:, :, C_GA:C_GA + 16]).then_inc(s_wsm, 16)
            sp.dma_start(wsm[:, :, 16:40], win_v[:, :, C_NG:C_NG + 24]).then_inc(s_wsm, 16)

            def load_unit(slot, src):
                sp.dma_start(raw[:, slot], src).then_inc(s_raw[slot], 16)

            def win_unit(col, half):
                return win_v[:, UK * half:UK * half + UK, col]

            for u in range(U_CMP + 1):
                g, half = u // 2, u % 2
                col = (FM_COLS + TM_COLS)[g]
                if u >= 3:
                    sp.wait_ge(s_lo, u - 2)
                load_unit(u % 3, win_unit(slice(col, col + CW), half))
                if u == 2:
                    sp.dma_start(wa, gla_wa[0]).then_inc(s_const, 16)
                    sp.dma_start(w2, cmp_w2[0].rearrange("c d o -> d c o")).then_inc(s_const, 16)
                    sp.dma_start(gng, gla_norm_g[0].partition_broadcast(P)).then_inc(s_const, 16)
            for i in range(N_CMPU):
                p = U_CMP + 1 + 2 * i
                if i == 0:
                    sp.wait_ge(s_lo, U_CMP - 1)
                else:
                    sp.wait_ge(s_lo, U_CMP + i)
                sp.dma_start(raw_cmp[:, p % 3], cmpw1_v[i // 2][:, 16 * (i % 2):16 * (i % 2) + 16]
                             ).then_inc(s_raw[p % 3], 16)
                u = U_CMP + 1 + i
                col = (FM_COLS + TM_COLS)[u // 2]
                if i == 0:
                    sp.wait_ge(s_lo, U_CMP)
                else:
                    sp.wait_ge(s_cmpu, i)
                load_unit((p + 1) % 3, win_unit(slice(col, col + CW), u % 2))
            for u in range(U_CMP + 1 + N_CMPU, U_MG):
                col = (FM_COLS + TM_COLS)[u // 2]
                if u == U_CMP + 2 + N_CMPU:
                    sp.wait_ge(s_cmpu, N_CMPU)
                else:
                    sp.wait_ge(s_lo, u - 2 if u > U_CMP + 2 + N_CMPU else u - 1)
                load_unit(load_of(u) % 3, win_unit(slice(col, col + CW), u % 2))

            for bi, branch in enumerate(BRANCH_ORDER):
                with sp.Fori(1, N_CG + 1) as m1:
                    for i in range(3):
                        sp.wait_ge(s_lo, m1 * 3 + (U_MG + 3 * N_CG * bi + i - 5))
                        if i < 2:
                            load_unit((U_MG + N_CMPU + i) % 3,
                                      win_unit(bass.ds(m1 * CW + (C_MG + branch * D - CW), CW), i))
                        else:
                            load_unit((U_MG + N_CMPU + i) % 3, br_v[branch][:, :, bass.ds(m1 * CW - CW, CW)])

            for i in range(2 * N_CG):
                u = U_WO + i
                sp.wait_ge(s_lo, u - 2)
                load_unit(load_of(u) % 3, wout_v[:, UK * (i % 2):UK * (i % 2) + UK, i // 2 * CW:i // 2 * CW + CW])
                if i == 2:
                    sp.wait_ge(s_use, U_WO)
                    for t in range(TT):
                        sp.dma_start(xs[:, t, :], x_v[t]).then_inc(s_xr, 16)
                if i == 3:
                    sp.dma_start(g2b, norm2_g[0].partition_broadcast(P)).then_inc(s_g2, 16)
                if i == 4:
                    sp.dma_start(rw[:, :, 0:GROUPS], rg_w[0].rearrange("(k p) n -> p k n", p=P)).then_inc(s_rw, 16)
                    sp.dma_start(rw[:, :, GROUPS:36], re_w[0].rearrange("(k p) n -> p k n", p=P)).then_inc(s_rw, 16)
                    sp.dma_start(rbb[:, 0:GROUPS], rg_b[0].partition_broadcast(P)).then_inc(s_rw, 16)
                    sp.dma_start(rbb[:, GROUPS:36], re_b[0].partition_broadcast(P)).then_inc(s_rw, 16)

            def load_gate(u, e, h):
                sp.dma_start(unit_g[u], gate_v[bass.ds(e, 1), :, 8 * h:8 * h + 8].rearrange(
                    "e p j f -> (e p) j f")).then_inc(s_u[u], 16)

            def load_up(u, e, h):
                sp.dma_start(unit_u[u], up_v[bass.ds(e, 1), :, 8 * h:8 * h + 8].rearrange(
                    "e p j f -> (e p) j f")).then_inc(s_u[u], 16)

            def load_gu(u, e, h):
                load_gate(u, e, h)
                load_up(u, e, h)

            def load_down(e, par, to):
                for h in range(2):
                    sp.dma_start(to[:, 2 * h:2 * h + 2], down_v[bass.ds(e, 1), :, 2 * h:2 * h + 2].rearrange(
                        "e p j n -> (e p) j n")).then_inc(s_wd[par], 16)

            load_down(0, 0, wd)
            load_up(2, 0, 0)
            sp.wait_ge(s_lo, U_END)
            load_up(1, 1, 1)
            sp.wait_ge(s_use, U_END)
            load_gu(3, 0, 1)
            sp.wait_ge(s_hg, N_CG)
            load_gate(2, 0, 0)
            load_gu(0, 1, 0)
            load_gate(1, 1, 1)
            sp.wait_ge(s_route, 1)
            npass = sp.value_load(npass_i[0:1, 0:1], min_val=1, max_val=T // SLOTS)

            def rest_of(n, e0):
                for q in range(2):
                    for h in range(2):
                        sp.wait_ge(s_gu0 if h == 0 else s_gu, n + q + 1)
                        load_gu((2, 0)[q] + h, e0 + 2 + q, h)
                    sp.wait_ge(s_dn, n + q + 1)
                    load_down(e0 + 1 + q, 1 - q, wd)

            with sp.Fori(0, NE // 2 - 1) as i:
                rest_of(2 * i, 2 * i)
            sp.wait_ge(s_gu, NE - 1)
            load_down(NE - 1, 1, wd_last)
            with sp.If(npass > 1):
                with sp.Fori(1, npass) as q:
                    base = q * NE
                    sp.wait_ge(s_gu, base - 1)
                    load_gu(3, 0, 1)
                    sp.wait_ge(s_dn, base - 1)
                    load_down(0, 0, wd)
                    for h in range(2):
                        sp.wait_ge(s_gu, base)
                        load_gu(h, 1, h)
                    sp.wait_ge(s_dn, base)
                    load_gu(2, 0, 0)
                    with sp.Fori(0, NE // 2 - 1) as i:
                        rest_of(base + 2 * i, 2 * i)
                    sp.wait_ge(s_gu, base + (NE - 1))
                    load_down(NE - 1, 1, wd_last)

            sp.wait_ge(s_gu, npass * NE)
            sp.dma_start(gfb, final_g.partition_broadcast(P)).then_inc(s_gf, 16)
            for t in range(TT):
                for h in range(2):
                    sp.wait_ge(s_y1, 2 * t + h + 1)
                    sp.dma_start(out_v[t][:, h * (D // 2):(h + 1) * (D // 2)],
                                 h2[:, t, h * (D // 2):(h + 1) * (D // 2)]).then_inc(s_out, 16)
            sp.wait_ge(s_out, 32 * TT)

        @block.gpsimd
        def _(pool):
            done = [0]

            def link(ins):
                done[0] += 1
                ins.then_inc(s_pl, 1)
                pool.wait_ge(s_pl, done[0])

            link(nc.gpsimd.memset(ident, 0.0))
            nc.gpsimd.affine_select(out=ident, in_=ident, compare_op=ALU.not_equal, fill=1.0,
                                    base=0, pattern=[[-1, P]], channel_multiplier=1).then_inc(s_ident, 1)
            link(nc.gpsimd.memset(causal, 0.0))
            nc.gpsimd.affine_select(out=causal, in_=causal, compare_op=ALU.is_ge, fill=NEG, base=0,
                                    pattern=[[-1, P]], channel_multiplier=1).then_inc(s_masks, 1)
            link(nc.gpsimd.memset(cadd, 0.0))
            link(nc.gpsimd.memset(cmul, 1.0))
            for t in range(TT):
                for m, fill in ((cadd, NEG), (cmul, 0.0)):
                    nc.gpsimd.affine_select(out=m[:, t], in_=m[:, t], compare_op=ALU.is_ge, fill=fill,
                                            base=t * P - CMP_LEN + 1, pattern=[[-CMP_STRIDE, NCMP]],
                                            channel_multiplier=1).then_inc(s_masks, 1)
            link(nc.gpsimd.memset(lmask, 0.0))
            for lv in range(LEVELS - 1):
                H = 1 << lv
                v = lmask[:, lv].rearrange("p (n two r) -> p n two r", two=2, r=H)[:, :, 1, :]
                link(nc.gpsimd.memset(v, 1.0))
                link(nc.gpsimd.affine_select(out=v, in_=v, compare_op=ALU.is_ge, fill=0.0, base=0,
                                             pattern=[[-2 * H, P // (2 * H)], [0, H]], channel_multiplier=1))
                nc.gpsimd.affine_select(out=v, in_=v, compare_op=ALU.is_ge, fill=0.0, base=H - 1,
                                        pattern=[[2 * H, P // (2 * H)], [0, H]],
                                        channel_multiplier=-1).then_inc(s_masks, 1)
            pool.wait_ge(s_use, U_WO)
            nc.gpsimd.iota(jm, pattern=[[1, NE]], base=-64, channel_multiplier=0,
                           allow_small_or_imprecise_dtypes=True).then_inc(s_rc, 1)
            nc.gpsimd.iota(iota, pattern=[[1, SLOTS]], base=0,
                           channel_multiplier=0, allow_small_or_imprecise_dtypes=True).then_inc(s_rc, 1)
            nc.gpsimd.memset(ones, 1.0).then_inc(s_rc, 1)
            link(nc.gpsimd.memset(tri, 1.0))
            nc.gpsimd.affine_select(out=tri, in_=tri, compare_op=ALU.is_gt, fill=0.0, base=0,
                                    pattern=[[1, P]], channel_multiplier=-1).then_inc(s_rc, 1)

        N_MASKS = 1 + 2 * TT + LEVELS - 1

        @block.tensor
        def _(pe):
            mm = nc.tensor.matmul

            pe.wait_ge(s_ident, 1)
            pe.wait_ge(s_rows, 48)
            nc.tensor.transpose(ps[:, 3, 0:KT], g1row, ident[0:KT, 0:KT])
            nc.tensor.transpose(ps[:, 3, 16:80], perow, ident[0:64, 0:64])
            nc.tensor.transpose(ps[:, 3, 80:84], barow, ident[0:GH, 0:GH]).then_inc(s_rowT, 1)
            pe.wait_ge(s_xn, TT)
            for i in range(KT // 2):
                if i >= 4:
                    pe.wait_ge(s_hlo, i - 3)
                for k in (2 * i, 2 * i + 1):
                    for t in range(TT):
                        last = nc.tensor.transpose(ps[:, 4 + i % 4, (k % 2) * T + t * P:(k % 2) * T + t * P + P],
                                                   xn[:, t, k * P:k * P + P], ident)
                last.then_inc(s_xT, 1)
            pe.wait_ge(s_hlo, KT // 2)

            def mm3(o, ah, al, bh, bl, start, stop):
                mm(o, ah, bh, start=start, stop=False)
                mm(o, ah, bl, start=False, stop=False)
                return mm(o, al, bh, start=False, stop=stop)

            pe.wait_ge(s_wsl, 1)
            for k in range(KT):
                last = mm3(ps[0:40, 3, 0:T], wsm_hi[:, k], wsm_lo[:, k], hThi[:, k], hTlo[:, k], k == 0, k == KT - 1)
            last.then_inc(s_smp, 1)

            def fm_unit(slot, bank, half, ah=None, al=None, whole=False):
                ah = hThi if ah is None else ah
                al = hTlo if al is None else al
                for b in range(2):
                    for k in range(UK):
                        kk = UK * half + k
                        o = ps[:, bank, b * T:b * T + T]
                        q = slice(b * P, b * P + P)
                        last = mm3(o, whi[:, slot, k, q], wlo[:, slot, k, q], ah[:, kk], al[:, kk],
                                   b == 0 and k == 0 and half == 0,
                                   b == 1 and k == UK - 1 and (half == 1 or whole))
                return last.then_inc(s_use, 1)

            def tm_unit(slot, bank, half, ah, al):
                for t in range(TT):
                    for k in range(UK):
                        kk = UK * half + k
                        q = slice(t * P, t * P + P)
                        last = mm3(ps[:, bank, t * CW:t * CW + CW], ah[:, kk, q], al[:, kk, q],
                                   whi[:, slot, k], wlo[:, slot, k],
                                   t == 0 and k == 0 and half == 0, t == 1 and k == UK - 1 and half == 1)
                return last.then_inc(s_use, 1)

            def fm_group_half(g, gi, half):
                pe.wait_ge(s_lo, g * 2 + (half + 1))
                if half == 0 and not (isinstance(g, int) and g < 3):
                    pe.wait_ge(s_ev, g - 2)
                fm_unit((2 * gi + half) % 3, gi % 3, half)

            for g in range(3):
                for half in range(2):
                    fm_group_half(g, g, half)
            with pe.Fori(1, G_LOOP // 3) as j:
                for gi in range(3):
                    for half in range(2):
                        fm_group_half(j * 3 + gi, gi, half)

            def scores(u):
                kind, h = unit_of(u)
                g = h // (NH // KVH)
                q = fm[:, (B_MQ if kind == "moba" else B_NQ) + h]
                k = fm[:, {"moba": B_MK + h, "slc": B_KSLC + g, "win": B_KWIN + g}[kind]]
                if u >= 1:
                    pe.wait_ge(s_exp, u)
                if u == 0:
                    pe.wait_ge(s_ev, N_FM)
                mm(ps[:, 6, 0:P], q[:, 0:P], k[:, 0:P], start=True, stop=False)
                mm(ps[:, 6, 0:P], ident, causal, start=False, stop=True)
                mm(ps[:, 6, P:3 * P], q[:, P:T], k, start=True, stop=False)
                last = mm(ps[:, 6, 2 * P:3 * P], ident, causal, start=False, stop=True)
                if kind == "slc":
                    pe.wait_ge(s_kvc, 1)
                    for t in range(TT):
                        o = ps[:, 6, 384 + 16 * t:384 + 16 * t + NCMP]
                        mm(o, q[:, t * P:t * P + P], kcT[:, g * NCMP:(g + 1) * NCMP], start=True, stop=False)
                        last = mm(o, ident, cadd[:, t], start=False, stop=True)
                last.then_inc(s_S, 1)

            def turn(u):
                kind, h = unit_of(u)
                pe.wait_ge(s_P, u + 1)
                for b in range(3):
                    last = nc.tensor.transpose(ps[:, 7, b * P:b * P + P], aP[u % 2][:, b * P:b * P + P], ident)
                if kind == "slc":
                    for t in range(TT):
                        last = nc.tensor.transpose(ps[0:NCMP, 5, t * P:t * P + P], cP[h % 2][:, t], ident)
                last.then_inc(s_T, 1)

            def values(u):
                kind, h = unit_of(u)
                g = h // (NH // KVH)
                o = ps[:, 4, (h % 2) * T:(h % 2) * T + T]
                pe.wait_ge(s_PT, u + 1)
                if kind != "win":
                    hh = h if kind == "moba" else MH + h
                    if hh >= 1:
                        pe.wait_ge(s_O, hh)
                    if hh == 0:
                        pe.wait_ge(s_gA, 9)
                if kind == "moba":
                    v = mv[:, :, h * HD:h * HD + HD]
                    if h == 0:
                        pe.wait_ge(s_ev, N_FM + 4)
                elif kind == "slc":
                    v = kv35[:, :, g * HD:g * HD + HD]
                    mm(o, vc[:, g], cPT[h % 2], start=True, stop=False)
                    if h == 0:
                        pe.wait_ge(s_ev, N_FM + TM_VW + 1)
                else:
                    v = kv35[:, :, CW + g * HD:CW + g * HD + HD]
                pt = aPT[u % 2]
                mm(o, v[:, 0], pt[:, 0:T], start=kind == "moba", stop=False)
                last = mm(o[:, P:T], v[:, 1], pt[:, T:T + P], start=False, stop=kind != "slc")
                last.then_inc(s_V, 1)

            def gla_values(h):
                if h == 0:
                    pe.wait_ge(s_gA, 9)
                    pe.wait_ge(s_ev, N_FM + 8)
                else:
                    pe.wait_ge(s_gcp, h)
                vh = gv[:, :, h * GDV:(h + 1) * GDV]
                mm(ps[:, 5, 0:GDV], gA[:, 0, h], vh[:, 0], start=True, stop=True)
                mm(ps[:, 5, GDV:2 * GDV], gAoff[:, h], vh[:, 0], start=True, stop=False)
                mm(ps[:, 5, GDV:2 * GDV], gA[:, 1, h], vh[:, 1], start=False, stop=True).then_inc(s_gpv, 1)

            def level(lv):
                pe.wait_ge(s_gG, lv + 1)
                pe.wait_ge(s_gA, lv + 1)
                g = gG[lv % 2].rearrange("p (h t) -> p h t", h=GH)
                if lv < LEVELS - 1:
                    for t in range(TT):
                        for h in range(GH):
                            last = mm(ps[:, 4 + t, h * P:h * P + P], g[:, h, t * P:t * P + P],
                                      g[:, h, t * P:t * P + P], start=True, stop=True)
                else:
                    for h in range(GH):
                        last = mm(ps[:, 4, h * P:h * P + P], g[:, h, 0:P], g[:, h, P:T], start=True, stop=True)
                last.then_inc(s_lv, 1)

            def mg_unit(u, slot, s, part, oh, ol):
                pe.wait_ge(s_lo, u + 1)
                if part < 2:
                    fm_unit(slot, 2 * s, part)
                else:
                    v8 = "p (b t) -> p b t"
                    fm_unit(slot, 2 * s + 1, 0, oh[:, :].rearrange(v8, t=T), ol[:, :].rearrange(v8, t=T), whole=True)

            for step in SCHED:
                if step[0] == "fm":
                    fm_group_half(step[1], step[1], step[2])
                elif step[0] == "gat":
                    pe.wait_ge(s_sma, 1)
                    for t in range(TT):
                        last = nc.tensor.transpose(ps[:, 3, 40 * t:40 * t + 40], smT[:, t * P:t * P + P],
                                                   ident[0:40, 0:40])
                    last.then_inc(s_gaT, 1)
                elif step[0] == "z":
                    pe.wait_ge(s_const, 48)
                    pe.wait_ge(s_gaTc, 1)
                    for h in range(GH):
                        last = mm(ps[:, 6 + h // 2, (h % 2) * T:(h % 2) * T + T], wa[:, h * P:h * P + P], smT[0:16],
                                  start=True, stop=True)
                    last.then_inc(s_z, 1)
                elif step[0] == "diag":
                    for t in range(TT):
                        for h in range(GH):
                            last = mm(ps[:, 4 + t, h * P:h * P + P], fm[:, B_GK + h, t * P:t * P + P],
                                      fm[:, B_GQ + h, t * P:t * P + P], start=True, stop=True)
                    last.then_inc(s_lv, 1)
                elif step[0] == "level":
                    level(step[1])
                elif step[0] == "tm":
                    _, g, half = step
                    G = N_FM + g
                    pe.wait_ge(s_lo, 2 * G + half + 1)
                    if half == 0:
                        pe.wait_ge(s_ev, G - 2)
                    tm_unit((2 * G + half) % 3, G % 3, half, hThi, hTlo)
                elif step[0] == "cmp1":
                    i = step[1]
                    r = U_CMP + 1 + 2 * i
                    if i == 0:
                        pe.wait_ge(s_flat, 1)
                        pe.wait_ge(s_gaTc, 1)
                    pe.wait_ge(s_raw[r % 3], 16 * (r // 3 + 1))
                    c = i // 2
                    for l in range(16):
                        j = l % 4
                        last = mm(ps[32 * j:32 * j + 32, 3, P * c:P * c + P], flat[:, c, 16 * (i % 2) + l],
                                  raw_cmp[:, r % 3, l], start=i % 2 == 0 and l < 4, stop=i % 2 == 1 and l >= 12)
                    last.then_inc(s_cmpu, 1)
                elif step[0] == "cmp2":
                    pe.wait_ge(s_hid4, 1)
                    for c in range(2):
                        last = mm(ps[:, 3, 256 + 32 * c:256 + 32 * c + 32], hid4[:, P * c:P * c + P], stack,
                                  start=True, stop=True)
                    last.then_inc(s_cmps, 1)
                elif step[0] == "cmp3":
                    pe.wait_ge(s_hid, 1)
                    mm(ps[:, 3, 0:30], w2[:, 0], hidT[:, 0], start=True, stop=True)
                    for g in range(KVH):
                        last = mm(ps[0:NCMP, 3, 64 + P * g:64 + P * g + P], hidT[:, 1, g * NCMP:(g + 1) * NCMP],
                                  w2[:, 1], start=True, stop=True)
                    last.then_inc(s_cmp2, 1)
                elif step[0] == "S":
                    scores(step[1])
                elif step[0] == "T":
                    turn(step[1])
                elif step[0] == "V":
                    values(step[1])
                elif step[0] == "gpv":
                    gla_values(step[1])
                elif step[0] == "gtr":
                    h = step[1]
                    pe.wait_ge(s_on, GH)
                    if h >= 1:
                        pe.wait_ge(s_ogT, h)
                    for eh in range(2):
                        for t in range(TT):
                            last = nc.tensor.transpose(ps[:, 5, eh * T + t * P:eh * T + t * P + P],
                                                       oraw[:, 2 * h + t, eh * P:eh * P + P], ident)
                    last.then_inc(s_gtr, 1)
                elif step[0] == "mg":
                    _, m, part = step
                    if part == 0:
                        if m < 2:
                            pe.wait_ge(s_ev, N_GROUP)
                            pe.wait_ge(s_kvc, 1)
                        else:
                            pe.wait_ge(s_mrg, m - 1)
                    if part == 2 and m == 0:
                        pe.wait_ge(s_olo, 1)
                    mg_unit(U_MG + 3 * m + part, slot_of(U_MG + part), m % 2, part, ohi[0], olo[0])

            for bi in (1, 2):
                def gate_step(m, s):
                    pe.wait_ge(s_mrg, m - 1)
                    for part in range(3):
                        mg_unit(m * 3 + (U_MG + part), slot_of(U_MG + part), s, part, ohi[bi], olo[bi])

                pe.wait_ge(s_olo, bi + 1)
                with pe.Fori(bi * (N_CG // 2), (bi + 1) * (N_CG // 2)) as j:
                    for s in range(2):
                        gate_step(j * 2 + s, s)

            mh = merged_hi[:, :].rearrange("p (k t) -> p k t", k=KT)
            ml = merged_lo[:, :].rearrange("p (k t) -> p k t", k=KT)
            pe.wait_ge(s_mlo, N_CG)
            pe.wait_ge(s_mrg, 3 * N_CG)

            def turn_x2(g):
                pe.wait_ge(s_hg, g + 1)
                if g >= 2:
                    pe.wait_ge(s_h2A, g - 1)
                for k in (2 * g, 2 * g + 1):
                    for t in range(TT):
                        last = nc.tensor.transpose(ps[:, 4 + g % 2, (k % 2) * T + t * P:(k % 2) * T + t * P + P],
                                                   h2[:, t, k * P:k * P + P], ident)
                last.then_inc(s_h2t, 1)

            def logits(g):
                if g == 0:
                    pe.wait_ge(s_rw, 64)
                pe.wait_ge(s_h2A, g + 1)
                for t in range(TT):
                    for k in (2 * g, 2 * g + 1):
                        last = mm(ps[:, 6 + t, 0:36], h2T[:, k, t * P:t * P + P], rw[:, k, :],
                                  start=k == 0, stop=k == KT - 1)
                if g == N_CG - 1:
                    last.then_inc(s_lgt, 1)

            for g in range(N_CG):
                for half in range(2):
                    pe.wait_ge(s_lo, U_WO + 2 * g + half + 1)
                    if half == 0 and g >= 3:
                        pe.wait_ge(s_x2, g - 2)
                    tm_unit(slot_of(U_WO + 2 * g + half), g % 3, half, mh, ml)
                    if half == 0 and g >= 1:
                        turn_x2(g - 1)
                    if half == 0 and g >= 2:
                        logits(g - 2)
            logits(N_CG - 2)
            turn_x2(N_CG - 1)
            logits(N_CG - 1)
            pe.wait_ge(s_rc, 4)
            pe.wait_ge(s_M, 1)
            mm(ps[:, 1, 0:NE], tri, M[:, 0], start=True, stop=True)
            mm(ps[:, 1, NE:2 * NE], ones, M[:, 0], start=True, stop=False)
            mm(ps[:, 1, NE:2 * NE], tri, M[:, 1], start=False, stop=True)
            mm(ps[:, 1, 2 * NE:3 * NE], ones, M[:, 0], start=True, stop=False)
            mm(ps[:, 1, 2 * NE:3 * NE], ones, M[:, 1], start=False, stop=True).then_inc(s_pos, 1)
            pe.wait_ge(s_h2, TT)
            pe.wait_ge(s_route, 1)
            npass = pe.value_load(npass_i[0:1, 0:1], min_val=1, max_val=T // SLOTS)

            def gather(m, half):
                for k in range(8 * half, 8 * half + 8):
                    o = ps[:, 2 + k // 4, (k % 4) * P:(k % 4 + 1) * P]
                    for t in range(TT):
                        last = mm(o, h2[:, t, :].rearrange("p (c k) -> p k c", k=KT)[:, k], Gb[:, t],
                                  start=t == 0, stop=t == TT - 1)
                last.then_inc(s_xg, 1)

            def scatter(m, t):
                if t == 0:
                    pe.wait_ge(s_osb, m * 2 + 2)
                for c in range(4):
                    if t == 1:
                        pe.wait_ge(s_add, m * 8 + (c + 9))
                    mm(ps[:, 2 + c, :], STb[:, t * P:t * P + P], osb[:, c * W:c * W + W],
                       start=True, stop=True).then_inc(s_sc, 1)

            def gate_up(n, par, uses, m):
                for h in range(2):
                    u = (2, 0)[par] + h
                    pe.wait_ge(s_u[u], uses * 32 + 32)
                    if h == 0 and par == 0:
                        pe.wait_ge(s_xgA, m + 1)
                        pe.wait_ge(s_xgD, m + 1)
                        pe.wait_ge(s_STc, m + 1)
                    for j in range(8):
                        k = 8 * h + j
                        xk = xgT[:, k, par * SLOTS:par * SLOTS + SLOTS]
                        mm(ps[0:SLOTS, 0, :], xk, unit_g[u][:, j], start=k == 0, stop=k == KT - 1)
                        a = mm(ps[SLOTS:P, 0, :], xk, unit_u[u][:, j], start=k == 0, stop=k == KT - 1)
                    a.then_inc(s_gu0 if h == 0 else s_gu, 1)

            def turn_gate_up(n):
                pe.wait_ge(s_gus, n + 1)
                for j in range(FT):
                    a = nc.tensor.transpose(ps[:, 1, j * P:j * P + P],
                                            gusb.rearrange("p (c j) -> p j c", j=FT)[:, j], ident)
                a.then_inc(s_tr, 1)

            def down(n, m, par, w):
                pe.wait_ge(s_mid, n + 1)
                pe.wait_ge(s_wd[par], m * 32 + 32)
                for c in range(2):
                    for j in range(FT):
                        mm(ps[0:SLOTS, 6 + c, :], hmid[:, j], w[:, j, c * W:c * W + W],
                           start=j == 0, stop=j == FT - 1)
                        a = mm(ps[SLOTS:P, 6 + c, :], hmid[:, j], w[:, j, 1024 + c * W:1024 + c * W + W],
                               start=j == 0, stop=j == FT - 1)
                a.then_inc(s_dn, 1)

            def pair(m, uses, first, last_of_pass):
                n = m * 2
                gate_up(n, 0, uses, m)
                if not first:
                    scatter(m - 1, 0)
                turn_gate_up(n)
                if not first:
                    scatter(m - 1, 1)
                down(n, m, 0, wd)
                gate_up(n + 1, 1, uses, m)
                if not last_of_pass:
                    pe.wait_ge(s_G, m + 2)
                    pe.wait_ge(s_add, m * 8 + 8)
                    gather(m + 1, 0)
                turn_gate_up(n + 1)
                if not last_of_pass:
                    gather(m + 1, 1)
                pe.wait_ge(s_Sm, m + 1)
                for t in range(TT):
                    a = nc.tensor.transpose(ps[:, 0, t * P:t * P + P], Sb[:, t], ident)
                a.then_inc(s_ST, 1)
                pe.wait_ge(s_osb, n + 1)
                down(n + 1, m, 1, wd_last if last_of_pass else wd)

            with pe.Fori(0, npass) as q:
                base = q * NPAIR
                pe.wait_ge(s_G, base + 1)
                pe.wait_ge(s_add, q * (8 * NPAIR) + 8)
                for half in range(2):
                    gather(base, half)
                pair(base, q * NPAIR, True, False)
                with pe.Fori(1, NPAIR - 1) as i:
                    pair(base + i, q * NPAIR + i, False, False)
                pair(base + (NPAIR - 1), q * NPAIR + (NPAIR - 1), False, True)
                for t in range(TT):
                    scatter(base + (NPAIR - 1), t)

        @block.scalar
        def _(act):
            done = [0]

            def link(ins):
                done[0] += 1
                ins.then_inc(s_act, 1)
                act.wait_ge(s_act, done[0])

            A = nc.scalar.activation
            for t in range(TT):
                act.wait_ge(s_x[t], 16)
                A(ar(TM0 + 2048 * t, D), xs[:, t, :], ACT.Square, accum_out=ssx[:, t:t + 1]).then_inc(s_ssx, 1)
            act.wait_ge(s_ms, 1)
            A(rx[:, 0:TT], ssx[:, 2:2 + TT], ACT.Sqrt).then_inc(s_sq, 1)
            act.wait_ge(s_rowT, 1)
            A(cols3, ps[:, 3, 0:84], ACT.Copy).then_inc(s_rowC, 1)
            act.wait_ge(s_rowC, 1)
            act.wait_ge(s_wsm, 32)
            A(wsm_hi, wsm, ACT.Copy).then_inc(s_wsh, 1)
            for i in range(KT // 2):
                act.wait_ge(s_xT, i + 1)
                for k in (2 * i, 2 * i + 1):
                    ins = nc.scalar.mul(hThi[:, k, :], ps[:, 4 + i % 4, (k % 2) * T:(k % 2) * T + T], g1T[:, k:k + 1])
                ins.then_inc(s_hhi, 1)

            def high_part(u, slot, rslot, uses):
                act.wait_ge(s_raw[rslot], uses * 16 + 16)
                if not (isinstance(u, int) and u < 3):
                    act.wait_ge(s_use, u - 2)
                A(whi[:, slot], raw[:, rslot], ACT.Copy).then_inc(s_hi, 1)

            def high_part_at(u):
                high_part(u, u % 3, load_of(u) % 3, load_of(u) // 3)

            def evac_fm(g, gi):
                act.wait_ge(s_use, g * 2 + 2)
                A(fm_flat[:, bass.ds(g * 512, 512)], ps[:, gi, :], ACT.Copy).then_inc(s_ev, 1)

            high_part_at(0)
            high_part_at(1)
            high_part_at(2)
            act.wait_ge(s_smp, 1)
            A(smT, ps[0:40, 3, 0:T], ACT.Copy).then_inc(s_sma, 1)
            for g in range(3):
                for half in range(2):
                    if 2 * g + half + 2 > 2:
                        high_part_at(2 * g + half + 2)
                evac_fm(g, g)
            with act.Fori(1, G_LOOP // 3) as j:
                for gi in range(3):
                    for half in range(2):
                        i = 2 * gi + half + 2
                        high_part(j * 6 + i, i % 3, i % 3, j * 2 + i // 3)
                    evac_fm(j * 3 + gi, gi)

            for step in SCHED:
                if step[0] in ("fm", "tm", "mg"):
                    u = {"fm": 2 * step[1] + step[2], "tm": U_TM + 2 * step[1] + step[2],
                         "mg": U_MG + 3 * step[1] + step[2]}[step[0]]
                    high_part_at(u + 2)
                if step[0] == "fm" and step[2] == 1:
                    evac_fm(step[1], step[1] % 3)
                elif step[0] == "gat":
                    act.wait_ge(s_gaT, 1)
                    A(ng, ps[:, 3, 0:80].rearrange("p (a n) -> p a n", a=TT)[:, :, 16:40], ACT.Sigmoid).then_inc(s_gaTc, 1)
                elif step[0] == "z":
                    act.wait_ge(s_y, 1)
                    A(gG[0], gG[0], ACT.Exp, scale=-1.0).then_inc(s_e, 1)
                    act.wait_ge(s_e, 1)
                    A(gG[0], gG[0], ACT.Ln, bias=1.0).then_inc(s_ln, 1)
                elif step[0] in ("diag", "level"):
                    lv = 0 if step[0] == "diag" else step[1] + 1
                    if lv < LEVELS:
                        act.wait_ge(s_gD, lv + 1)
                        A(gd, gd, ACT.Exp, scale=1.0 / TAU).then_inc(s_gE, 1)
                elif step[0] == "tm" and step[2] == 1:
                    g = step[1]
                    G = N_FM + g
                    act.wait_ge(s_use, 2 * G + 2)
                    dst, c = ((mv, g) if g < 4 else (gv, g - 4) if g < 8 else (kv35, g - 8) if g < TM_GG
                              else (gg, g - TM_GG))
                    A(dst[:, :, c * CW:c * CW + CW], ps[:, G % 3, :].rearrange("p (a n) -> p a n", a=TT),
                      ACT.Silu if g >= TM_GG else ACT.Copy).then_inc(s_ev, 1)
                elif step[0] == "cmp1":
                    if step[1] == N_CMPU - 1:
                        act.wait_ge(s_cmpu, N_CMPU)
                        A(hid4, ps[:, 3, 0:2 * P], ACT.Copy).then_inc(s_hid4, 1)
                elif step[0] == "cmp2":
                    act.wait_ge(s_cmps, 1)
                    A(hidT, ps[:, 3, 256:320].rearrange("p (c n) -> p c n", c=2)[:, :, 0:30], ACT.Silu
                      ).then_inc(s_hid, 1)
                elif step[0] == "cmp3":
                    act.wait_ge(s_cmp2, 1)
                    A(kcT, ps[:, 3, 0:30], ACT.Copy)
                    A(vc, ps[0:NCMP, 3, 64:64 + 2 * P].rearrange("p (g n) -> p g n", g=KVH), ACT.Copy).then_inc(s_kvc, 1)
                elif step[0] == "S":
                    u = step[1]
                    kind, h = unit_of(u)
                    act.wait_ge(s_nb, u + 1)
                    b = nb[u % 2]
                    A(aP[u % 2][:, 0:P], ps[:, 6, 0:P], ACT.Exp, bias=b[:, 0:1], scale=SCALE,
                      accum_out=su[u % 2][:, 0:1])
                    last = A(aP[u % 2][:, P:3 * P], ps[:, 6, P:3 * P], ACT.Exp, bias=b[:, 1:2], scale=SCALE,
                             accum_out=su[u % 2][:, 1:2])
                    if kind == "slc":
                        for t in range(TT):
                            last = A(cP[h % 2][:, t], ps[:, 6, 384 + 16 * t:384 + 16 * t + NCMP], ACT.Exp,
                                     bias=b[:, 2 + t:3 + t], scale=SCALE, accum_out=su[u % 2][:, 2 + t:3 + t])
                    last.then_inc(s_exp, 1)
                elif step[0] == "T":
                    u = step[1]
                    kind, h = unit_of(u)
                    act.wait_ge(s_T, u + 1)
                    last = A(aPT[u % 2], ps[:, 7, 0:3 * P], ACT.Copy)
                    if kind == "slc":
                        last = A(cPT[h % 2], ps[0:NCMP, 5, 0:T], ACT.Copy)
                    last.then_inc(s_PT, 1)
                elif step[0] == "gpv":
                    h = step[1]
                    act.wait_ge(s_gcp, h + 1)
                    if h >= 1:
                        act.wait_ge(s_gsq, h)
                    link(A(junk256, oraw[:, 2 * h], ACT.Square, accum_out=ssg[:, 2 * h:2 * h + 1]))
                    A(junk256, oraw[:, 2 * h + 1], ACT.Square, accum_out=ssg[:, 2 * h + 1:2 * h + 2]).then_inc(s_gsq, 1)
                elif step[0] == "gms":
                    act.wait_ge(s_gms, 1)
                    A(rg, ssg, ACT.Sqrt).then_inc(s_grt, 1)
                elif step[0] == "gtr":
                    h = step[1]
                    act.wait_ge(s_gtr, h + 1)
                    A(ogT[:, 2 * h:2 * h + 2].rearrange("p b t -> p (b t)"), ps[:, 5, :], ACT.Copy).then_inc(s_ogT, 1)
                elif step[0] == "osplit":
                    b = step[1]
                    if b == 1:
                        act.wait_ge(s_ogT, GH)
                    else:
                        act.wait_ge(s_O, MH if b == 0 else MH + NH)
                    if b == 2:
                        act.wait_ge(s_use, U_MG + 3 * N_CG)
                    A(ohi[b][:, :], osrc[b], ACT.Copy).then_inc(s_ohi, 1)
                elif step[0] == "mg" and step[2] == 2:
                    m = step[1]
                    act.wait_ge(s_use, U_MG + 3 * m + 3)
                    if m >= 2:
                        act.wait_ge(s_mrg, m - 1)
                    A(sg[m % 2], ps[:, 2 * (m % 2), :], ACT.Sigmoid).then_inc(s_sig, 1)

            for bi in (1, 2):
                with act.Fori(bi * (N_CG // 2), (bi + 1) * (N_CG // 2)) as j:
                    for s in range(2):
                        m = j * 2 + s
                        for part in range(3):
                            i = 3 * s + part + 2
                            high_part(j * 6 + (U_MG + i), (U_MG + i) % 3, (U_MG + N_CMPU + i) % 3,
                                      j * 2 + (U_MG + N_CMPU + i) // 3)
                        act.wait_ge(s_use, m * 3 + (U_MG + 3))
                        act.wait_ge(s_mrg, m - 1)
                        A(sg[s], ps[:, 2 * s, :], ACT.Sigmoid).then_inc(s_sig, 1)
                        if bi == 2:
                            act.wait_ge(s_mrg, m + 1)
                            q = bass.ds(j * 1024 + (s * 512 - N_CG * 2 * 512), 512)
                            A(merged_hi[:, q], merged_flat[:, q], ACT.Copy).then_inc(s_mhi, 1)

            def square_group(g):
                act.wait_ge(s_x2, g + 1)
                for t in range(TT):
                    if g + t >= 1:
                        act.wait_ge(s_ss2p, 2 * g + t)
                    A(squares, xs[:, t, g * CW:g * CW + CW], ACT.Square, accum_out=ss2p[:, t, g:g + 1]
                      ).then_inc(s_ss2p, 1)

            def copy_h2T(g):
                act.wait_ge(s_h2t, g + 1)
                A(h2T[:, 2 * g:2 * g + 2, :].rearrange("p k t -> p (k t)"), ps[:, 4 + g % 2, :], ACT.Copy
                  ).then_inc(s_h2A, 1)

            for g in range(N_CG):
                if g < N_CG - 1:
                    high_part_at(U_WO + 2 * g + 2)
                if g >= 1:
                    square_group(g - 1)
                if g < N_CG - 1:
                    high_part_at(U_WO + 2 * g + 3)
                if g >= 1:
                    copy_h2T(g - 1)
            square_group(N_CG - 1)
            act.wait_ge(s_ms2, 1)
            A(r2[:, 0:TT], ss2[:, 2:4], ACT.Sqrt).then_inc(s_sq2, 1)
            copy_h2T(N_CG - 1)
            act.wait_ge(s_r2, 1)
            for t in range(TT):
                nc.scalar.mul(h2[:, t, :], h2[:, t, :], r2[:, 2 + t:3 + t]).then_inc(s_h2, 1)
            act.wait_ge(s_re, 1)
            A(t8, t8, ACT.Exp)
            A(rs[:, 5], rs[:, 5], ACT.Exp).then_inc(s_rex, 1)
            act.wait_ge(s_route, 1)
            npass = act.value_load(npass_i[0:1, 0:1], min_val=1, max_val=T // SLOTS)

            def copy_xg(m):
                act.wait_ge(s_xg, m * 2 + 1)
                A(xgT[:, 0:8].rearrange("p k s -> p (k s)"), ps[:, 2:4, :].rearrange("p a n -> p (a n)"),
                  ACT.Copy).then_inc(s_xgA, 1)

            def copy_gu(n):
                act.wait_ge(s_gu, n + 1)
                A(gusb, ps[:, 0, :], ACT.Copy).then_inc(s_gus, 1)

            def silu(n):
                act.wait_ge(s_tr, n + 1)
                tr = ps[:, 1, :].rearrange("p (j two s) -> p j two s", two=2, s=SLOTS)
                A(hmid, tr[:, :, 0], ACT.Silu).then_inc(s_silu, 1)

            def copy_out(n, par):
                act.wait_ge(s_dn, n + 1)
                o = osb[par * SLOTS:par * SLOTS + SLOTS]
                A(o[:, 0:1024], ps[0:SLOTS, 6:8, :].rearrange("p a n -> p (a n)"), ACT.Copy)
                A(o[:, 1024:D], ps[SLOTS:P, 6:8, :].rearrange("p a n -> p (a n)"), ACT.Copy).then_inc(s_osb, 1)

            def pair(m, last_of_pass):
                n = m * 2
                copy_gu(n)
                silu(n)
                copy_out(n, 0)
                copy_gu(n + 1)
                if not last_of_pass:
                    copy_xg(m + 1)
                silu(n + 1)
                act.wait_ge(s_ST, m + 1)
                A(STb, ps[:, 0, 0:T], ACT.Copy).then_inc(s_STc, 1)
                copy_out(n + 1, 1)

            with act.Fori(0, npass) as q:
                base = q * NPAIR
                copy_xg(base)
                with act.Fori(0, NPAIR - 1) as i:
                    pair(base + i, False)
                pair(base + (NPAIR - 1), True)

            for t in range(TT):
                for c in range(4):
                    act.wait_ge(s_add, npass * (8 * NPAIR) + (4 * t + c + 1))
                    q = slice(c * W, c * W + W)
                    A(h2[:, t, q], xs[:, t, q], ACT.Square, accum_out=ssfp[:, t, c:c + 1]).then_inc(s_ssfp, 1)
            act.wait_ge(s_msf, 1)
            A(r2[:, 0:TT], ss2[:, 2:4], ACT.Sqrt).then_inc(s_sqf, 1)

        @block.vector
        def _(dve):
            done = [0]
            v = nc.vector

            def link(ins):
                done[0] += 1
                ins.then_inc(s_dve, 1)
                dve.wait_ge(s_dve, done[0])

            def rms_scale(ss, r, width, s_in, s_out, s_root, n, inputs=None, s_ready=None):
                dve.wait_ge(s_in, inputs or n)
                v.tensor_scalar(ss[:, n:2 * n], ss[:, 0:n], 1.0 / width, EPS, ALU.mult, ALU.add).then_inc(s_out, 1)
                dve.wait_ge(s_root, 1)
                ins = v.reciprocal(r[:, n:2 * n], r[:, 0:n])
                if s_ready is None:
                    link(ins)
                else:
                    ins.then_inc(s_ready, 1)
                    dve.wait_ge(s_ready, 1)

            rms_scale(ssx, rx, D, s_ssx, s_ms, s_sq, TT)
            for t in range(TT):
                v.tensor_scalar(xn[:, t, :], xs[:, t, :], rx[:, 2 + t:3 + t], None, ALU.mult).then_inc(s_xn, 1)
            dve.wait_ge(s_wsh, 1)
            v.tensor_tensor(wsm_lo, wsm, wsm_hi.bitcast(F32), ALU.subtract).then_inc(s_wsl, 1)
            dve.wait_ge(s_rowC, 1)
            for i in range(KT // 2):
                dve.wait_ge(s_hhi, i + 1)
                for k in (2 * i, 2 * i + 1):
                    ins = v.scalar_tensor_tensor(out=hTlo[:, k, :], in0=ps[:, 4 + i % 4, (k % 2) * T:(k % 2) * T + T],
                                                 scalar=g1T[:, k:k + 1], in1=hThi[:, k, :].bitcast(F32),
                                                 op0=ALU.mult, op1=ALU.subtract)
                ins.then_inc(s_hlo, 1)

            def rest(u, slot, rslot):
                dve.wait_ge(s_hi, u + 1)
                v.tensor_tensor(wlo[:, slot], raw[:, rslot], whi[:, slot].bitcast(F32), ALU.subtract).then_inc(s_lo, 1)

            def rest_at(u):
                rest(u, u % 3, load_of(u) % 3)

            for u in range(2 * G_LOOP // 5 + 2):
                rest_at(u)
            with dve.Fori(1, G_LOOP // 3) as j:
                for i in range(2, 8):
                    rest(j * 6 + i, i % 3, i % 3)

            def halves(ap, H):
                w4 = ap.rearrange("p (n two r) -> p n two r", two=2, r=H)
                return w4[:, :, 0, :], w4[:, :, 1, :]

            qflat, kflat = fm_flat[:, 0:1024], fm_flat[:, 1024:2048]

            def level_diffs(lv):
                H = 1 << lv
                b0, b1 = halves(gb, H)
                ref = b0[:, :, H - 1:H].to_broadcast([P, 1024 // (2 * H), H])
                d0, d1 = halves(gd, H)
                v.tensor_tensor(d0, ref, b0, ALU.subtract)
                v.tensor_tensor(d1, b1, ref, ALU.subtract).then_inc(s_gD, 1)

            def level_product(lv):
                H = 1 << lv
                dve.wait_ge(s_gE, lv + 1)
                d0, d1 = halves(gd, H)
                o0, o1 = halves(gG[lv % 2], H)
                if lv >= 2:
                    dve.wait_ge(s_lv, lv)
                v.tensor_tensor(o0, d0, halves(kflat, H)[0], ALU.mult)
                v.scalar_tensor_tensor(out=o1, in0=d1, scalar=SCALE, in1=halves(qflat, H)[1],
                                       op0=ALU.mult, op1=ALU.mult).then_inc(s_gG, 1)

            for step in SCHED:
                if step[0] in ("fm", "tm", "mg"):
                    u = {"fm": 2 * step[1] + step[2], "tm": U_TM + 2 * step[1] + step[2],
                         "mg": U_MG + 3 * step[1] + step[2]}[step[0]]
                    rest_at(u + 2)
                if step[0] == "z":
                    dve.wait_ge(s_z, 1)
                    for h in range(GH):
                        ins = v.tensor_scalar(gd[:, h * T:h * T + T], ps[:, 6 + h // 2, (h % 2) * T:(h % 2) * T + T],
                                              baT[:, h:h + 1], None, ALU.add)
                    link(ins)
                    v.scalar_tensor_tensor(out=gG[0], in0=gd, scalar=-1.0, in1=gd, op0=ALU.mult,
                                           op1=ALU.max).then_inc(s_y, 1)
                    link(v.tensor_scalar(gG[1], gd, 0.0, None, ALU.min))
                    dve.wait_ge(s_ln, 1)
                    for h in range(GH):
                        q = slice(h * T, h * T + T)
                        ins = v.tensor_tensor_scan(gb[:, q], gG[1][:, q], gG[0][:, q], 0.0, ALU.add, ALU.subtract)
                    link(ins)
                    level_diffs(0)
                elif step[0] == "diag":
                    level_product(0)
                    dve.wait_ge(s_lv, 1)
                    for t in range(TT):
                        ins = v.scalar_tensor_tensor(out=gA[:, t], in0=ps[:, 4 + t, :].rearrange("p (h t) -> p h t", h=GH),
                                                     scalar=SCALE, in1=ident.unsqueeze(1).to_broadcast([P, GH, P]),
                                                     op0=ALU.mult, op1=ALU.mult)
                    ins.then_inc(s_gA, 1)
                    dve.wait_ge(s_masks, N_MASKS)
                    dve.wait_ge(s_gG, 1)
                    level_diffs(1)
                elif step[0] == "level":
                    lv = step[1]
                    if lv + 1 < LEVELS:
                        level_product(lv + 1)
                    if lv + 2 < LEVELS:
                        dve.wait_ge(s_gG, lv + 2)
                        level_diffs(lv + 2)
                    dve.wait_ge(s_lv, lv + 2)
                    dve.wait_ge(s_gA, lv + 1)
                    if lv < LEVELS - 1:
                        for t in range(TT):
                            ins = v.copy_predicated(gA[:, t],
                                                    lmask[:, lv].bitcast(I32).unsqueeze(1).to_broadcast([P, GH, P]),
                                                    ps[:, 4 + t, :].rearrange("p (h t) -> p h t", h=GH))
                    else:
                        ins = v.tensor_copy(gAoff, ps[:, 4, :].rearrange("p (h t) -> p h t", h=GH))
                    ins.then_inc(s_gA, 1)
                elif step[0] == "flat":
                    dve.wait_ge(s_ev, N_FM - 2)
                    for c in range(2):
                        for g in range(KVH):
                            for a in range(2):
                                src = fm[:, B_KCMP + 2 * c + g, 16 * a:16 * a + 240].rearrange("p (n b) -> p b n", b=16)
                                pe_ = peT[:, 32 * c + 16 * a:32 * c + 16 * a + 16].unsqueeze(2).to_broadcast([P, 16, NCMP])
                                ins = v.tensor_tensor(flat[:, c, 16 * a:16 * a + 16, g * NCMP:(g + 1) * NCMP],
                                                      src, pe_, ALU.add)
                    v.memset(flat[:, :, :, 2 * NCMP:32], 0.0)
                    v.tensor_reduce(out=stack, in_=ident.rearrange("p (j n) -> p n j", n=32), axis=AX_X,
                                    op=ALU.add).then_inc(s_flat, 1)
                elif step[0] == "S":
                    u = step[1]
                    kind, h = unit_of(u)
                    n = 4 if kind == "slc" else 2
                    m_, b_, s_, r_ = mx[u % 2], nb[u % 2], su[u % 2], rr[u % 2]
                    dve.wait_ge(s_S, u + 1)
                    v.tensor_reduce(m_[:, 0:1], ps[:, 6, 0:P], AX_X, ALU.max)
                    ins = v.tensor_reduce(m_[:, 1:2], ps[:, 6, P:3 * P], AX_X, ALU.max)
                    if kind == "slc":
                        ins = v.tensor_reduce(m_[:, 2:4], ps[:, 6, 384:416].rearrange("p (a n) -> p a n", a=2)[:, :, 0:NCMP],
                                              AX_X, ALU.max)
                    link(ins)
                    v.tensor_scalar(b_[:, 0:n], m_[:, 0:n], -SCALE, 1e28, ALU.mult, ALU.min).then_inc(s_nb, 1)
                    dve.wait_ge(s_exp, u + 1)
                    if kind == "slc":
                        link(v.tensor_scalar(s_[:, 2:4], s_[:, 2:4], 1e-30, None, ALU.max))
                    link(v.reciprocal(r_[:, 0:n], s_[:, 0:n]))
                    if kind != "moba":
                        br = {"slc": 1, "win": 2}[kind]
                        ins = v.tensor_tensor(r_[:, 0:2], r_[:, 0:2], ng[:, :, 3 * h + br], ALU.mult)
                        if kind == "slc":
                            ins = v.tensor_tensor(r_[:, 2:4], r_[:, 2:4], ng[:, :, 3 * h], ALU.mult)
                        link(ins)
                    p_ = aP[u % 2]
                    v.tensor_scalar(p_[:, 0:P], p_[:, 0:P], r_[:, 0:1], None, ALU.mult)
                    ins = v.tensor_scalar(p_[:, P:3 * P], p_[:, P:3 * P], r_[:, 1:2], None, ALU.mult)
                    if kind == "slc":
                        for t in range(TT):
                            ins = v.scalar_tensor_tensor(out=cP[h % 2][:, t], in0=cP[h % 2][:, t],
                                                         scalar=r_[:, 2 + t:3 + t], in1=cmul[:, t],
                                                         op0=ALU.mult, op1=ALU.mult)
                    ins.then_inc(s_P, 1)
                elif step[0] == "V":
                    u = step[1]
                    kind, h = unit_of(u)
                    if kind != "slc":
                        dve.wait_ge(s_V, u + 1)
                        b = (B_MQ if kind == "moba" else B_NQ) + h
                        v.tensor_copy(fm[:, b], ps[:, 4, (h % 2) * T:(h % 2) * T + T]).then_inc(s_O, 1)
                elif step[0] == "gpv":
                    h = step[1]
                    dve.wait_ge(s_gpv, h + 1)
                    v.tensor_copy(oraw[:, 2 * h:2 * h + 2].rearrange("p i n -> p (i n)"), ps[:, 5, :]).then_inc(s_gcp, 1)
                elif step[0] == "gms":
                    dve.wait_ge(s_gsq, GH)
                    v.tensor_scalar(ssg, ssg, 1.0 / GDV, EPS, ALU.mult, ALU.add).then_inc(s_gms, 1)
                    dve.wait_ge(s_grt, 1)
                    link(v.reciprocal(rg, rg))
                elif step[0] == "gnorm":
                    h = step[1]
                    if h == 0:
                        dve.wait_ge(s_ev, N_GROUP)
                    for t in range(TT):
                        i = 2 * h + t
                        ins = v.scalar_tensor_tensor(out=oraw[:, i], in0=oraw[:, i], scalar=rg[:, i:i + 1], in1=gng,
                                                     op0=ALU.mult, op1=ALU.mult)
                    link(ins)
                    for t in range(TT):
                        i = 2 * h + t
                        ins = v.tensor_tensor(oraw[:, i], oraw[:, i], gg[:, t, h * GDV:(h + 1) * GDV], ALU.mult)
                    ins.then_inc(s_on, 1)
                elif step[0] == "osplit":
                    b = step[1]
                    dve.wait_ge(s_ohi, b + 1)
                    v.tensor_tensor(olo[b][:, :], osrc[b], ohi[b][:, :].bitcast(F32), ALU.subtract).then_inc(s_olo, 1)
                elif step[0] == "mg" and step[2] == 2:
                    m = step[1]
                    dve.wait_ge(s_sig, m + 1)
                    v.tensor_tensor(merged_flat[:, 512 * m:512 * m + 512], sg[m % 2],
                                    ps[:, 2 * (m % 2) + 1, :], ALU.mult).then_inc(s_mrg, 1)
            for bi in (1, 2):
                with dve.Fori(bi * (N_CG // 2), (bi + 1) * (N_CG // 2)) as j:
                    for s in range(2):
                        m = j * 2 + s
                        for part in range(3):
                            i = 3 * s + part + 2
                            rest(j * 6 + (U_MG + i), (U_MG + i) % 3, (U_MG + N_CMPU + i) % 3)
                        dve.wait_ge(s_sig, m + 1)
                        q = bass.ds(j * 1024 + (s * 512 - N_CG * bi * 512), 512)
                        v.tensor_tensor(sg[s], sg[s], ps[:, 2 * s + 1, :], ALU.mult).then_inc(s_tmp, 1)
                        dve.wait_ge(s_tmp, m - (N_CG - 1))
                        v.tensor_tensor(merged_flat[:, q], merged_flat[:, q], sg[s], ALU.add).then_inc(s_mrg, 1)
                        if bi == 2:
                            dve.wait_ge(s_mhi, m - (2 * N_CG - 1))
                            v.tensor_tensor(merged_lo[:, q], merged_flat[:, q], merged_hi[:, q].bitcast(F32),
                                            ALU.subtract).then_inc(s_mlo, 1)

            def add_out(g):
                dve.wait_ge(s_use, U_WO + 2 * g + 2)
                q = slice(g * CW, g * CW + CW)
                v.tensor_tensor(xs[:, :, q], xs[:, :, q], ps[:, g % 3, :].rearrange("p (a n) -> p a n", a=TT), ALU.add
                                ).then_inc(s_x2, 1)
                if g == 0:
                    dve.wait_ge(s_g2, 16)
                dve.wait_ge(s_x2, g + 1)
                v.tensor_tensor(h2[:, :, q], xs[:, :, q], g2b[:, q].unsqueeze(1).to_broadcast([P, TT, CW]), ALU.mult
                                ).then_inc(s_hg, 1)

            for g in range(N_CG):
                for half in range(2):
                    if 2 * g + half + 2 < 2 * N_CG:
                        rest_at(U_WO + 2 * g + half + 2)
                if g == 0:
                    dve.wait_ge(s_xr, 16 * TT)
                add_out(g)

            dve.wait_ge(s_ss2p, TT * N_CG)
            v.tensor_reduce(ss2[:, 0:TT], ss2p, AX_X, ALU.add).then_inc(s_ss2, 1)
            rms_scale(ss2, r2, D, s_ss2, s_ms2, s_sq2, TT, 1, s_r2)

            def bc(ap, n):
                return ap.unsqueeze(2).to_broadcast([P, TT, n])

            def first_max(vals, mxv, mnv, tmp, oh, n):
                link(v.tensor_reduce(mxv, vals, AX_X, ALU.max))
                link(v.tensor_tensor(oh, vals, bc(mxv, n), ALU.is_equal))
                link(v.tensor_tensor(tmp, oh, jm[:, 0:n].unsqueeze(1).to_broadcast([P, TT, n]), ALU.mult))
                link(v.tensor_reduce(mnv, tmp, AX_X, ALU.min))
                link(v.tensor_tensor(oh, tmp, bc(mnv, n), ALU.is_equal))

            dve.wait_ge(s_lgt, 1)
            dve.wait_ge(s_rc, 4)
            for t in range(TT):
                ins = v.scalar_tensor_tensor(out=lg[:, t], in0=ps[:, 6 + t, 0:36], scalar=r2[:, 2 + t:3 + t], in1=rbb,
                                             op0=ALU.mult, op1=ALU.add)
            link(ins)
            gl, el = lg[:, :, 0:GROUPS], lg[:, :, GROUPS:36]
            first_max(gl, rs[:, 0], rs[:, 1], t8, goh, GROUPS)
            link(v.tensor_tensor(t8, gl, bc(rs[:, 0], GROUPS), ALU.subtract))
            gx = [goh[:, t].unsqueeze(2).to_broadcast([P, GROUPS, EPG]) for t in range(TT)]
            for t in range(TT):
                ins = v.tensor_tensor(em[:, t].rearrange("p (g e) -> p g e", g=GROUPS),
                                      el[:, t].rearrange("p (g e) -> p g e", g=GROUPS), gx[t], ALU.mult)
            link(ins)
            link(v.tensor_scalar(oh1[:, :, 0:GROUPS], goh, -1.0, -NEG, ALU.add, ALU.mult))
            for t in range(TT):
                ins = v.tensor_tensor(em[:, t].rearrange("p (g e) -> p g e", g=GROUPS),
                                      em[:, t].rearrange("p (g e) -> p g e", g=GROUPS),
                                      oh1[:, t, 0:GROUPS].unsqueeze(2).to_broadcast([P, GROUPS, EPG]), ALU.add)
            link(ins)
            first_max(em, rs[:, 2], rs[:, 3], t64, oh1, NE)
            link(v.scalar_tensor_tensor(out=em, in0=oh1, scalar=10 * NEG, in1=em, op0=ALU.mult, op1=ALU.add))
            first_max(em, rs[:, 4], rs[:, 3], t64, oh2, NE)
            link(v.tensor_tensor(M, oh1, oh2, ALU.add))
            v.tensor_copy(M, M).then_inc(s_M, 1)
            v.tensor_tensor(rs[:, 5], rs[:, 4], rs[:, 2], ALU.subtract).then_inc(s_re, 1)
            dve.wait_ge(s_rex, 1)
            link(v.tensor_reduce(rs[:, 6], t8, AX_X, ALU.add))
            link(v.tensor_scalar(rs[:, 7], rs[:, 5], 1.0, None, ALU.add))
            link(v.tensor_tensor(rs[:, 6], rs[:, 6], rs[:, 7], ALU.mult))
            link(v.reciprocal(rs[:, 8], rs[:, 6]))
            link(v.tensor_tensor(rs[:, 9], rs[:, 8], rs[:, 5], ALU.mult))
            link(v.tensor_tensor(oh1, oh1, bc(rs[:, 8], NE), ALU.mult))
            link(v.tensor_tensor(oh2, oh2, bc(rs[:, 9], NE), ALU.mult))
            link(v.tensor_tensor(wgt, oh1, oh2, ALU.add))
            dve.wait_ge(s_pos, 1)
            link(v.tensor_scalar(t64, M, -1.0, 1e6, ALU.add, ALU.mult))
            link(v.tensor_tensor(posm, ps[:, 1, 0:2 * NE].rearrange("p (a e) -> p a e", a=TT), t64, ALU.add))
            link(v.tensor_reduce(rs[:, 10, 0:1], ps[:, 1, 2 * NE:3 * NE], AX_X, ALU.max))
            link(v.tensor_scalar(rs[:, 11, 0:1], rs[:, 10, 0:1], float(SLOTS), 1.0, ALU.is_gt, ALU.add))
            for k in range(2, T // SLOTS):
                link(v.tensor_scalar(rs[:, 12, 0:1], rs[:, 10, 0:1], float(SLOTS * k), None, ALU.is_gt))
                link(v.tensor_tensor(rs[:, 11, 0:1], rs[:, 11, 0:1], rs[:, 12, 0:1], ALU.add))
            v.tensor_copy(npass_i, rs[:, 11, 0:1]).then_inc(s_route, 1)
            v.memset(npass_f[:, 1:2], 0.0).then_inc(s_add, 8)
            v.memset(npass_f[:, 2:3], 0.0).then_inc(s_STc, 1)
            dve.wait_ge(s_route, 1)
            npass = dve.value_load(npass_i[0:1, 0:1], min_val=1, max_val=T // SLOTS)

            def make_g(e):
                for par in range(2):
                    for t in range(TT):
                        ins = v.tensor_scalar(Gb[:, t, par * SLOTS:par * SLOTS + SLOTS], iota,
                                              posm[:, t, bass.ds(e + par, 1)], None, ALU.is_equal)
                ins.then_inc(s_G, 1)

            def make_s(e):
                for par in range(2):
                    for t in range(TT):
                        ins = v.tensor_scalar(Sb[:, t, par * SLOTS:par * SLOTS + SLOTS], iota,
                                              posm[:, t, bass.ds(e + par, 1)], wgt[:, t, bass.ds(e + par, 1)],
                                              ALU.is_equal, ALU.mult)
                ins.then_inc(s_Sm, 1)

            def copy_xg(m):
                dve.wait_ge(s_xg, m * 2 + 2)
                v.tensor_copy(xgT[:, 8:16].rearrange("p k s -> p (k s)"),
                              ps[:, 4:6, :].rearrange("p a n -> p (a n)")).then_inc(s_xgD, 1)

            def middle(n):
                dve.wait_ge(s_silu, n + 1)
                tr = ps[:, 1, :].rearrange("p (j two s) -> p j two s", two=2, s=SLOTS)
                v.tensor_tensor(hmid, hmid, tr[:, :, 1], ALU.mult).then_inc(s_mid, 1)

            def adds(m, t):
                for c in range(4):
                    dve.wait_ge(s_sc, m * 8 + (4 * t + c + 1))
                    xc = xs[:, t, c * W:c * W + W]
                    v.tensor_tensor(xc, xc, ps[:, 2 + c, :], ALU.add).then_inc(s_add, 1)

            def pair(m, e, first, last_of_pass):
                n = m * 2
                if not last_of_pass:
                    make_g(e + 2)
                if not first:
                    adds(m - 1, 0)
                middle(n)
                if not first:
                    adds(m - 1, 1)
                middle(n + 1)
                if not last_of_pass:
                    copy_xg(m + 1)
                    dve.wait_ge(s_ST, m + 1)
                    make_s(e + 2)

            with dve.Fori(0, npass) as q:
                base = q * NPAIR
                make_g(0)
                make_s(0)
                copy_xg(base)
                pair(base, 0, True, False)
                with dve.Fori(1, NPAIR - 1) as i:
                    pair(base + i, i * 2, False, False)
                pair(base + (NPAIR - 1), NE - 2, False, True)
                for t in range(TT):
                    adds(base + (NPAIR - 1), t)
                v.tensor_scalar(posm, posm, -float(SLOTS), None, ALU.add).then_inc(s_M, 1)
                dve.wait_ge(s_M, q + 2)

            dve.wait_ge(s_ssfp, TT * 4)
            v.tensor_reduce(ss2[:, 0:TT], ssfp, AX_X, ALU.add).then_inc(s_ssf, 1)
            rms_scale(ss2, r2, D, s_ssf, s_msf, s_sqf, TT, 1)
            dve.wait_ge(s_gf, 16)
            for t in range(TT):
                for h in range(2):
                    q = slice(h * (D // 2), (h + 1) * (D // 2))
                    v.scalar_tensor_tensor(out=h2[:, t, q], in0=xs[:, t, q], scalar=r2[:, 2 + t:3 + t], in1=gfb[:, q],
                                           op0=ALU.mult, op1=ALU.mult).then_inc(s_y1, 1)


_INS = ['x', 'norm1_g', 'w_in', 'nsa_cmp_pe', 'nsa_cmp_w1', 'nsa_cmp_w2', 'gla_wa', 'gla_ba', 'gla_norm_g',
        'w_br_moba', 'w_br_nsa', 'w_br_gla', 'w_out', 'norm2_g', 'router_group_w', 'router_group_b',
        'router_expert_w', 'router_expert_b', 'expert_w_gate', 'expert_w_up', 'expert_w_down', 'final_norm_g']
_OUTS = [((1, 256, 2048), 'float32')]


def kernel(**inputs):
    import numpy as _np
    import concourse.bacc as _bacc
    from concourse import mybir as _mybir
    from concourse.bass_utils import run_bass_kernel_spmd as _run

    nc = _bacc.Bacc("TRN2", target_bir_lowering=False, num_devices=1, dynamic_dma_scratch_size=1024)
    arrays, args = {}, []
    for name in _INS:
        a = _np.ascontiguousarray(inputs[name])
        arrays[f"in_{name}_dram"] = a
        args.append(nc.dram_tensor(f"in_{name}_dram", a.shape, _mybir.dt.from_np(a.dtype), kind="ExternalInput").ap())
    for i, (shape, dtype) in enumerate(_OUTS):
        dt = _mybir.dt.from_np(_np.dtype(dtype))
        args.append(nc.dram_tensor(f"out_{i}_dram", shape, dt, kind="ExternalOutput").ap())
    build(nc, *args)
    r = _run(nc, [arrays], core_ids=[0])
    return r.results[0]["out_0_dram"]
```
